# Optimizing a Trainium2 kernel written in Bass

```python
import math
import jax, jax.numpy as jnp
from jax import lax
import numpy as np

D_MODEL = 1024
BATCH = 1
SEQ = 512
DEPTH = 2

HGRN_HEADS = 4
HGRN_DK = D_MODEL // (2 * HGRN_HEADS)
HGRN_DV = D_MODEL // (2 * HGRN_HEADS)
RET_HEADS = 4
RET_DK = D_MODEL // (2 * RET_HEADS)
RET_DV = D_MODEL // (2 * RET_HEADS)
LIN_CHUNK = 64
EVEN_COLS = [HGRN_HEADS * HGRN_DK, HGRN_HEADS * HGRN_DK, HGRN_HEADS * HGRN_DV, HGRN_HEADS * HGRN_DV,
             RET_HEADS * RET_DK, RET_HEADS * RET_DK, RET_HEADS * RET_DV, RET_HEADS * RET_DV]
EVEN_MIX_OUT = HGRN_HEADS * HGRN_DV + RET_HEADS * RET_DV

NSA_HD = 64
NSA_HEADS = D_MODEL // NSA_HD
NSA_KV_GROUPS = 2
CMP_BLOCK = 32
CMP_STRIDE = 16
SLC_BLOCK = 64
SLC_TOPN = 16
WINDOW = 512
Q_BLOCK = 128
KVW = NSA_KV_GROUPS * NSA_HD
ODD_COLS = [NSA_HEADS * NSA_HD, KVW, KVW, KVW, KVW, KVW, KVW, 3 * NSA_HEADS]

FFN_HIDDEN = ((8 * D_MODEL // 3 + 255) // 256) * 256
N_EVEN = (DEPTH + 1) // 2
N_ODD = DEPTH // 2
RMS_EPS = 1e-6
NEG_INF = -1e30
FORCE_SCORE = 1e9


def rmsnorm(x, g):
    xf = x.astype(jnp.float32)
    y = xf * lax.rsqrt(jnp.mean(xf * xf, axis=-1, keepdims=True) + RMS_EPS)
    return (y * g.astype(jnp.float32)).astype(x.dtype)

def split_cols(a, sizes):
    return jnp.split(a, np.cumsum(sizes)[:-1].tolist(), axis=-1)

def to_chunks(a, c):
    b, t, h, d = a.shape
    return a.reshape(b, t // c, c, h, d).transpose(1, 0, 3, 2, 4)

def from_chunks(a):
    n, b, h, c, d = a.shape
    return a.transpose(1, 0, 3, 2, 4).reshape(b, n * c, h, d)

def hgrn2_chunked(q, k, v, log_f):
    b_, t_, h_, dk = q.shape
    dv = v.shape[-1]
    c = LIN_CHUNK
    causal = jnp.tril(jnp.ones((c, c), dtype=bool))[:, :, None]

    def step(state, inp):
        qi, ki, vi, gi = inp
        cum = jnp.cumsum(gi, axis=2)
        diff = cum[:, :, :, None, :] - cum[:, :, None, :, :]
        decay = jnp.exp(jnp.where(causal, diff, NEG_INF))
        attn = jnp.einsum('bhid,bhjd,bhijd->bhij', qi, ki, decay)
        out = jnp.einsum('bhij,bhjv->bhiv', attn, vi) + jnp.einsum('bhid,bhdv->bhiv', qi * jnp.exp(cum), state)
        last = cum[:, :, -1:, :]
        state = jnp.exp(last[:, :, 0, :])[..., None] * state + jnp.einsum('bhjd,bhjv->bhdv', ki * jnp.exp(last - cum), vi)
        return state, out

    s0 = jnp.zeros((b_, h_, dk, dv), jnp.float32)
    xs = tuple(to_chunks(a.astype(jnp.float32), c) for a in (q, k, v, log_f))
    _, o = lax.scan(step, s0, xs)
    return from_chunks(o)

def retention_chunked(q, k, v, log_gamma):
    b_, t_, h_, dk = q.shape
    dv = v.shape[-1]
    c = LIN_CHUNK
    pos = jnp.arange(c, dtype=jnp.float32)
    rel = pos[:, None] - pos[None, :]
    decay = jnp.where(rel[None] >= 0, jnp.exp(jnp.maximum(rel, 0.0)[None] * log_gamma[:, None, None]), 0.0)
    q_decay = jnp.exp((pos + 1.0)[None, :] * log_gamma[:, None])[..., None]
    k_decay = jnp.exp((c - 1.0 - pos)[None, :] * log_gamma[:, None])[..., None]
    chunk_decay = jnp.exp(c * log_gamma)[:, None, None]

    def step(state, inp):
        qi, ki, vi = inp
        attn = jnp.einsum('bhid,bhjd->bhij', qi, ki) * decay
        out = jnp.einsum('bhij,bhjv->bhiv', attn, vi) + jnp.einsum('bhid,bhdv->bhiv', qi * q_decay, state)
        state = chunk_decay * state + jnp.einsum('bhjd,bhjv->bhdv', ki * k_decay, vi)
        return state, out

    s0 = jnp.zeros((b_, h_, dk, dv), jnp.float32)
    xs = tuple(to_chunks(a.astype(jnp.float32), c) for a in (q, k, v))
    _, o = lax.scan(step, s0, xs)
    return from_chunks(o)

def even_mixer(h, w_in, lower_bound, hgrn_norm, ret_norm, w_out):
    b_, t_, _ = h.shape
    hq, hf, hi, hg, rq, rk, rv, rg = split_cols(h @ w_in, EVEN_COLS)
    heads = lambda a, n: a.reshape(b_, t_, n, -1)
    f = lower_bound + (1.0 - lower_bound) * jax.nn.sigmoid(hf.astype(jnp.float32))
    o_h = hgrn2_chunked(heads(jax.nn.silu(hq), HGRN_HEADS), heads(1.0 - f, HGRN_HEADS),
                        heads(hi, HGRN_HEADS), heads(jnp.log(f), HGRN_HEADS))
    o_h = rmsnorm(o_h, hgrn_norm) * jax.nn.silu(heads(hg, HGRN_HEADS).astype(jnp.float32))
    log_gamma = jnp.log(1.0 - jnp.exp2(-5.0 - jnp.arange(RET_HEADS, dtype=jnp.float32)))
    o_r = retention_chunked(heads(rq, RET_HEADS), heads(rk, RET_HEADS) * (RET_DK ** -0.5),
                            heads(rv, RET_HEADS), log_gamma)
    o_r = rmsnorm(o_r, ret_norm) * jax.nn.silu(heads(rg, RET_HEADS).astype(jnp.float32))
    o = jnp.concatenate([o_h.reshape(b_, t_, -1), o_r.reshape(b_, t_, -1)], axis=-1)
    return o.astype(h.dtype) @ w_out

def alibi_slopes(n):
    return jnp.exp2(-8.0 * jnp.arange(1, n + 1, dtype=jnp.float32) / n)

def compress_blocks(k, pos_emb, w1, w2):
    b_, t_, g_, d = k.shape
    r = CMP_BLOCK // CMP_STRIDE
    ch = k.reshape(b_, t_ // CMP_STRIDE, CMP_STRIDE, g_, d)
    nc = t_ // CMP_STRIDE - r + 1
    blocks = jnp.concatenate([ch[:, j:j + nc] for j in range(r)], axis=2)
    blocks = blocks + pos_emb[None, None, :, None, :]
    flat = blocks.transpose(0, 1, 3, 2, 4).reshape(b_, nc, g_, CMP_BLOCK * d)
    return jax.nn.silu(flat @ w1) @ w2

def cmp_to_slc_overlap(nc, ns):
    c0 = jnp.arange(nc) * CMP_STRIDE
    s0 = jnp.arange(ns) * SLC_BLOCK
    lo = jnp.maximum(c0[:, None], s0[None, :])
    hi = jnp.minimum(c0[:, None] + CMP_BLOCK, s0[None, :] + SLC_BLOCK)
    return (jnp.maximum(hi - lo, 0) / CMP_BLOCK).astype(jnp.float32)

def odd_mixer(h, w_in, cmp_pos_k, cmp_pos_v, cmp_w1_k, cmp_w2_k, cmp_w1_v, cmp_w2_v, w_out):
    b_, t_, _ = h.shape
    H, G, d = NSA_HEADS, NSA_KV_GROUPS, NSA_HD
    R = H // G
    q, kc, vc, ks, vs, kw, vw, gl = split_cols(h @ w_in, ODD_COLS)
    q = q.reshape(b_, t_, H, d) * (d ** -0.5)
    kvh = lambda a: a.reshape(b_, t_, G, d)
    k_cmp = compress_blocks(kvh(kc), cmp_pos_k, cmp_w1_k, cmp_w2_k)
    v_cmp = compress_blocks(kvh(vc), cmp_pos_v, cmp_w1_v, cmp_w2_v)
    nc = k_cmp.shape[1]
    ns = t_ // SLC_BLOCK
    n_sel = min(SLC_TOPN, ns)
    overlap = cmp_to_slc_overlap(nc, ns)
    c_end = jnp.arange(nc) * CMP_STRIDE + CMP_BLOCK - 1
    k_sb = kvh(ks).reshape(b_, ns, SLC_BLOCK, G, d).transpose(0, 3, 1, 2, 4)
    v_sb = kvh(vs).reshape(b_, ns, SLC_BLOCK, G, d).transpose(0, 3, 1, 2, 4)
    kw_pad = jnp.pad(kvh(kw), ((0, 0), (WINDOW, 0), (0, 0), (0, 0)))
    vw_pad = jnp.pad(kvh(vw), ((0, 0), (WINDOW, 0), (0, 0), (0, 0)))
    slopes = alibi_slopes(H).reshape(G, R)
    gates = jax.nn.sigmoid(gl.astype(jnp.float32)).reshape(b_, t_, H, 3)
    gather = jax.vmap(jax.vmap(lambda tbl, ix: tbl[ix]))
    nq = t_ // Q_BLOCK
    f32 = jnp.float32

    def block(args):
        n, qb, gb = args
        qg = qb.reshape(b_, Q_BLOCK, G, R, d)
        t = n * Q_BLOCK + jnp.arange(Q_BLOCK)
        s_c = jnp.einsum('bqgrd,bcgd->bgrqc', qg, k_cmp, preferred_element_type=f32)
        dist_c = (t[:, None] - c_end[None, :]).astype(f32)
        valid_c = dist_c >= 0
        s_c = jnp.where(valid_c, s_c - slopes[None, :, :, None, None] * dist_c, NEG_INF)
        p_c = jax.nn.softmax(s_c, axis=-1) * valid_c
        o_c = jnp.einsum('bgrqc,bcgd->bqgrd', p_c, v_cmp.astype(f32))
        p_slc = jnp.einsum('bgrqc,cj->bgqj', p_c, overlap)
        qblk = t // SLC_BLOCK
        js = jnp.arange(ns)
        forced = (js[None, :] == 0) | (js[None, :] == qblk[:, None]) | (js[None, :] == qblk[:, None] - 1)
        allowed = js[None, :] <= qblk[:, None]
        score = jnp.where(forced, FORCE_SCORE, jnp.where(allowed, p_slc, NEG_INF))
        _, idx = lax.top_k(score, n_sel)
        kg = gather(k_sb, idx)
        vg = gather(v_sb, idx)
        s_s = jnp.einsum('bqgrd,bgqnld->bgrqnl', qg, kg, preferred_element_type=f32)
        spos = idx[..., None] * SLC_BLOCK + jnp.arange(SLC_BLOCK)
        dist_s = (t[None, None, :, None, None] - spos).astype(f32)[:, :, None]
        s_s = jnp.where(dist_s >= 0, s_s - slopes[None, :, :, None, None, None] * dist_s, NEG_INF)
        p_s = jax.nn.softmax(s_s.reshape(b_, G, R, Q_BLOCK, -1), axis=-1).reshape(s_s.shape)
        o_s = jnp.einsum('bgrqnl,bgqnld->bqgrd', p_s, vg.astype(f32))
        kwb = lax.dynamic_slice_in_dim(kw_pad, n * Q_BLOCK, WINDOW + Q_BLOCK, axis=1)
        vwb = lax.dynamic_slice_in_dim(vw_pad, n * Q_BLOCK, WINDOW + Q_BLOCK, axis=1)
        wpos = n * Q_BLOCK - WINDOW + jnp.arange(WINDOW + Q_BLOCK)
        dist_w = t[:, None] - wpos[None, :]
        valid_w = (dist_w >= 0) & (dist_w < WINDOW) & (wpos[None, :] >= 0)
        s_w = jnp.einsum('bqgrd,bkgd->bgrqk', qg, kwb, preferred_element_type=f32)
        s_w = jnp.where(valid_w, s_w - slopes[None, :, :, None, None] * dist_w.astype(f32), NEG_INF)
        p_w = jax.nn.softmax(s_w, axis=-1)
        o_w = jnp.einsum('bgrqk,bkgd->bqgrd', p_w, vwb.astype(f32))
        g5 = gb.reshape(b_, Q_BLOCK, G, R, 3)
        o = g5[..., 0:1] * o_c + g5[..., 1:2] * o_s + g5[..., 2:3] * o_w
        return o.reshape(b_, Q_BLOCK, H * d)

    qblocks = q.reshape(b_, nq, Q_BLOCK, H, d).transpose(1, 0, 2, 3, 4)
    gblocks = gates.reshape(b_, nq, Q_BLOCK, H, 3).transpose(1, 0, 2, 3, 4)
    out = lax.map(block, (jnp.arange(nq), qblocks, gblocks))
    out = out.transpose(1, 0, 2, 3).reshape(b_, t_, H * d)
    return out.astype(h.dtype) @ w_out

def swiglu(h, w_gate_up, w_down):
    g, u = jnp.split(h @ w_gate_up, 2, axis=-1)
    return (jax.nn.silu(g) * u) @ w_down

def first_inputs(seed: int = 0) -> dict:
    key = jax.random.key(seed)
    ks = jax.random.split(key, 20)
    f32 = jnp.float32
    w = lambda k, shape, fan_in: jax.random.normal(k, shape, f32) * (fan_in ** -0.5)
    gain = lambda k, shape: 1.0 + 0.02 * jax.random.normal(k, shape, f32)
    even_in = sum(EVEN_COLS)
    odd_in = sum(ODD_COLS)
    return {
        'x': jax.random.normal(ks[0], (BATCH, SEQ, D_MODEL), f32),
        'mix_norm': gain(ks[1], (DEPTH, D_MODEL)),
        'ffn_norm': gain(ks[2], (DEPTH, D_MODEL)),
        'final_norm': gain(ks[3], (D_MODEL,)),
        'even_w_in': w(ks[4], (N_EVEN, D_MODEL, even_in), D_MODEL),
        'hgrn_lower_bounds': 0.1 * jax.random.normal(ks[5], (N_EVEN + 1, HGRN_HEADS * HGRN_DK), f32),
        'hgrn_out_norm': gain(ks[6], (N_EVEN, HGRN_DV)),
        'ret_out_norm': gain(ks[7], (N_EVEN, RET_DV)),
        'even_w_out': w(ks[8], (N_EVEN, EVEN_MIX_OUT, D_MODEL), EVEN_MIX_OUT),
        'odd_w_in': w(ks[9], (N_ODD, D_MODEL, odd_in), D_MODEL),
        'cmp_pos_k': 0.1 * jax.random.normal(ks[10], (N_ODD, CMP_BLOCK, NSA_HD), f32),
        'cmp_pos_v': 0.1 * jax.random.normal(ks[11], (N_ODD, CMP_BLOCK, NSA_HD), f32),
        'cmp_w1_k': w(ks[12], (N_ODD, CMP_BLOCK * NSA_HD, NSA_HD), CMP_BLOCK * NSA_HD),
        'cmp_w2_k': w(ks[13], (N_ODD, NSA_HD, NSA_HD), NSA_HD),
        'cmp_w1_v': w(ks[14], (N_ODD, CMP_BLOCK * NSA_HD, NSA_HD), CMP_BLOCK * NSA_HD),
        'cmp_w2_v': w(ks[15], (N_ODD, NSA_HD, NSA_HD), NSA_HD),
        'odd_w_out': w(ks[16], (N_ODD, NSA_HEADS * NSA_HD, D_MODEL), NSA_HEADS * NSA_HD),
        'ffn_w_gate_up': w(ks[17], (DEPTH, D_MODEL, 2 * FFN_HIDDEN), D_MODEL),
        'ffn_w_down': w(ks[18], (DEPTH, FFN_HIDDEN, D_MODEL), FFN_HIDDEN),
    }

def first_block(x, mix_norm, ffn_norm, final_norm, even_w_in, hgrn_lower_bounds, hgrn_out_norm,
              ret_out_norm, even_w_out, odd_w_in, cmp_pos_k, cmp_pos_v, cmp_w1_k, cmp_w2_k,
              cmp_w1_v, cmp_w2_v, odd_w_out, ffn_w_gate_up, ffn_w_down):
    lb_all = jnp.cumsum(jax.nn.softmax(hgrn_lower_bounds.astype(jnp.float32), axis=0), axis=0)
    h = x
    for layer in range(DEPTH):
        hn = rmsnorm(h, mix_norm[layer])
        if layer % 2 == 0:
            e = layer // 2
            h = h + even_mixer(hn, even_w_in[e], lb_all[e], hgrn_out_norm[e], ret_out_norm[e], even_w_out[e])
        else:
            o = layer // 2
            h = h + odd_mixer(hn, odd_w_in[o], cmp_pos_k[o], cmp_pos_v[o], cmp_w1_k[o], cmp_w2_k[o],
                              cmp_w1_v[o], cmp_w2_v[o], odd_w_out[o])
        h = h + swiglu(rmsnorm(h, ffn_norm[layer]), ffn_w_gate_up[layer], ffn_w_down[layer])
    return rmsnorm(h, final_norm)


GRID_W = 64
CTX_LEN = 256
HEAD_DIM = 64
A_HEADS = 4
A_VDIM = 2 * HEAD_DIM
A_WIDTH = A_HEADS * A_VDIM
B_HEADS = 8
B_KV_HEADS = 2
B_REP = B_HEADS // B_KV_HEADS
B_WIDTH = B_HEADS * HEAD_DIM
A_Q_COLS = A_HEADS * 2 * HEAD_DIM
A_K_COLS = A_HEADS * 2 * HEAD_DIM
A_V_COLS = A_WIDTH
B_Q_COLS = B_HEADS * HEAD_DIM
B_K_COLS = B_KV_HEADS * HEAD_DIM
B_V_COLS = B_KV_HEADS * HEAD_DIM
IN_COLS = A_Q_COLS + A_K_COLS + A_V_COLS + B_Q_COLS + B_K_COLS + B_V_COLS
IN_SPLITS = (A_Q_COLS,
             A_Q_COLS + A_K_COLS,
             A_Q_COLS + A_K_COLS + A_V_COLS,
             A_Q_COLS + A_K_COLS + A_V_COLS + B_Q_COLS,
             A_Q_COLS + A_K_COLS + A_V_COLS + B_Q_COLS + B_K_COLS)
MIX_WIDTH = A_WIDTH + B_WIDTH
CONV_WIDTH = 3
MLP_HIDDEN = 4 * D_MODEL
ROPE_THETA = 10000.0
ROPE_FREQS = HEAD_DIM // 4
N_EVEN_2 = (DEPTH + 1) // 2
N_ODD_2 = DEPTH // 2
N_MOD = 6
DEEPNORM_ALPHA = (2 * DEPTH) ** 0.25
DEEPNORM_BETA = (8 * DEPTH) ** -0.25
EPS = 1e-6


def layer_norm(x, g, b):
    xf = x.astype(jnp.float32)
    mu = jnp.mean(xf, axis=-1, keepdims=True)
    var = jnp.mean(jnp.square(xf - mu), axis=-1, keepdims=True)
    return ((xf - mu) * lax.rsqrt(var + EPS) * g + b).astype(x.dtype)

def rms_norm(x, g):
    xf = x.astype(jnp.float32)
    return (xf * lax.rsqrt(jnp.mean(xf * xf, axis=-1, keepdims=True) + EPS) * g).astype(x.dtype)

def modulate(h, shift, scale):
    return h * (1.0 + scale) + shift

def rope_tables(n_tokens):
    rows = n_tokens // GRID_W
    row = jnp.broadcast_to(jnp.arange(rows)[:, None], (rows, GRID_W)).reshape(-1).astype(jnp.float32)
    col = jnp.broadcast_to(jnp.arange(GRID_W)[None, :], (rows, GRID_W)).reshape(-1).astype(jnp.float32)
    inv_freq = ROPE_THETA ** (-jnp.arange(ROPE_FREQS, dtype=jnp.float32) / ROPE_FREQS)
    ang = jnp.stack([row, col], axis=-1)[:, :, None] * inv_freq
    return jnp.cos(ang), jnp.sin(ang)

def apply_rope_2d(x, cos, sin):
    shp = x.shape
    xs = x.astype(jnp.float32).reshape(*shp[:-1], 2, 2, ROPE_FREQS)
    x1, x2 = xs[..., 0, :], xs[..., 1, :]
    n_head_axes = x.ndim - 3
    c = cos.reshape(cos.shape[0], *([1] * n_head_axes), 2, ROPE_FREQS)
    s = sin.reshape(sin.shape[0], *([1] * n_head_axes), 2, ROPE_FREQS)
    o1 = x1 * c - x2 * s
    o2 = x2 * c + x1 * s
    return jnp.stack([o1, o2], axis=-2).reshape(shp).astype(x.dtype)

def diff_attention(q, k, v, lam, lam_init, subln_g):
    s = jnp.einsum('bqhid,bkhid->bhiqk', q, k) * (HEAD_DIM ** -0.5)
    p = jax.nn.softmax(s.astype(jnp.float32), axis=-1)
    attn = (p[:, :, 0] - lam * p[:, :, 1]).astype(v.dtype)
    o = jnp.einsum('bhqk,bkhe->bqhe', attn, v)
    o = rms_norm(o, subln_g) * (1.0 - lam_init)
    return o.reshape(o.shape[0], o.shape[1], A_WIDTH)

def gqa_attention(q, k, v):
    bsz, nq = q.shape[0], q.shape[1]
    q = q.reshape(bsz, nq, B_KV_HEADS, B_REP, HEAD_DIM)
    s = jnp.einsum('bqgrd,bkgd->bgrqk', q, k) * (HEAD_DIM ** -0.5)
    p = jax.nn.softmax(s.astype(jnp.float32), axis=-1).astype(v.dtype)
    o = jnp.einsum('bgrqk,bkgd->bqgrd', p, v)
    return o.reshape(bsz, nq, B_WIDTH)

def even_mixer_2(h_lat, h_ctx, w_in, w_out, lam_vecs, subln_g, qn_g, kn_g, lam_init, cos, sin, ctx_out):
    bsz, n_lat = h_lat.shape[0], h_lat.shape[1]

    def project(h, use_rope):
        n = h.shape[1]
        z = h @ w_in
        aq, ak, av, bq, bk, bv = jnp.split(z, IN_SPLITS, axis=-1)
        aq = aq.reshape(bsz, n, A_HEADS, 2, HEAD_DIM)
        ak = ak.reshape(bsz, n, A_HEADS, 2, HEAD_DIM)
        av = av.reshape(bsz, n, A_HEADS, A_VDIM)
        bq = rms_norm(bq.reshape(bsz, n, B_HEADS, HEAD_DIM), qn_g)
        bk = rms_norm(bk.reshape(bsz, n, B_KV_HEADS, HEAD_DIM), kn_g)
        bv = bv.reshape(bsz, n, B_KV_HEADS, HEAD_DIM)
        if use_rope:
            aq = apply_rope_2d(aq, cos, sin)
            ak = apply_rope_2d(ak, cos, sin)
            bq = apply_rope_2d(bq, cos, sin)
            bk = apply_rope_2d(bk, cos, sin)
        return aq, ak, av, bq, bk, bv

    lv = lam_vecs.astype(jnp.float32)
    lam = jnp.exp(jnp.sum(lv[0] * lv[1])) - jnp.exp(jnp.sum(lv[2] * lv[3])) + lam_init

    caq, cak, cav, cbq, cbk, cbv = project(h_ctx, False)
    laq, lak, lav, lbq, lbk, lbv = project(h_lat, True)
    ak_all = jnp.concatenate([cak, lak], axis=1)
    av_all = jnp.concatenate([cav, lav], axis=1)
    bk_all = jnp.concatenate([cbk, lbk], axis=1)
    bv_all = jnp.concatenate([cbv, lbv], axis=1)

    nb = n_lat // Q_BLOCK

    def to_blocks(t):
        return jnp.moveaxis(t.reshape(bsz, nb, Q_BLOCK, *t.shape[2:]), 1, 0)

    def block(qs):
        qa, qb = qs
        return jnp.concatenate([diff_attention(qa, ak_all, av_all, lam, lam_init, subln_g),
                                gqa_attention(qb, bk_all, bv_all)], axis=-1)

    o = lax.map(block, (to_blocks(laq), to_blocks(lbq)))
    o = jnp.moveaxis(o, 0, 1).reshape(bsz, n_lat, MIX_WIDTH)
    y_lat = o @ w_out
    y_ctx = None
    if ctx_out:
        oc = jnp.concatenate([diff_attention(caq, cak, cav, lam, lam_init, subln_g),
                              gqa_attention(cbq, cbk, cbv)], axis=-1)
        y_ctx = oc @ w_out
    return y_lat, y_ctx

def conv_mixer(h, w_in, conv_w, conv_b, w_out):
    n = h.shape[1]
    z = h @ w_in
    gate_b, gate_c, xv = jnp.split(z, 3, axis=-1)
    u = gate_c * xv
    up = jnp.pad(u, ((0, 0), (1, 1), (0, 0)))
    y = up[:, :n] * conv_w[0] + up[:, 1:n + 1] * conv_w[1] + up[:, 2:n + 2] * conv_w[2] + conv_b
    return (gate_b * y) @ w_out

def sq_relu_mlp(h, w1, w2):
    return jnp.square(jax.nn.relu(h @ w1)) @ w2

def second_inputs(seed: int = 0) -> dict:
    key = jax.random.key(seed)
    ks = jax.random.split(key, 20)
    f32 = jnp.float32
    nrm = lambda k, shp: jax.random.normal(k, shp, f32)
    d = D_MODEL
    return {
        "x": nrm(ks[0], (BATCH, SEQ, d)),
        "c": nrm(ks[1], (BATCH, d)),
        "ctx": nrm(ks[2], (BATCH, CTX_LEN, d)),
        "c_ctx": nrm(ks[3], (d,)),
        "ada_w": nrm(ks[4], (DEPTH, d, N_MOD * d)) * (0.5 * d ** -0.5),
        "ada_b": nrm(ks[5], (DEPTH, N_MOD * d)) * 0.02,
        "attn_w_in": nrm(ks[6], (N_EVEN_2, d, IN_COLS)) * d ** -0.5,
        "attn_w_out": nrm(ks[7], (N_EVEN_2, MIX_WIDTH, d)) * (MIX_WIDTH ** -0.5 * DEEPNORM_BETA),
        "diff_lambda": nrm(ks[8], (N_EVEN_2, 4, HEAD_DIM)) * 0.1,
        "diff_subln_g": 1.0 + 0.02 * nrm(ks[9], (N_EVEN_2, A_VDIM)),
        "q_norm_g": 1.0 + 0.02 * nrm(ks[10], (N_EVEN_2, HEAD_DIM)),
        "k_norm_g": 1.0 + 0.02 * nrm(ks[11], (N_EVEN_2, HEAD_DIM)),
        "conv_w_in": nrm(ks[12], (N_ODD_2, d, 3 * d)) * d ** -0.5,
        "conv_w": nrm(ks[13], (N_ODD_2, CONV_WIDTH, d)) * CONV_WIDTH ** -0.5,
        "conv_b": nrm(ks[14], (N_ODD_2, d)) * 0.02,
        "conv_w_out": nrm(ks[15], (N_ODD_2, d, d)) * (d ** -0.5 * DEEPNORM_BETA),
        "mlp_w1": nrm(ks[16], (DEPTH, d, MLP_HIDDEN)) * d ** -0.5,
        "mlp_w2": nrm(ks[17], (DEPTH, MLP_HIDDEN, d)) * (MLP_HIDDEN ** -0.5 * DEEPNORM_BETA),
        "ln_g": 1.0 + 0.02 * nrm(ks[18], (DEPTH, 2, d)),
        "ln_b": 0.02 * nrm(ks[19], (DEPTH, 2, d)),
    }

def second_block(x, c, ctx, c_ctx, ada_w, ada_b, attn_w_in, attn_w_out, diff_lambda, diff_subln_g,
              q_norm_g, k_norm_g, conv_w_in, conv_w, conv_b, conv_w_out, mlp_w1, mlp_w2, ln_g, ln_b):
    n_lat = x.shape[1]
    cos, sin = rope_tables(n_lat)
    c_act = jax.nn.silu(c)
    cc_act = jax.nn.silu(c_ctx)
    x_ctx = ctx
    for l in range(DEPTH):
        even = (l % 2 == 0)
        ctx_out = any(j % 2 == 0 for j in range(l + 1, DEPTH))
        need_ctx = even or ctx_out
        mod = (c_act @ ada_w[l] + ada_b[l])[:, None, :]
        sh1, sc1, g1, sh2, sc2, g2 = jnp.split(mod, N_MOD, axis=-1)
        h = modulate(x, sh1, sc1)
        if need_ctx:
            mod_c = cc_act @ ada_w[l] + ada_b[l]
            csh1, csc1, cg1, csh2, csc2, cg2 = jnp.split(mod_c, N_MOD, axis=-1)
            hc = modulate(x_ctx, csh1, csc1)
        if even:
            e = l // 2
            lam_init = 0.8 - 0.6 * math.exp(-0.3 * l)
            y, yc = even_mixer_2(h, hc, attn_w_in[e], attn_w_out[e], diff_lambda[e], diff_subln_g[e],
                               q_norm_g[e], k_norm_g[e], lam_init, cos, sin, ctx_out)
        else:
            o = l // 2
            y = conv_mixer(h, conv_w_in[o], conv_w[o], conv_b[o], conv_w_out[o])
            yc = conv_mixer(hc, conv_w_in[o], conv_w[o], conv_b[o], conv_w_out[o]) if ctx_out else None
        x = layer_norm(DEEPNORM_ALPHA * x + g1 * y, ln_g[l, 0], ln_b[l, 0])
        h = modulate(x, sh2, sc2)
        x = layer_norm(DEEPNORM_ALPHA * x + g2 * sq_relu_mlp(h, mlp_w1[l], mlp_w2[l]), ln_g[l, 1], ln_b[l, 1])
        if ctx_out:
            x_ctx = layer_norm(DEEPNORM_ALPHA * x_ctx + cg1 * yc, ln_g[l, 0], ln_b[l, 0])
            hc = modulate(x_ctx, csh2, csc2)
            x_ctx = layer_norm(DEEPNORM_ALPHA * x_ctx + cg2 * sq_relu_mlp(hc, mlp_w1[l], mlp_w2[l]),
                               ln_g[l, 1], ln_b[l, 1])
    return x


def setup_inputs(seed=0):
    out = dict(first_inputs(seed))
    for name, value in second_inputs(seed + 1).items():
        if name != "x":
            out[name + "_2"] = value
    return out


def reference(
    x, mix_norm, ffn_norm, final_norm, even_w_in, hgrn_lower_bounds, hgrn_out_norm,
    ret_out_norm, even_w_out, odd_w_in, cmp_pos_k, cmp_pos_v, cmp_w1_k, cmp_w2_k, cmp_w1_v,
    cmp_w2_v, odd_w_out, ffn_w_gate_up, ffn_w_down, c_2, ctx_2, c_ctx_2, ada_w_2, ada_b_2,
    attn_w_in_2, attn_w_out_2, diff_lambda_2, diff_subln_g_2, q_norm_g_2, k_norm_g_2,
    conv_w_in_2, conv_w_2, conv_b_2, conv_w_out_2, mlp_w1_2, mlp_w2_2, ln_g_2, ln_b_2,
):
    x = first_block(
        x, mix_norm, ffn_norm, final_norm, even_w_in, hgrn_lower_bounds, hgrn_out_norm,
        ret_out_norm, even_w_out, odd_w_in, cmp_pos_k, cmp_pos_v, cmp_w1_k, cmp_w2_k, cmp_w1_v,
        cmp_w2_v, odd_w_out, ffn_w_gate_up, ffn_w_down,
    )
    return second_block(
        x, c_2, ctx_2, c_ctx_2, ada_w_2, ada_b_2, attn_w_in_2, attn_w_out_2, diff_lambda_2,
        diff_subln_g_2, q_norm_g_2, k_norm_g_2, conv_w_in_2, conv_w_2, conv_b_2, conv_w_out_2,
        mlp_w1_2, mlp_w2_2, ln_g_2, ln_b_2,
    )


_drawn_inputs = setup_inputs


def setup_inputs(seed=0):
    import zlib

    import numpy as np

    out = dict(_drawn_inputs(seed))
    spreads = {}
    factors = {'ffn_norm': 2.9,
     'final_norm': 2.957,
     'hgrn_lower_bounds': 8.0,
     'hgrn_out_norm': 5.912,
     'ret_out_norm': 5.916,
     'cmp_pos_k': 64.0,
     'ctx_2': 4.413,
     'ada_b_2': 2.771,
     'diff_lambda_2': 8.0,
     'diff_subln_g_2': 64.0,
     'q_norm_g_2': 39.863,
     'k_norm_g_2': 34.915,
     'conv_b_2': 23.494,
     'cmp_pos_v': 7.491,
     'cmp_w1_k': 4.456,
     'cmp_w2_k': 4.784}
    for name, (base, spread) in spreads.items():
        noise = np.random.default_rng([zlib.crc32(name.encode()), seed]).standard_normal(out[name].shape)
        drawn = base * np.exp(spread * noise) if base else spread * noise
        out[name] = __import__('jax').numpy.asarray(drawn.astype(out[name].dtype))
    for name, factor in factors.items():
        out[name] = (out[name] * factor).astype(out[name].dtype)
    return out
```

```python
from contextlib import ExitStack

import numpy as np

import concourse.bass as bass
from concourse import mybir

F32 = mybir.dt.float32
F32R = mybir.dt.float32r
U32 = mybir.dt.uint32
ACT = mybir.ActivationFunctionType
ALU = mybir.AluOpType
AX = mybir.AxisListType

P = 128
T = 512
TT = T // P
D = 1024
KT = D // P
CTX = 256
NK = CTX + T
KEY_TILES = NK // P
HEADS_L = 4
NSA_HEADS, NSA_GROUPS, NSA_D = 16, 2, 64
CMP_BLOCK, CMP_STRIDE = 32, 16
NC = T // CMP_STRIDE - CMP_BLOCK // CMP_STRIDE + 1
CHUNK = 64
EPS = 1e-6
BIG = 1e33
ALPHA = 4 ** 0.25
LAM_INIT = 0.8 - 0.6
FFN_GROUPS = (8, 8, 6)
MLP_GROUPS = (8, 8, 8, 8)

STOP = 99
PLAN = [("hgrn_in", 16), ("ret_in", 16), ("out0", 8)]
PLAN += [(f"ffn0_{d}{g}", n) for g, w in enumerate(FFN_GROUPS) for d, n in (("up", 2 * w), ("down", 8))]
PLAN += [("nsa_in", 14), ("out1", 8)]
PLAN += [(f"ffn1_{d}{g}", n) for g, w in enumerate(FFN_GROUPS) for d, n in (("up", 2 * w), ("down", 8))]
PLAN += [("attn_in", 18), ("out2", 8)]
PLAN += [(f"mlp0_{d}{g}", 8) for g in range(4) for d in ("up", "down")]
PLAN += [("conv_in", 24), ("out3", 8)]
PLAN += [(f"mlp1_{d}{g}", 8) for g in range(4) for d in ("up", "down")]
PLAN = PLAN[:STOP]
PAIR0, PAIRS, UNITS = {}, {}, 0
for _name, _n in PLAN:
    PAIR0[_name], PAIRS[_name] = UNITS // 2, _n // 2
    UNITS += _n
LAST_PAIR = UNITS // 2 - 1
ADA = 96
ADA_REST = PAIR0["attn_in"] - ADA


def with_ada(name, first=0):
    return PAIR0[name] < PAIR0["attn_in"] and not (name == "nsa_in" and first)


def ada_skipped(name):
    return ADA_REST if PAIR0[name] > PAIR0["nsa_in"] else 0

VEC, _c = {}, 0
for _name, _n in [("mix0", 8), ("mix1", 8), ("ffn0", 8), ("ffn1", 8), ("final", 8), ("lb", 8), ("hgrn_g", 1),
                  ("ret_g", 1), ("c", 8), ("cc", 8), ("ada_b", 96), ("subln", 1), ("qn", 1), ("kn", 1),
                  ("conv_w", 24), ("conv_b", 8), ("ln_g", 32), ("ln_b", 32), ("lam", 4)]:
    VEC[_name] = _c
    _c += _n
NVEC = _c

TAB, _c = {}, 0
for _name, _n in [("ident", P), ("ones", P), ("half_ones", P), ("rot", P), ("eps", 1)]:
    TAB[_name] = _c
    _c += _n
NTAB = _c
LEVELS = (1, 2, 4, 8, 16, 32, 64)
HGRN_TAB = P * (1 + len(LEVELS))
RET_TAB = HEADS_L * T
NCP = 32
SLOPES = [2.0 ** (-8.0 * (h + 1) / NSA_HEADS) for h in range(NSA_HEADS)]


def counts_before(step):
    at, before = 0, {}
    for name, _ in PLAN:
        before[name] = at
        at += step(name)
    return before


HIDDEN_BEFORE = counts_before(lambda n: 8 if n[:3] == "mlp" and "up" in n or n == "conv_in"
                              else PAIRS[n] if "up" in n else 0)
G_BEFORE = counts_before(lambda n: 8 if n in ("ret_in", "nsa_in", "attn_in", "conv_in") else 0)
X_BEFORE = counts_before(lambda n: 1 if "down" in n or "out" in n else 0)
X_TOTAL = sum("down" in n or "out" in n for n, _ in PLAN)


NSA_JOBS = 8 * TT * 2
ATT_JOBS = 32
ROPE_TILES = [("aq", m) for m in range(4)] + [("ak", m) for m in range(4)] + [("bq", m) for m in range(4)] + [("bk", 0)]
TURNS = [[j] if j < 16 else [16 + 2 * (j - 16), 17 + 2 * (j - 16)] for j in range(ATT_JOBS)]
N_TURNS = 48


def out_tile(t):
    return t // 4 if t < 16 else 4 + (t - 16) // 8


O_READY_AT = {(4 * (u + 1) if u < 4 else 16 + 8 * (u - 3)): (u, (4 * (u + 1) if u < 4 else 16 + 8 * (u - 3)) - 1)
              for u in range(7)}


def row(ap):
    return ap.rearrange("p (a n) -> p a n", a=1)


def program(nc, dram, out):
    with ExitStack() as ctx:
        def sem(name):
            return ctx.enter_context(nc.semaphore(name))

        cursor = [nc.sbuf_base]
        cursor[0] = (cursor[0] + 63) // 64 * 64

        def size_of(shape):
            n = 4
            for k in shape[1:]:
                n *= k
            return (n + 63) // 64 * 64

        def sb(name, shape, dt=F32):
            t = nc.alloc_sbuf_tensor_at(name, shape, dt, offset=cursor[0])
            cursor[0] += size_of(shape)
            return t

        def overlay(prefix, items, start=0):
            at, made = ARENA + start, {}
            for name, shape in items:
                made[name] = nc.alloc_sbuf_tensor_at(prefix + name, shape, F32, offset=at)
                at += size_of(shape)
            assert at <= LIMIT, (prefix, at - LIMIT)
            return made

        LIMIT = nc.sbuf_usable_end() if callable(nc.sbuf_usable_end) else nc.sbuf_usable_end
        x = sb("x", [P, KT, T])
        h_hi, h_lo = sb("h_hi", [P, KT, T], F32R), sb("h_lo", [P, KT, T], F32R)
        g_hi, g_lo = sb("g_hi", [P, KT, T], F32R), sb("g_lo", [P, KT, T], F32R)
        w_raw = [sb(f"w_raw{s}", [P, KT, P]) for s in range(2)]
        w_hi = [sb(f"w_hi{s}", [P, KT, P], F32R) for s in range(2)]
        w_lo = [sb(f"w_lo{s}", [P, KT, P], F32R) for s in range(2)]
        ada_raw = sb("ada_raw", [P, KT, P])
        tab = sb("tab", [P, NTAB])
        vec = sb("vec", [P, NVEC])
        mod = sb("mod", [P, 96, 2])
        c_act = sb("c_act", [P, KT, 2])
        sb_aux = sb("aux", [P, 64])
        ARENA = cursor[0]

        banks = ctx.enter_context(nc.psum_tensor("banks", [P, 8, T], F32))
        psum = [banks[:, b, :] for b in range(8)]

        def table(name, rows=P, cols=P):
            return tab[0:rows, TAB[name]:TAB[name] + cols]

        ident, ones, half_ones, rot = (table(n) for n in ("ident", "ones", "half_ones", "rot"))

        eps = table("eps", cols=1)

        def v(name, k=0, rows=P):
            return vec[0:rows, VEC[name] + k:VEC[name] + k + 1]

        N = overlay("norm_", [("sq", [P, KT, T]), ("y", [P, KT, T]), ("xc", [P, KT, T]), ("rstd", [P, T])])
        F = overlay("ffn_", [("act", [P, 2, T]), ("hid", [P, 2, T])])
        A = overlay("hgrn_", [("q", [P, 4, T]), ("k", [P, 4, T]), ("cum", [P, 4, T]), ("d", [P, 4, T]),
                              ("v", [P, 4, T]), ("gate", [P, 4, T]), ("x0", [P, 4, T]), ("x1", [P, 4, T]),
                              ("attn", [P, 4, 10, P]), ("mask", [P, 1 + len(LEVELS), P]),
                              ("adj", [P, 4, 4, 8]), ("lb", [P, 4, 4]), ("ex", [P, 4, 2]),
                              ("o", [P, 2, T])])
        A["osq"], A["rstd"] = A["d"][:, 0, :], A["d"][:, 1, :]
        R = overlay("ret_", [("q", [P, 4, T]), ("k", [P, 4, T]), ("vt", [P, 4, T]), ("v", [P, 4, T]),
                             ("gate", [P, 4, T]), ("gamma", [P, 4, T]), ("attn", [P, 2, 1280]),
                             ("o", [P, 2, T]), ("osq", [P, T]), ("rstd", [P, T])])

        low_items = [("q", [P, 8, T]), ("ks", [P, 2, T]), ("kw", [P, 2, T]), ("raw", [P, 4, T]), ("vs", [P, TT, P]),
                     ("vw", [P, TT, P]), ("flat", [P, 2, CMP_BLOCK, NC]), ("pc", [P, 2, 8, NCP]), ("kc", [P, 2, NCP]),
                     ("vrep", [P, 4, NCP]), ("vz", [P, 4, P]), ("hid", [P, 2, NCP]), ("gates", [P, TT, 48]),
                     ("cm", [P, 2, 8]), ("cr", [P, 2, 8]), ("nm", [P, 2, 2]), ("sum", [P, 2, 2]), ("r", [P, 2, 2])]
        S = overlay("nsa_", low_items)
        NSA_HIGH = max(sum(size_of(shape) for _, shape in low_items), (3 * KT + 1) * T * 4)
        S1 = overlay("nsa1_", [("w1", [P, 2, CMP_BLOCK, P]), ("w2", [P, 2, P]), ("pos", [P, 2, CMP_BLOCK]),
                               ("glw", [P, KT, 48]), ("tab", [P, T + 4 * NCP + 16 * 4 * NCP])], NSA_HIGH)
        S2 = overlay("nsa2_", [("s", [P, 3, 2, T]), ("pt", [P, 2, 2, T]), ("pct", [P, TT, 4, P])], NSA_HIGH)
        dist = S1["tab"][:, 0:T]
        cvalid = S1["tab"][:, T:T + 4 * NCP].rearrange("p (q c) -> p q c", q=TT)
        cbias = S1["tab"][:, T + 4 * NCP:].rearrange("p (q r m c) -> p q r m c", q=TT, r=2, m=8)
        keep = [("aq", [P, 4, T]), ("bq", [P, 4, T]), ("ak", [P, 4, NK]), ("bk", [P, 2, NK]),
                ("av", [P, KEY_TILES, T]), ("bv", [P, KEY_TILES, P]), ("ao", [P, 4, T]), ("lam", [P, 4]),
                ("nm", [P, 2, 2]), ("sum", [P, 2, 2]), ("r", [P, 2, 2])]
        B2 = overlay("attn_", keep)
        ATT_HIGH = sum(size_of(shape) for _, shape in keep)
        B3 = overlay("attn1_", [("ctx", [P, KT, CTX]), ("avt", [P, 4, NK]), ("bvt", [P, NK]), ("bkt", [P, NK]),
                                ("rope", [P, 2, T]), ("sq", [P, NK]), ("rstd", [P, NK])], ATT_HIGH)
        B4 = overlay("attn2_", [("e", [P, 3, 2, NK]), ("comb", [P, 2, NK]), ("pt", [P, 2, NK]), ("osq", [P, T]),
                                ("rstd", [P, T]), ("o", [P, 2, T])], ATT_HIGH)
        C = overlay("conv_", [("u", [P, T + 2]), ("c", [P, T]), ("y", [P, KT, T]), ("hid", [P, 2, T])])
        cosines, sines = B3["rope"][:, 0, :], B3["rope"][:, 1, :]

        w_loaded = [sem(f"w_loaded{s}") for s in range(2)]
        w_hi_done, w_lo_done = sem("w_hi_done"), sem("w_lo_done")
        unit_done = sem("unit_done")
        bank_free = [sem(f"bank_free{s}") for s in range(2)]
        tab_in, x_in = sem("tab_in"), sem("x_in")
        mask_in, gamma_in = sem("mask_in"), sem("gamma_in")
        out_done = sem("out_done")
        dve_step, act_step = sem("dve_step"), sem("act_step")
        c_silu, c_hi, c_ready = sem("c_silu"), sem("c_hi"), sem("c_ready")
        ada_loaded, ada_done, ada_taken = sem("ada_loaded"), sem("ada_done"), sem("ada_taken")
        x_ready = sem("x_ready")
        sq_done, stat_done = sem("sq_done"), sem("stat_done")
        y_done, y_hi, h_ready = sem("y_done"), sem("y_hi"), sem("h_ready")
        hid_done, hid_hi, g_ready = sem("hid_done"), sem("hid_hi"), sem("g_ready")
        hg_act, hg_v, hg_f, hg_log, hg_cum = sem("hg_act"), sem("hg_v"), sem("hg_f"), sem("hg_log"), sem("hg_cum")
        lb_m, lb_e, tr_done, tr_copied = sem("lb_m"), sem("lb_e"), sem("tr_done"), sem("tr_copied")
        lv_d, lv_e, lv_x, lv_gram, lv_kept = (sem(n) for n in ("lv_d", "lv_e", "lv_x", "lv_gram", "lv_kept"))
        o_sum, o_sq, o_stat, o_done, o_hi = (sem(n) for n in ("o_sum", "o_sq", "o_stat", "o_done", "o_hi"))
        root_done, o_root = sem("root_done"), sem("o_root")
        nsa_in, att_in, ctx_in, ctx_h = sem("nsa_in"), sem("att_in"), sem("ctx_in"), sem("ctx_h")
        vt_done, vt_copied, gl_done, gl_ready = sem("vt_done"), sem("vt_copied"), sem("gl_done"), sem("gl_ready")
        flat_done, cmp_sum, cmp_act, cmp_out, cmp_kept = (sem(n) for n in ("flat_done", "cmp_sum", "cmp_act",
                                                                          "cmp_out", "cmp_kept"))
        c_s, c_sub, c_exp, c_p, c_turned, c_kept = (sem(n) for n in ("c_s", "c_sub", "c_exp", "c_p", "c_turned",
                                                                    "c_kept"))
        n_s, n_max, n_exp, n_p, n_t, n_tk, n_o = (sem(n) for n in ("n_s", "n_max", "n_exp", "n_p", "n_t", "n_tk",
                                                                  "n_o"))
        n_hi = sem("n_hi")
        a_s, a_max, a_exp, a_p, a_t, a_tk, a_o, a_hi = (sem(n) for n in ("a_s", "a_max", "a_exp", "a_p", "a_t",
                                                                        "a_tk", "a_o", "a_hi"))
        mean_done, xc_done, x_new = sem("mean_done"), sem("xc_done"), sem("x_new")
        rope_rot, rope_sq, rope_st, rope_root, rope_n, rope_done = (sem(n) for n in (
            "rope_rot", "rope_sq", "rope_st", "rope_root", "rope_n", "rope_done"))
        lam_prod, lam_sum, lam_exp, u_done = sem("lam_prod"), sem("lam_sum"), sem("lam_exp"), sem("u_done")
        f_sq, f_stat, f_root, f_o, f_hi = (sem(n) for n in ("f_sq", "f_stat", "f_root", "f_o", "f_hi"))
        ret_in, ret_s, ret_a = sem("ret_in"), sem("ret_s"), sem("ret_a")

        h_mod, hid_lo = sem("h_mod"), sem("hid_lo")
        turned = banks[:, 6:8, :].rearrange("p b t -> p (b t)")[:, 0:NK]
        aux = sb_aux

        def rope_raw(kind, m):
            return {"aq": B2["aq"][:, m, :], "ak": B2["ak"][:, m, :], "bq": B2["bq"][:, m, :],
                    "bk": B3["bkt"][:]}[kind]

        block = ctx.enter_context(nc.Block())

        @block.sync
        def _(sp):
            for s in range(2):
                sp.dma_start(w_raw[s][:], dram["weights"][s]).then_inc(w_loaded[s], 16)
            with sp.Fori(1, LAST_PAIR + 1) as i:
                for s in range(2):
                    sp.wait_ge(w_lo_done, 2 * i + s - 1)
                    sp.dma_start(w_raw[s][:], dram["weights"][bass.ds(2 * i + s, 1)].rearrange(
                        "a p (k n) -> p (a k) n", n=P)).then_inc(w_loaded[s], 16)
            sp.wait_ge(x_new, 5 * KT)
            sp.dma_start(out.rearrange("(k p) t -> p k t", p=P), x[:]).then_inc(out_done, 16)
            sp.wait_ge(out_done, 16)

        @block.gpsimd
        def _(pool):
            pool.dma_start(ada_raw[:], dram["ada"][0]).then_inc(ada_loaded, 16)
            with pool.Fori(1, ADA) as a:
                pool.wait_ge(ada_done, a)
                pool.dma_start(ada_raw[:], dram["ada"][bass.ds(a, 1)].rearrange("a p (k n) -> p (a k) n", n=P))\
                    .then_inc(ada_loaded, 16)

        @block.scalar
        def _(act):
            steps = [0]

            def landed(ins):
                ins.then_inc(act_step, 1)
                steps[0] += 1
                act.wait_ge(act_step, steps[0])

            act.dma_start(vec[:], dram["vecs"]).then_inc(tab_in, 16)
            act.dma_start(tab[:], dram["tables"]).then_inc(tab_in, 16)
            act.dma_start(x[:], dram["x"].rearrange("(k p) t -> p k t", p=P)).then_inc(x_in, 16)
            act.dma_start(A["mask"][:], dram["hgrn_tab"].rearrange("p (l n) -> p l n", n=P)).then_inc(mask_in, 16)

            def split_hi(i, s):
                act.wait_ge(w_loaded[s], 16 * i + 16)
                if not isinstance(i, int) or i > 0:
                    act.wait_ge(unit_done, 2 * i + s - 1)
                act.activation(w_hi[s][:], w_raw[s][:], ACT.Copy).then_inc(w_hi_done, 1)

            def split_next(i, s):
                if s == 0:
                    split_hi(i, 1)
                elif not isinstance(i, int) or i < LAST_PAIR:
                    split_hi(i + 1, 0)

            def pairs(name, body, first=0, count=None):
                p0 = PAIR0[name] + first
                p1 = PAIR0[name] + PAIRS[name] if count is None else p0 + count
                if p0 == 0:
                    for s in range(2):
                        split_next(0, s)
                        body(0, s, s)
                    p0 = 1
                tail = p1 - 1 == LAST_PAIR
                with act.Fori(p0, p1 - tail) as i:
                    for s in range(2):
                        split_next(i, s)
                        body(i, s, 2 * (i - PAIR0[name]) + s)
                if tail:
                    for s in range(2):
                        split_next(LAST_PAIR, s)
                        body(LAST_PAIR, s, 2 * (LAST_PAIR - PAIR0[name]) + s)

            def nothing(i, s, m):
                pass

            def norm(r, before):
                if before is None:
                    act.wait_ge(x_in, 16)
                else:
                    act.wait_ge(x_ready, X_BEFORE[before])
                for k in range(KT):
                    act.activation(N["sq"][:, k, :], x[:, k, :], ACT.Square).then_inc(sq_done, 1)
                act.wait_ge(stat_done, r + 1)
                act.activation(N["rstd"][:], psum[2], ACT.Sqrt, bias=eps, scale=1.0 / D).then_inc(root_done, 1)
                for k in range(KT):
                    act.wait_ge(y_done, KT * r + k + 1)
                    act.activation(h_hi[:, k, :], N["y"][:, k, :], ACT.Copy).then_inc(y_hi, 1)

            def head_norm(n):
                bank = psum[6 + n % 2]
                B = A if n < 4 else R
                act.wait_ge(o_sum, n + 1)
                if n > 0:
                    act.wait_ge(o_stat, n)
                act.activation(B["osq"][:], bank, ACT.Square).then_inc(o_sq, 1)
                act.wait_ge(o_stat, n + 1)
                act.activation(B["rstd"][:], psum[4 + n % 2], ACT.Sqrt, bias=eps, scale=1.0 / P).then_inc(o_root, 1)
                act.wait_ge(o_done, n + 1)
                act.activation(g_hi[:, n, :], B["o"][:, n % 2, :], ACT.Copy).then_inc(o_hi, 1)

            act.wait_ge(tab_in, 32)
            for j, name in enumerate(("c", "cc")):
                src = vec[:, VEC[name]:VEC[name] + KT]
                act.activation(c_act[:, :, j], src, ACT.Silu).then_inc(c_silu, 1)
            split_hi(0, 0)

            norm(0, None)

            act.wait_ge(lb_m, 2)
            act.activation(A["ex"][:], A["ex"][:], ACT.Exp).then_inc(lb_e, 1)

            def take(dst, func):
                def body(i, s, m):
                    act.wait_ge(unit_done, 2 * i + s + 1)
                    act.activation(dst(m), row(psum[s]), func).then_inc(bank_free[s], 1)
                return body

            def sig(i, s, m):
                act.wait_ge(unit_done, 2 * i + s + 1)
                act.activation(A["k"][:, bass.ds(m - 4, 1), :], row(psum[s]), ACT.Sigmoid).then_inc(bank_free[s], 1)

            pairs("hgrn_in", take(lambda m: A["q"][:, bass.ds(m, 1), :], ACT.Silu), 0, 2)
            pairs("hgrn_in", sig, 2, 2)
            pairs("hgrn_in", nothing, 4, 2)
            pairs("hgrn_in", take(lambda m: A["gate"][:, bass.ds(m - 12, 1), :], ACT.Silu), 6, 2)
            act.wait_ge(hg_f, 4)
            act.activation(A["cum"][:], A["cum"][:], ACT.Ln).then_inc(hg_log, 1)
            for e in range(1, 10):
                act.wait_ge(lv_d, 2 * e)
                act.activation(A["d"][:], A["d"][:], ACT.Exp).then_inc(lv_e, 1)
            for n in range(4):
                head_norm(n)

            act.wait_ge(o_stat, 4)
            act.dma_start(R["gamma"][:], dram["ret_tab"].rearrange("p (h t) -> p h t", t=T)).then_inc(gamma_in, 16)
            pairs("ret_in", nothing, 0, 6)
            pairs("ret_in", take(lambda m: R["gate"][:, bass.ds(m - 12, 1), :], ACT.Silu), 6, 2)
            for n in range(4, 8):
                head_norm(n)
            pairs("out0", nothing)

            def ffn(layer, groups):
                for g, w in enumerate(groups):
                    name = f"ffn{layer}_up{g}"

                    def gate(i, s, m, base=HIDDEN_BEFORE[name]):
                        if s == 0:
                            act.wait_ge(unit_done, 2 * i + 1)
                            act.activation(F["act"][:, 0, :], psum[0], ACT.Silu).then_inc(bank_free[0], 1)
                        else:
                            h = i - PAIR0[name]
                            act.wait_ge(hid_done, base + h + 1)
                            act.activation(g_hi[:, bass.ds(h, 1), :], row(F["hid"][:, 0, :]), ACT.Copy)\
                               .then_inc(hid_hi, 1)
                    pairs(name, gate)
                    pairs(f"ffn{layer}_down{g}", nothing)

            norm(1, "ffn0_up0")
            act.dma_start(S1["w1"][:], dram["cmp_w1"].rearrange("p (b k n) -> p b k n", b=2, n=P)).then_inc(nsa_in, 16)
            act.dma_start(S1["w2"][:], dram["cmp_w2"].rearrange("p (b n) -> p b n", b=2)).then_inc(nsa_in, 16)
            act.dma_start(S1["pos"][:], dram["cmp_pos"].rearrange("p (b n) -> p b n", b=2)).then_inc(nsa_in, 16)
            act.dma_start(S1["glw"][:], dram["gate_w"].rearrange("p (k n) -> p k n", k=KT)).then_inc(nsa_in, 16)
            act.dma_start(S1["tab"][:], dram["nsa_tab"]).then_inc(nsa_in, 16)
            ffn(0, FFN_GROUPS)
            norm(2, "nsa_in")

            pairs("nsa_in", nothing)
            act.wait_ge(gl_done, 1)
            act.activation(S["gates"][:], psum[2][:, 0:TT * 48].rearrange("p (q n) -> p q n", q=TT), ACT.Sigmoid)\
               .then_inc(gl_ready, 1)
            for b in range(2):
                act.wait_ge(cmp_sum, b + 1)
                act.activation(S["hid"][:, b, 0:NC], psum[4 + b][:, 0:NC], ACT.Silu).then_inc(cmp_act, 1)
            for qi in range(TT):
                act.wait_ge(c_sub, qi + 1)
                act.activation(S["pc"][:], S["pc"][:], ACT.Exp).then_inc(c_exp, 1)
            for j in range(NSA_JOBS + 2):
                if j < NSA_JOBS:
                    qi, W = (j // 2) % TT, P * ((j // 2) % TT + 1)
                    act.wait_ge(n_max, j + 1)
                    if j > 1:
                        act.wait_ge(n_p, 2 * j - 2)
                    for b in range(2):
                        s2 = S2["s"][:, j % 3, b, 0:W]
                        act.activation(s2, s2, ACT.Exp, bias=S["nm"][:, j % 2, b:b + 1],
                                       accum_out=S["sum"][:, j % 2, b:b + 1]).then_inc(n_exp, 1)
                if j > 1:
                    i = j - 2
                    W = P * ((i // 2) % TT + 1)
                    for b in range(2):
                        act.wait_ge(n_t, 2 * i + b + 1)
                        if i > 1:
                            act.wait_ge(n_o, i - 1)
                        act.activation(S2["pt"][:, i % 2, b, 0:W], psum[6 + b][:, 0:W], ACT.Copy).then_inc(n_tk, 1)
                    if i % 8 == 1 and i > 8:
                        m = i // 8 - 1
                        act.wait_ge(n_o, 8 * (m + 1))
                        act.activation(g_hi[:, m, :], psum[m % 2], ACT.Copy).then_inc(n_hi, 1)
            act.wait_ge(n_o, NSA_JOBS)
            act.activation(g_hi[:, 7, :], psum[1], ACT.Copy).then_inc(n_hi, 1)
            pairs("out1", nothing)
            norm(3, "ffn1_up0")
            ffn(1, FFN_GROUPS)

            act.dma_start(B3["ctx"][:], dram["ctx"].rearrange("(k p) t -> p k t", p=P)).then_inc(ctx_in, 16)
            act.dma_start(B3["rope"][:], dram["rope_tab"].rearrange("p (c t) -> p c t", c=2)).then_inc(att_in, 16)

            def settle(k, bias, scale):
                act.activation(x[:, k, :], N["y"][:, k, :], ACT.Identity, scale=scale, bias=bias).then_inc(x_new, 1)

            def norm_mod(r, before, bias, centred=True):
                act.wait_ge(x_ready, X_BEFORE[before] if before else X_TOTAL)
                for k in range(KT):
                    if centred:
                        act.wait_ge(xc_done, KT * (r - 5) + k + 1)
                    act.activation(N["sq"][:, k, :], (N["xc"] if centred else x)[:, k, :], ACT.Square)\
                       .then_inc(sq_done, 1)
                act.wait_ge(stat_done, r + 1)
                act.activation(N["rstd"][:], psum[2], ACT.Sqrt, bias=eps, scale=1.0 / D).then_inc(root_done, 1)
                for k in range(KT):
                    act.wait_ge(y_done, KT * r + k + 1)
                    settle(k, bias(k), ALPHA if before else 1.0)
                    if before:
                        act.wait_ge(h_mod, KT * (r - 4) + k + 1)
                        act.activation(h_hi[:, k, :], N["sq"][:, k, :], ACT.Copy).then_inc(y_hi, 1)

            norm_mod(4, "attn_in", lambda k: 0.0, centred=False)
            for k in range(KT):
                act.wait_ge(ctx_h, k + 1)
                act.activation(g_hi[:, k, 0:CTX], B3["ctx"][:, k, :], ACT.Copy).then_inc(c_hi, 1)

            def rope_steps():
                for n, (kind, m) in enumerate(ROPE_TILES):
                    raw = rope_raw(kind, m)
                    if kind[0] == "b":
                        u = n - 8
                        act.wait_ge(rope_done, n)
                        w = raw.shape[1]
                        act.activation(B3["sq"][:, 0:w], raw, ACT.Square).then_inc(rope_sq, 1)
                        act.wait_ge(rope_st, u + 1)
                        act.activation(B3["rstd"][:, 0:w], banks[:, 4:6, :].rearrange("p b t -> p (b t)")[:, 0:w],
                                       ACT.Sqrt, bias=eps, scale=1.0 / 64).then_inc(rope_root, 1)

            pairs("attn_in", nothing)
            act.wait_ge(lam_sum, 1)
            act.activation(B2["lam"][:, 0:2], psum[2][:, 0:2], ACT.Exp).then_inc(lam_exp, 1)
            rope_steps()

            for j in range(ATT_JOBS + 2):
                if j < ATT_JOBS:
                    if j > 1:
                        act.wait_ge(a_p, TURNS[j - 2][-1] + 1)
                    if j > 2:
                        act.wait_ge(a_t, TURNS[j - 3][-1] + 1)
                    for b in range(2):
                        act.wait_ge(a_max, 2 * j + b + 1)
                        src = banks[:, 2 + 2 * b:4 + 2 * b, :].rearrange("p a t -> p (a t)")[:, 0:NK]
                        act.activation(B4["e"][:, j % 3, b, :], src, ACT.Exp, bias=B2["nm"][:, j % 2, b:b + 1],
                                       accum_out=B2["sum"][:, j % 2, b:b + 1]).then_inc(a_exp, 1)
                if j > 1:
                    for t in TURNS[j - 2]:
                        act.wait_ge(a_t, t + 1)
                        if t > 1:
                            act.wait_ge(a_o, t - 1)
                        act.activation(B4["pt"][:, t % 2, :], turned, ACT.Copy).then_inc(a_tk, 1)
                        if O_READY_AT.get(t) is not None:
                            u, last = O_READY_AT[t]
                            act.wait_ge(a_o, last + 1)
                            dst = B2["ao"][:, u, :] if u < 4 else g_hi[:, u, :]
                            act.activation(dst, psum[u % 2], ACT.Copy).then_inc(a_hi, 1)
            act.wait_ge(a_o, N_TURNS)
            act.activation(g_hi[:, 7, :], psum[1], ACT.Copy).then_inc(a_hi, 1)
            for h in range(4):
                if h:
                    act.wait_ge(f_stat, h)
                act.activation(B4["osq"][:], B2["ao"][:, h, :], ACT.Square).then_inc(f_sq, 1)
                act.wait_ge(f_stat, h + 1)
                act.activation(B4["rstd"][:], psum[2 + h], ACT.Sqrt, bias=eps, scale=1.0 / P).then_inc(f_root, 1)
                act.wait_ge(f_o, h + 1)
                act.activation(g_hi[:, h, :], B4["o"][:, h % 2, :], ACT.Copy).then_inc(f_hi, 1)
            pairs("out2", nothing)

            def mlp(layer):
                for g in range(4):
                    name = f"mlp{layer}_up{g}"

                    def hidden(i, s, m, base=HIDDEN_BEFORE[name]):
                        act.wait_ge(unit_done, 2 * i + s + 1)
                        act.activation(F["act"][:, s, :], psum[s], ACT.Relu).then_inc(bank_free[s], 1)
                        act.wait_ge(hid_done, base + m + 1)
                        act.activation(g_hi[:, bass.ds(m, 1), :], row(F["hid"][:, s, :]), ACT.Copy).then_inc(hid_hi, 1)
                    pairs(name, hidden)
                    pairs(f"mlp{layer}_down{g}", nothing)

            def ln_bias(j):
                return lambda k: aux[:, 8 * j + k:8 * j + k + 1] if j < 3 else v("ln_b", 24 + k)

            norm_mod(5, "mlp0_up0", ln_bias(0))
            mlp(0)
            norm_mod(6, "conv_in", ln_bias(1))

            def take_c(i, s, m):
                if s == 0:
                    act.wait_ge(unit_done, 2 * i + 1)
                    act.activation(C["c"][:], psum[0], ACT.Copy).then_inc(bank_free[0], 1)
                else:
                    act.wait_ge(bank_free[1], i + 1)

            def gated(i, s, m):
                k = m - 16
                act.wait_ge(hid_done, HIDDEN_BEFORE["conv_in"] + k + 1)
                act.activation(g_hi[:, bass.ds(k, 1), :], row(C["hid"][:, s, :]), ACT.Copy).then_inc(hid_hi, 1)

            pairs("conv_in", take_c, 0, 8)
            pairs("conv_in", gated, 8, 4)
            pairs("out3", nothing)
            norm_mod(7, "mlp1_up0", ln_bias(2))
            mlp(1)
            norm_mod(8, None, ln_bias(3))

        @block.vector
        def _(dve):
            steps = [0]

            def landed(ins):
                ins.then_inc(dve_step, 1)
                steps[0] += 1
                dve.wait_ge(dve_step, steps[0])

            def split_lo(i, s):
                dve.wait_ge(w_hi_done, 2 * i + s + 1)
                dve.tensor_tensor(w_lo[s][:], w_raw[s][:], w_hi[s][:].bitcast(F32), ALU.subtract)\
                   .then_inc(w_lo_done, 1)

            def split_next(i, s):
                if s == 0:
                    split_lo(i, 1)
                elif not isinstance(i, int) or i < LAST_PAIR:
                    split_lo(i + 1, 0)

            def take_ada(name, i, first):
                if with_ada(name, first):
                    a = i - ada_skipped(name)
                    dve.wait_ge(ada_done, a + 1)
                    dve.tensor_scalar(mod[:, bass.ds(a, 1), :], row(psum[3][:, 0:2]),
                                      vec[:, bass.ds(VEC["ada_b"] + a, 1)], None, ALU.add).then_inc(ada_taken, 1)

            def pairs(name, body, first=0, count=None):
                p0 = PAIR0[name] + first
                p1 = PAIR0[name] + PAIRS[name] if count is None else p0 + count
                if p0 == 0:
                    for s in range(2):
                        split_next(0, s)
                        body(0, s, s)
                    take_ada(name, 0, first)
                    p0 = 1
                tail = p1 - 1 == LAST_PAIR
                with dve.Fori(p0, p1 - tail) as i:
                    for s in range(2):
                        split_next(i, s)
                        body(i, s, 2 * (i - PAIR0[name]) + s)
                    take_ada(name, i, first and name == "nsa_in")
                if tail:
                    for s in range(2):
                        split_next(LAST_PAIR, s)
                        body(LAST_PAIR, s, 2 * (LAST_PAIR - PAIR0[name]) + s)

            def nothing(i, s, m):
                pass

            def norm(r, gain):
                dve.wait_ge(root_done, r + 1)
                landed(dve.reciprocal(N["rstd"][:], N["rstd"][:]))

                def low(k):
                    dve.wait_ge(y_hi, KT * r + k + 1)
                    dve.tensor_tensor(h_lo[:, k, :], N["y"][:, k, :], h_hi[:, k, :].bitcast(F32), ALU.subtract)\
                       .then_inc(h_ready, 1)
                for k in range(KT):
                    dve.scalar_tensor_tensor(N["y"][:, k, :], x[:, k, :], v(gain, k), N["rstd"][:],
                                             ALU.mult, ALU.mult).then_inc(y_done, 1)
                    if k:
                        low(k - 1)
                low(KT - 1)

            def add_residual(i, s, m):
                dve.wait_ge(unit_done, 2 * i + s + 1)
                dve.tensor_tensor(x[:, bass.ds(m, 1), :], x[:, bass.ds(m, 1), :], row(psum[s]), ALU.add)\
                   .then_inc(bank_free[s], 1)

            def residual(name):
                pairs(name, add_residual)
                dve.wait_ge(bank_free[1], PAIR0[name] + PAIRS[name])
                dve.sem_inc(x_ready, 1)

            def head_norm(n):
                bank = psum[6 + n % 2]
                B = A if n < 4 else R
                dve.wait_ge(o_root, n + 1)
                landed(dve.reciprocal(B["rstd"][:], B["rstd"][:]))
                o = B["o"][:, n % 2, :]
                landed(dve.scalar_tensor_tensor(o, bank, v("hgrn_g" if n < 4 else "ret_g"), B["rstd"][:],
                                                ALU.mult, ALU.mult))
                dve.tensor_tensor(o, o, B["gate"][:, n % 4, :], ALU.mult).then_inc(o_done, 1)
                dve.wait_ge(o_hi, n + 1)
                dve.tensor_tensor(g_lo[:, n, :], o, g_hi[:, n, :].bitcast(F32), ALU.subtract).then_inc(g_ready, 1)

            split_lo(0, 0)
            norm(0, "mix0")

            lb0 = vec[:, VEC["lb"]:VEC["lb"] + 4]
            lb1 = vec[:, VEC["lb"] + 4:VEC["lb"] + 8]
            mx, den, low, rest = (A["lb"][:, :, j] for j in range(4))
            landed(dve.tensor_tensor(mx, lb0, lb1, ALU.max))
            dve.tensor_tensor(A["ex"][:, :, 0], lb0, mx, ALU.subtract).then_inc(lb_m, 1)
            dve.tensor_tensor(A["ex"][:, :, 1], lb1, mx, ALU.subtract).then_inc(lb_m, 1)
            dve.wait_ge(lb_e, 1)
            landed(dve.tensor_tensor(den, A["ex"][:, :, 0], A["ex"][:, :, 1], ALU.add))
            landed(dve.reciprocal(den, den))
            landed(dve.tensor_tensor(low, A["ex"][:, :, 0], den, ALU.mult))
            landed(dve.tensor_scalar(rest, low, -1.0, 1.0, ALU.mult, ALU.add))

            def forget(i, s, m):
                h = i * 2 + s - 2 * PAIR0["hgrn_in"] - 4
                dve.wait_ge(bank_free[s], i + 1)
                dve.tensor_scalar(A["cum"][:, bass.ds(h, 1), :], A["k"][:, bass.ds(h, 1), :],
                                  A["lb"][:, bass.ds(h, 1), 3], A["lb"][:, bass.ds(h, 1), 2], ALU.mult, ALU.add)\
                   .then_inc(hg_f, 1)
                dve.wait_ge(hg_f, h + 1)
                dve.tensor_scalar(A["k"][:, bass.ds(h, 1), :], A["cum"][:, bass.ds(h, 1), :],
                                  -1.0, 1.0, ALU.mult, ALU.add).then_inc(hg_v, 1)

            def take(dst, scale=None):
                def body(i, s, m):
                    dve.wait_ge(unit_done, 2 * i + s + 1)
                    if scale is None:
                        dve.tensor_copy(dst(m), row(psum[s])).then_inc(bank_free[s], 1)
                    else:
                        dve.tensor_scalar(dst(m), row(psum[s]), scale, None, ALU.mult).then_inc(bank_free[s], 1)
                return body

            pairs("hgrn_in", nothing, 0, 2)
            pairs("hgrn_in", forget, 2, 2)
            pairs("hgrn_in", take(lambda m: A["d"][:, bass.ds(m - 8, 1), :]), 4, 2)
            pairs("hgrn_in", nothing, 6, 2)

            def copy_turned(B, n0):
                for h in range(4):
                    dve.wait_ge(tr_done, n0 + h + 1)
                    dve.tensor_copy(B["v"][:, h, :], psum[2 + h]).then_inc(tr_copied, 1)

            copy_turned(A, 0)
            reset = A["x0"][:].rearrange("p h t -> p (h t)")
            landed(dve.memset(reset, 1.0))
            landed(dve.memset(reset.rearrange("p (c t) -> p c t", t=CHUNK)[:, :, 0:1], 0.0))
            dve.wait_ge(hg_log, 1)
            cum = A["cum"][:].rearrange("p h t -> p (h t)")
            landed(dve.tensor_tensor_scan(cum, reset, cum, 0.0, ALU.mult, ALU.add))
            total = cum.rearrange("p (h c t) -> p h c t", h=4, t=CHUNK)[:, :, :, CHUNK - 1]
            adj = A["adj"]
            fwd128, bwd128, fwd256, bwd256 = (adj[:, :, j, :] for j in range(4))
            landed(dve.memset(adj[:], 0.0))
            for c in (3, 7):
                landed(dve.tensor_copy(fwd128[:, :, c], total[:, :, c - 1]))
            for c in (0, 4):
                landed(dve.tensor_tensor(bwd128[:, :, c], total[:, :, c], total[:, :, c + 1], ALU.add))
            for c in (1, 5):
                landed(dve.tensor_copy(bwd128[:, :, c], total[:, :, c]))
            for c in (5, 6, 7):
                landed(dve.tensor_tensor(fwd256[:, :, c], fwd256[:, :, c - 1], total[:, :, c - 1], ALU.add))
            landed(dve.tensor_copy(bwd256[:, :, 3], total[:, :, 3]))
            for c in (2, 1, 0):
                landed(dve.tensor_tensor(bwd256[:, :, c], bwd256[:, :, c + 1], total[:, :, c], ALU.add))

            def halves(t, B):
                s = t[:].rearrange("p h (n s b) -> p (h n) s b", s=2, b=B)
                return s[:, :, 0, :], s[:, :, 1, :]

            def exponents(e):
                B = 1 << (e - 1)
                c0, c1 = halves(A["cum"], B)
                d0, d1 = halves(A["d"], B)
                if B < 64:
                    ref = c0[:, :, B - 1:B].broadcast_to([P, 4 * T // (2 * B), B])
                    dve.tensor_tensor(d0, ref, c0, ALU.subtract).then_inc(lv_d, 1)
                    dve.tensor_tensor(d1, c1, ref, ALU.subtract).then_inc(lv_d, 1)
                elif B == 64:
                    ref = c0[:, :, B - 1:B].broadcast_to([P, 4 * T // (2 * B), B])
                    dve.tensor_tensor(d0, ref, c0, ALU.subtract).then_inc(lv_d, 1)
                    dve.tensor_copy(d1, c1).then_inc(lv_d, 1)
                else:
                    fwd, bwd = (fwd128, bwd128) if B == 128 else (fwd256, bwd256)
                    n = B // CHUNK
                    def cut(t):
                        return t[:].rearrange("p h (m s c t) -> p h m s c t", s=2, c=n, t=CHUNK)
                    cc, dd = cut(A["cum"]), cut(A["d"])
                    last = None
                    for h in range(4):
                        for m in range(4 // n if n == 2 else 1):
                            c = 2 * n * m
                            b = bwd[:, h, c:c + n].rearrange("p (c o) -> p c o", o=1).broadcast_to([P, n, CHUNK])
                            f = fwd[:, h, c + n:c + 2 * n].rearrange("p (c o) -> p c o", o=1)\
                                .broadcast_to([P, n, CHUNK])
                            dve.tensor_tensor(dd[:, h, m, 0], b, cc[:, h, m, 0], ALU.subtract)
                            last = dve.tensor_tensor(dd[:, h, m, 1], cc[:, h, m, 1], f, ALU.add)
                    last.then_inc(lv_d, 2)

            dve.wait_ge(tr_done, 4)
            dve.wait_ge(mask_in, 16)
            for e in range(0, 11):
                if 1 <= e < 10:
                    exponents(e)
                if e:
                    for h in range(4):
                        j = 4 * (e - 1) + h
                        dve.wait_ge(lv_gram, j + 1)
                        if e > 1:
                            dve.wait_ge(lv_kept, j - 3)
                        grams, kept = psum[2 + h], A["attn"][:, h]
                        blocks = grams.rearrange("p (b n) -> p b n", n=P)
                        if e == 1:
                            mask = A["mask"][:, 0:1, :].broadcast_to([P, 4, P])
                            ins = dve.tensor_tensor(kept[:, 0:4, :], blocks, mask, ALU.mult)
                        elif e < 9:
                            mask = A["mask"][:, e - 1:e, :].bitcast(U32).broadcast_to([P, 4, P])
                            ins = dve.copy_predicated(kept[:, 0:4, :], mask, blocks)
                        elif e == 9:
                            ins = dve.tensor_copy(kept[:, 4:6, :], blocks[:, 0:2, :])
                        else:
                            ins = dve.tensor_copy(kept[:, 6:10, :], blocks)
                        ins.then_inc(lv_kept, 1)
                if 1 <= e < 10:
                    X = A["x0"] if e % 2 else A["x1"]
                    dve.wait_ge(lv_e, e)
                    B = 1 << (e - 1)
                    (e0, e1), (x0, x1) = halves(A["d"], B), halves(X, B)
                    (k0, _), (_, q1) = halves(A["k"], B), halves(A["q"], B)
                    dve.tensor_tensor(x0, e0, k0, ALU.mult).then_inc(lv_x, 1)
                    dve.tensor_tensor(x1, e1, q1, ALU.mult).then_inc(lv_x, 1)
                    dve.wait_ge(lv_x, 2 * e)
            for n in range(4):
                head_norm(n)

            dve.wait_ge(o_done, 4)
            pairs("ret_in", take(lambda m: R["q"][:, bass.ds(m, 1), :]), 0, 2)
            pairs("ret_in", take(lambda m: R["k"][:, bass.ds(m - 4, 1), :], P ** -0.5), 2, 2)
            pairs("ret_in", take(lambda m: R["vt"][:, bass.ds(m - 8, 1), :]), 4, 2)
            pairs("ret_in", nothing, 6, 2)
            copy_turned(R, 4)
            dve.wait_ge(gamma_in, 16)
            for n in range(4):
                at = 0
                for jt in range(TT):
                    w = T - P * jt
                    dve.wait_ge(ret_s, 4 * n + jt + 1)
                    if n > 1:
                        dve.wait_ge(o_sum, 4 + n - 1)
                    dve.tensor_tensor(R["attn"][:, n % 2, at:at + w], psum[2 + jt % 2][:, 0:w],
                                      R["gamma"][:, n, 0:w], ALU.mult).then_inc(ret_a, 1)
                    at += w
                if n:
                    head_norm(4 + n - 1)
            head_norm(7)
            residual("out0")

            def ffn(layer, groups):
                for g, w in enumerate(groups):
                    name = f"ffn{layer}_up{g}"

                    def hidden(i, s, m, base=HIDDEN_BEFORE[name]):
                        h = i - PAIR0[name]
                        if s == 1:
                            dve.wait_ge(bank_free[0], i + 1)
                            dve.wait_ge(unit_done, 2 * i + 2)
                            dve.tensor_tensor(F["hid"][:, 0, :], F["act"][:, 0, :], psum[1], ALU.mult)\
                               .then_inc(hid_done, 1)
                            dve.wait_ge(hid_hi, base + h + 1)
                            dve.tensor_tensor(g_lo[:, bass.ds(h, 1), :], row(F["hid"][:, 0, :]),
                                              g_hi[:, bass.ds(h, 1), :].bitcast(F32), ALU.subtract)\
                               .then_inc(bank_free[1], 1)
                    pairs(name, hidden)
                    residual(f"ffn{layer}_down{g}")

            norm(1, "ffn0")
            ffn(0, FFN_GROUPS)
            norm(2, "mix1")

            def nsa_keys(dst, bank, inc):
                n = 0
                for g in range(2):
                    for half in range(2):
                        ins = dve.tensor_copy(dst[64 * half:64 * half + 64, g, :], bank[64 * g:64 * g + 64, :])
                        n += 1
                ins.then_inc(*inc)

            pairs("nsa_in", take(lambda m: S["q"][:, bass.ds(m, 1), :], NSA_D ** -0.5), 0, 4)
            p0 = PAIR0["nsa_in"]
            slots = {0: 0, 1: 1, 3: 2, 5: 3}
            for u in range(6):
                i, s = p0 + 4 + u // 2, u % 2
                split_next(i, s)
                dve.wait_ge(unit_done, 2 * i + s + 1)
                if u in slots:
                    dve.tensor_copy(S["raw"][:, slots[u], :], psum[s]).then_inc(bank_free[s], 1)
                else:
                    nsa_keys(S["ks"] if u == 2 else S["kw"], psum[s], (bank_free[s], 1))
            dve.wait_ge(nsa_in, 80)
            dve.wait_ge(bank_free[1], p0 + 7)
            for b in range(2):
                for a in range(2):
                    src = S["raw"][:, b, 16 * a:16 * a + 16 * NC].rearrange("p (i c) -> p c i", c=16)
                    pos = S1["pos"][:, b, 16 * a:16 * a + 16].rearrange("p (c o) -> p c o", o=1)\
                        .broadcast_to([P, 16, NC])
                    dve.tensor_tensor(S["flat"][:, b, 16 * a:16 * a + 16, :], src, pos, ALU.add).then_inc(flat_done, 1)
            landed(dve.memset(S["kc"][:], 0.0))
            landed(dve.memset(S["vrep"][:], 0.0))
            landed(dve.memset(S["vz"][:], 0.0))
            for b in range(2):
                dve.wait_ge(vt_done, b + 1)
                dve.tensor_copy(S["vs" if b == 0 else "vw"][:], psum[6 + b].rearrange("p (q n) -> p q n", q=TT))\
                   .then_inc(vt_copied, 1)
            dve.wait_ge(cmp_out, 1)
            for g in range(2):
                for half in range(2):
                    landed(dve.tensor_copy(S["kc"][64 * half:64 * half + 64, g, 0:NC],
                                           psum[3][64 * g:64 * g + 64, 0:NC]))
            dve.wait_ge(cmp_out, 2)
            out_v = psum[4][:, 0:NC].rearrange("p (o n) -> p o n", o=1).broadcast_to([P, 4, NC])
            dve.tensor_copy(S["vrep"][:, :, 0:NC], out_v).then_inc(cmp_kept, 1)
            dve.wait_ge(cmp_out, 3)
            for j in range(4):
                ins = dve.tensor_copy(S["vz"][32 * j:32 * j + 32, j, :], psum[5][32 * j:32 * j + 32, 0:P])
            ins.then_inc(cmp_kept, 1)
            dve.wait_ge(gl_ready, 1)
            for qi in range(TT):
                dve.wait_ge(c_s, qi + 1)
                if qi:
                    dve.wait_ge(c_turned, qi)
                for par in range(2):
                    landed(dve.tensor_tensor(S["pc"][:, par], psum[2 + par][:, 0:256].rearrange(
                        "p (m c) -> p m c", m=8), cbias[:, qi, par], ALU.add))
                landed(dve.tensor_reduce(S["cm"][:], S["pc"][:], AX.X, ALU.max))
                cm = S["cm"][:].rearrange("p r (m o) -> p r m o", o=1).broadcast_to([P, 2, 8, NCP])
                dve.tensor_tensor(S["pc"][:], S["pc"][:], cm, ALU.subtract).then_inc(c_sub, 1)
                dve.wait_ge(c_exp, qi + 1)
                landed(dve.tensor_reduce(S["cr"][:], S["pc"][:], AX.X, ALU.add))
                landed(dve.reciprocal(S["cr"][:], S["cr"][:]))
                gate = S["gates"][:, qi, :].rearrange("p (m r c) -> p r m c", r=2, c=3)[:, :, :, 0]
                landed(dve.tensor_tensor(S["cr"][:], S["cr"][:], gate, ALU.mult))
                cr = S["cr"][:].rearrange("p r (m o) -> p r m o", o=1).broadcast_to([P, 2, 8, NCP])
                landed(dve.tensor_tensor(S["pc"][:], S["pc"][:], cr, ALU.mult))
                valid = cvalid[:, qi, :].rearrange("p (o c) -> p o c", o=1).broadcast_to([P, 16, NCP])
                pc = S["pc"][:].rearrange("p r m c -> p (r m) c")
                dve.tensor_tensor(pc, pc, valid, ALU.mult).then_inc(c_p, 1)
                dve.wait_ge(c_turned, qi + 1)
                dve.tensor_copy(S2["pct"][:, qi], psum[7].rearrange("p (g n) -> p g n", g=4)).then_inc(c_kept, 1)

            def low_out(m, ready, bank):
                dve.wait_ge(ready, m + 1)
                dve.tensor_tensor(g_lo[:, m, :], bank, g_hi[:, m, :].bitcast(F32), ALU.subtract).then_inc(g_ready, 1)

            for j in range(NSA_JOBS + 1):
                if j < NSA_JOBS:
                    m, qi, half = j // 8, (j // 2) % TT, j % 2
                    h, W = 2 * m + half, P * (qi + 1)
                    dve.wait_ge(n_s, j + 1)
                    if j > 2:
                        dve.wait_ge(n_t, 2 * (j - 2))
                    far = dist[:, T - W:T].rearrange("p (o n) -> p o n", o=1).broadcast_to([P, 2, W])
                    s2 = S2["s"][:, j % 3, :, 0:W]
                    sums = banks[:, 2 + 2 * (j % 2):4 + 2 * (j % 2), 0:W]
                    landed(dve.scalar_tensor_tensor(s2, far, -SLOPES[h], sums, ALU.mult, ALU.add))
                    dve.tensor_reduce(S["nm"][:, j % 2, :], s2, AX.X, ALU.max, negate=True).then_inc(n_max, 1)
                if j:
                    i = j - 1
                    m, qi, half = i // 8, (i // 2) % TT, i % 2
                    h, W = 2 * m + half, P * (qi + 1)
                    dve.wait_ge(n_exp, 2 * i + 2)
                    r = S["r"][:, i % 2, :]
                    landed(dve.reciprocal(r, S["sum"][:, i % 2, :]))
                    landed(dve.tensor_tensor(r, r, S["gates"][:, qi, 3 * h + 1:3 * h + 3], ALU.mult))
                    for b in range(2):
                        p = S2["s"][:, i % 3, b, 0:W]
                        dve.tensor_scalar(p, p, S["r"][:, i % 2, b:b + 1], None, ALU.mult).then_inc(n_p, 1)
                    if i % 8 == 3 and i > 8:
                        low_out(i // 8 - 1, n_hi, psum[(i // 8 - 1) % 2])
            low_out(7, n_hi, psum[1])
            residual("out1")
            norm(3, "ffn1")
            ffn(1, FFN_GROUPS)

            dve.wait_ge(ada_taken, ADA)
            for j in (1, 4, 7, 10):
                landed(dve.tensor_scalar(mod[:, 8 * j:8 * j + 8, :], mod[:, 8 * j:8 * j + 8, :], 1.0, None, ALU.add))
            lnb = vec[:, VEC["ln_b"]:VEC["ln_b"] + 32]
            landed(dve.tensor_scalar(aux[:, 0:32], lnb, ALPHA, None, ALU.mult))
            for j, (sc, sh) in enumerate(((4, 3), (7, 6), (10, 9))):
                dst = aux[:, 32 + 8 * j:40 + 8 * j]
                landed(dve.tensor_tensor(dst, lnb[:, 8 * j:8 * j + 8], mod[:, 8 * sc:8 * sc + 8, 0], ALU.mult))
                landed(dve.tensor_tensor(dst, dst, mod[:, 8 * sh:8 * sh + 8, 0], ALU.add))

            def norm_mod(r, gain, modulation, centred=True):
                if centred:
                    dve.wait_ge(mean_done, r - 4)
                    for k in range(KT):
                        dve.scalar_tensor_tensor(N["xc"][:, k, :], psum[3], -1.0 / D, x[:, k, :],
                                                 ALU.mult, ALU.add).then_inc(xc_done, 1)
                    dve.wait_ge(xc_done, KT * (r - 4))
                dve.wait_ge(root_done, r + 1)
                landed(dve.reciprocal(N["rstd"][:], N["rstd"][:]))

                def low(k):
                    dve.wait_ge(y_hi, KT * r + k + 1)
                    dve.tensor_tensor(h_lo[:, k, :], N["sq"][:, k, :], h_hi[:, k, :].bitcast(F32), ALU.subtract)\
                       .then_inc(h_ready, 1)
                for k in range(KT):
                    src = (N["xc"] if centred else x)[:, k, :]
                    dve.scalar_tensor_tensor(N["y"][:, k, :], src, gain(k), N["rstd"][:], ALU.mult, ALU.mult)\
                       .then_inc(y_done, 1)
                    if modulation:
                        dve.wait_ge(y_done, KT * r + k + 1)
                        scale, shift = modulation(k)
                        dve.tensor_scalar(N["sq"][:, k, :], N["y"][:, k, :], scale, shift, ALU.mult, ALU.add)\
                           .then_inc(h_mod, 1)
                        if k:
                            low(k - 1)
                if modulation:
                    low(KT - 1)

            def modcol(part, k, who=0):
                return mod[:, 8 * part + k, who:who + 1]

            norm_mod(4, lambda k: v("final", k), lambda k: (modcol(1, k), modcol(0, k)), centred=False)
            dve.wait_ge(ctx_in, 16)
            for k in range(KT):
                dve.tensor_scalar(B3["ctx"][:, k, :], B3["ctx"][:, k, :], modcol(1, k, 1), modcol(0, k, 1),
                                  ALU.mult, ALU.add).then_inc(ctx_h, 1)
            for k in range(KT):
                dve.wait_ge(c_hi, k + 1)
                dve.tensor_tensor(g_lo[:, k, 0:CTX], B3["ctx"][:, k, :], g_hi[:, k, 0:CTX].bitcast(F32), ALU.subtract)\
                   .then_inc(c_ready, 1)
            lam = vec[0:64, VEC["lam"]:VEC["lam"] + 4].rearrange("p (a b) -> p a b", b=2)
            dve.memset(B2["lam"][:, 2:4], 0.0).then_inc(lam_prod, 1)
            dve.wait_ge(lam_prod, 1)
            dve.tensor_tensor(B2["lam"][0:64, 2:4], lam[:, :, 0], lam[:, :, 1], ALU.mult).then_inc(lam_prod, 1)

            def take2(dst, scale=None):
                def body(i, s, m):
                    dve.wait_ge(unit_done, 2 * i + s + 1)
                    d = dst(m)
                    dve.tensor_copy(d[:, :, 0:CTX], row(psum[2 + s][:, 0:CTX]))
                    dve.tensor_copy(d[:, :, CTX:NK], row(psum[s])).then_inc(bank_free[s], 1)
                return body

            pairs("attn_in", take(lambda m: B2["aq"][:, bass.ds(m, 1), :], 0.125), 0, 2)
            pairs("attn_in", take2(lambda m: B2["ak"][:, bass.ds(m - 4, 1), :]), 2, 2)
            pairs("attn_in", take2(lambda m: B3["avt"][:, bass.ds(m - 8, 1), :]), 4, 2)
            pairs("attn_in", take(lambda m: B2["bq"][:, bass.ds(m - 12, 1), :]), 6, 2)
            i = PAIR0["attn_in"] + 8
            split_next(i, 0)
            take2(lambda m: row(B3["bkt"][:]))(i, 0, 16)
            split_next(i, 1)
            take2(lambda m: row(B3["bvt"][:]))(i, 1, 17)
            for n in range(5):
                dve.wait_ge(vt_done, 2 + n + 1)
                bank = banks[:, 4 + 2 * (n % 2):6 + 2 * (n % 2), :].rearrange("p b t -> p (b t)")[:, 0:NK]
                bank = bank.rearrange("p (k n) -> p k n", n=P)
                dst = B2["av"][:, :, n * P:(n + 1) * P] if n < 4 else B2["bv"][:]
                dve.tensor_copy(dst, bank).then_inc(vt_copied, 1)
            dve.wait_ge(lam_exp, 1)
            lc = B2["lam"]
            landed(dve.tensor_tensor(lc[:, 2:3], lc[:, 1:2], lc[:, 0:1], ALU.subtract))
            landed(dve.tensor_scalar(lc[:, 3:4], lc[:, 2:3], -LAM_INIT, None, ALU.add))
            landed(dve.tensor_scalar(lc[:, 2:3], v("subln"), 1.0 - LAM_INIT, None, ALU.mult))
            dve.wait_ge(att_in, 16)
            for n, (kind, m) in enumerate(ROPE_TILES):
                raw = rope_raw(kind, m)
                w = raw.shape[1]
                if kind[0] == "b":
                    u = n - 8
                    dve.wait_ge(rope_root, u + 1)
                    landed(dve.reciprocal(B3["rstd"][:, 0:w], B3["rstd"][:, 0:w]))
                    landed(dve.scalar_tensor_tensor(raw, raw, v("qn" if kind == "bq" else "kn"), B3["rstd"][:, 0:w],
                                                    ALU.mult, ALU.mult))
                    if kind == "bq":
                        landed(dve.tensor_scalar(raw, raw, 0.125, None, ALU.mult))
                    dve.sem_inc(rope_n, 1)
                dve.wait_ge(rope_rot, n + 1)
                lat = raw[:, w - T:w]
                landed(dve.tensor_tensor(lat, lat, cosines, ALU.mult))
                landed(dve.tensor_tensor(B3["sq"][:, 0:T], psum[2 + n % 2], sines, ALU.mult))
                ins = dve.tensor_tensor(lat, lat, B3["sq"][:, 0:T], ALU.add)
                if kind == "bk":
                    landed(ins)
                    for g in range(2):
                        for half in range(2):
                            landed(dve.tensor_copy(B2["bk"][64 * half:64 * half + 64, g, :],
                                                   raw[64 * g:64 * g + 64, :]))
                    dve.sem_inc(rope_done, 1)
                else:
                    ins.then_inc(rope_done, 1)

            def low_out2(u):
                dve.wait_ge(a_hi, u + 1)
                dve.tensor_tensor(g_lo[:, u, :], psum[u % 2], g_hi[:, u, :].bitcast(F32), ALU.subtract)\
                   .then_inc(g_ready, 1)

            for j in range(ATT_JOBS + 1):
                if j < ATT_JOBS:
                    if j > 1:
                        dve.wait_ge(a_exp, 2 * j - 2)
                    for b in range(2):
                        dve.wait_ge(a_s, 2 * j + b + 1)
                        sums = banks[:, 2 + 2 * b:4 + 2 * b, :].rearrange("p a t -> p (a t)")[:, 0:NK]
                        dve.tensor_reduce(B2["nm"][:, j % 2, b:b + 1], sums, AX.X, ALU.max, negate=True)\
                           .then_inc(a_max, 1)
                if j:
                    i = j - 1
                    dve.wait_ge(a_exp, 2 * i + 2)
                    e, r = B4["e"][:, i % 3], B2["r"][:, i % 2, :]
                    landed(dve.reciprocal(r, B2["sum"][:, i % 2, :]))
                    if i < 16:
                        landed(dve.tensor_scalar(r[:, 1:2], r[:, 1:2], lc[:, 3:4], None, ALU.mult))
                        landed(dve.tensor_scalar(e[:, 1, :], e[:, 1, :], r[:, 1:2], None, ALU.mult))
                        if i > 1:
                            dve.wait_ge(a_t, i - 1)
                        dve.scalar_tensor_tensor(B4["comb"][:, i % 2, :], e[:, 0, :], r[:, 0:1], e[:, 1, :],
                                                 ALU.mult, ALU.add).then_inc(a_p, 1)
                    else:
                        for b in range(2):
                            dve.tensor_scalar(e[:, b, :], e[:, b, :], r[:, b:b + 1], None, ALU.mult).then_inc(a_p, 1)
                        if i in (22, 26, 30):
                            low_out2(4 + (i - 22) // 4)
            low_out2(7)
            for h in range(4):
                dve.wait_ge(f_root, h + 1)
                landed(dve.reciprocal(B4["rstd"][:], B4["rstd"][:]))
                o = B4["o"][:, h % 2, :]
                dve.scalar_tensor_tensor(o, B2["ao"][:, h, :], lc[:, 2:3], B4["rstd"][:], ALU.mult, ALU.mult)\
                   .then_inc(f_o, 1)
                dve.wait_ge(f_hi, h + 1)
                dve.tensor_tensor(g_lo[:, h, :], o, g_hi[:, h, :].bitcast(F32), ALU.subtract).then_inc(g_ready, 1)

            def gated_residual(name, part):
                def body(i, s, m):
                    dve.wait_ge(unit_done, 2 * i + s + 1)
                    dve.scalar_tensor_tensor(x[:, bass.ds(m, 1), :], row(psum[s]), mod[:, bass.ds(8 * part + m, 1), 0],
                                             x[:, bass.ds(m, 1), :], ALU.mult, ALU.add).then_inc(bank_free[s], 1)
                pairs(name, body)
                dve.wait_ge(bank_free[1], PAIR0[name] + PAIRS[name])
                dve.sem_inc(x_ready, 1)

            def mlp(layer):
                for g in range(4):
                    name = f"mlp{layer}_up{g}"

                    def hidden(i, s, m, base=HIDDEN_BEFORE[name]):
                        dve.wait_ge(bank_free[s], i + 1)
                        dve.tensor_tensor(F["hid"][:, s, :], F["act"][:, s, :], F["act"][:, s, :], ALU.mult)\
                           .then_inc(hid_done, 1)
                        dve.wait_ge(hid_hi, base + m + 1)
                        dve.tensor_tensor(g_lo[:, bass.ds(m, 1), :], row(F["hid"][:, s, :]),
                                          g_hi[:, bass.ds(m, 1), :].bitcast(F32), ALU.subtract).then_inc(hid_lo, 1)
                    pairs(name, hidden)
                    gated_residual(f"mlp{layer}_down{g}", 6 * layer + 5)

            def ln_gain(j):
                return lambda k: v("ln_g", 8 * j + k)

            def ln_mod(j, sc):
                return lambda k: (modcol(sc, k), aux[:, 32 + 8 * j + k:33 + 8 * j + k])

            gated_residual("out2", 2)
            norm_mod(5, ln_gain(0), ln_mod(0, 4))
            mlp(0)
            norm_mod(6, ln_gain(1), ln_mod(1, 7))

            dve.wait_ge(h_ready, 7 * KT)
            landed(dve.memset(C["u"][:, 0:1], 0.0))
            landed(dve.memset(C["u"][:, T + 1:T + 2], 0.0))

            def convolve(i, s, m):
                if s == 1:
                    k = i - PAIR0["conv_in"]
                    dve.wait_ge(bank_free[0], i + 1)
                    dve.wait_ge(unit_done, 2 * i + 2)
                    dve.tensor_tensor(C["u"][:, 1:T + 1], C["c"][:], psum[1], ALU.mult).then_inc(bank_free[1], 1)
                    dve.wait_ge(bank_free[1], i + 1)
                    y = C["y"][:, bass.ds(k, 1), :]
                    for n in range(3):
                        u = row(C["u"][:, n:n + T])
                        gain = vec[:, bass.ds(VEC["conv_w"] + 8 * n + k, 1)]
                        if n == 0:
                            ins = dve.tensor_scalar(y, u, gain, vec[:, bass.ds(VEC["conv_b"] + k, 1)], ALU.mult, ALU.add)
                        else:
                            ins = dve.scalar_tensor_tensor(y, u, gain, y, ALU.mult, ALU.add)
                        ins.then_inc(u_done, 1)
                        dve.wait_ge(u_done, 3 * k + n + 1)

            def gated(i, s, m):
                k = m - 16
                dve.wait_ge(unit_done, 2 * i + s + 1)
                dve.tensor_tensor(row(C["hid"][:, s, :]), C["y"][:, bass.ds(k, 1), :], row(psum[s]), ALU.mult)\
                   .then_inc(hid_done, 1)
                dve.wait_ge(hid_hi, HIDDEN_BEFORE["conv_in"] + k + 1)
                dve.tensor_tensor(g_lo[:, bass.ds(k, 1), :], row(C["hid"][:, s, :]),
                                  g_hi[:, bass.ds(k, 1), :].bitcast(F32), ALU.subtract).then_inc(g_ready, 1)
                dve.wait_ge(g_ready, G_BEFORE["conv_in"] + k + 1)
                dve.sem_inc(bank_free[s], 1)

            pairs("conv_in", convolve, 0, 8)
            pairs("conv_in", gated, 8, 4)
            gated_residual("out3", 8)
            norm_mod(7, ln_gain(2), ln_mod(2, 10))
            mlp(1)
            norm_mod(8, ln_gain(3), None)

        @block.tensor
        def _(pe):
            def unit(i, s, moving, kts=KT, fresh=None):
                pe.wait_ge(w_lo_done, 2 * i + s + 1)
                if not isinstance(i, int) or i > 0:
                    pe.wait_ge(bank_free[s], i)
                for bank, hi, lo in moving:
                    for n, k in enumerate(fresh[2][:kts] if fresh else range(kts)):
                        if fresh:
                            pe.wait_ge(fresh[0], fresh[1] + n + 1)
                        for a, (w, m) in enumerate(((w_hi, hi), (w_hi, lo), (w_lo, hi))):
                            mm = pe.matmul(bank, w[s][:, k, :], m[:, k, :], start=(n == 0 and a == 0),
                                           stop=(n == kts - 1 and a == 2))
                mm.then_inc(unit_done, 1)

            def ada_unit(name, i, first):
                if with_ada(name, first):
                    a = i - ada_skipped(name)
                    pe.wait_ge(ada_loaded, 16 * a + 16)
                    if not isinstance(a, int) or a > 0:
                        pe.wait_ge(ada_taken, a)
                    for k in range(KT):
                        mm = pe.matmul(psum[3][:, 0:2], ada_raw[:, k, :], c_act[:, k, :], start=(k == 0),
                                       stop=(k == KT - 1))
                    mm.then_inc(ada_done, 1)

            IN_ORDER = tuple(range(KT))

            def pairs(name, hi, lo, kts=KT, first=0, count=None, fresh=None):
                p0 = PAIR0[name] + first
                p1 = PAIR0[name] + PAIRS[name] if count is None else p0 + count
                if fresh:
                    unit(p0, 0, [(psum[0], hi, lo)], kts, fresh)
                    ada_unit(name, p0, first)
                    unit(p0, 1, [(psum[1], hi, lo)], kts)
                    p0 += 1
                with pe.Fori(p0, p1) as i:
                    unit(i, 0, [(psum[0], hi, lo)], kts)
                    ada_unit(name, i, first)
                    unit(i, 1, [(psum[1], hi, lo)], kts)

            def norm(r):
                for k in range(KT):
                    pe.wait_ge(sq_done, KT * r + k + 1)
                    mm = pe.matmul(psum[2], ones, N["sq"][:, k, :], start=(k == 0), stop=(k == KT - 1))
                mm.then_inc(stat_done, 1)

            def turn(B, name, n0, ready):
                pe.wait_ge(ada_taken, ready + 4)
                for h in range(4):
                    pe.wait_ge(bank_free[h % 2], ready + h // 2 + 1)
                    for t in range(TT):
                        mm = pe.transpose(psum[2 + h][:, t * P:(t + 1) * P], B[name][:, h, t * P:(t + 1) * P], ident)
                    mm.then_inc(tr_done, 1)

            def stat(n):
                B = A if n < 4 else R
                pe.wait_ge(o_sq, n + 1)
                if n > 1:
                    pe.wait_ge(o_done, n - 1)
                pe.matmul(psum[4 + n % 2], ones, B["osq"][:], start=True, stop=True).then_inc(o_stat, 1)

            pe.wait_ge(c_silu, 2)
            norm(0)
            pairs("hgrn_in", h_hi, h_lo, fresh=(h_ready, 0, IN_ORDER))
            turn(A, "d", 0, PAIR0["hgrn_in"] + 4)
            for e in range(10):
                if e:
                    pe.wait_ge(lv_x, 2 * e)
                else:
                    pe.wait_ge(hg_v, 4)
                    pe.wait_ge(tr_copied, 4)
                for h in range(4):
                    grams = psum[2 + h]
                    if e:
                        pe.wait_ge(lv_kept, 4 * (e - 1) + h + 1)
                    X = A["x0"] if e % 2 else A["x1"]
                    left, right = (A["k"], A["q"]) if e == 0 else (X, X)

                    def cols(t, n=1):
                        return slice(t * P, (t + n) * P)
                    if e < 8:
                        for t in range(TT):
                            mm = pe.matmul(grams[:, cols(t)], left[:, h, cols(t)], right[:, h, cols(t)],
                                           start=True, stop=True)
                    elif e == 8:
                        for t in (0, 2):
                            mm = pe.matmul(grams[:, cols(t // 2)], X[:, h, cols(t)], X[:, h, cols(t + 1)],
                                           start=True, stop=True)
                    else:
                        for t in (0, 1):
                            mm = pe.matmul(grams[:, cols(2 * t, 2)], X[:, h, cols(t)], X[:, h, cols(2, 2)],
                                           start=True, stop=True)
                    mm.then_inc(lv_gram, 1)
            where = {(t, t): t for t in range(4)} | {(0, 1): 4, (2, 3): 5, (0, 2): 6, (0, 3): 7, (1, 2): 8, (1, 3): 9}
            for n in range(4):
                pe.wait_ge(lv_kept, 40)
                if n > 1:
                    pe.wait_ge(o_done, n - 1)
                for it in range(TT):
                    for jt in range(it + 1):
                        mm = pe.matmul(psum[6 + n % 2][:, it * P:(it + 1) * P], A["v"][:, n, jt * P:(jt + 1) * P],
                                       A["attn"][:, n, where[jt, it], :], start=(jt == 0), stop=(jt == it))
                mm.then_inc(o_sum, 1)
                stat(n)

            pairs("ret_in", h_hi, h_lo)
            turn(R, "vt", 4, PAIR0["ret_in"] + 4)
            pe.wait_ge(tr_copied, 8)
            for n in range(4):
                for jt in range(TT):
                    w = T - P * jt
                    if 4 * n + jt >= 2:
                        pe.wait_ge(ret_a, 4 * n + jt - 1)
                    pe.matmul(psum[2 + jt % 2][:, 0:w], R["k"][:, n, jt * P:(jt + 1) * P], R["q"][:, n, jt * P:T],
                              start=True, stop=True).then_inc(ret_s, 1)
                if n > 1:
                    pe.wait_ge(o_done, 4 + n - 1)
                at = 0
                for jt in range(TT):
                    pe.wait_ge(ret_a, 4 * n + jt + 1)
                    w = T - P * jt
                    mm = pe.matmul(psum[6 + n % 2][:, jt * P:T], R["v"][:, n, jt * P:(jt + 1) * P],
                                   R["attn"][:, n % 2, at:at + w], start=(jt == 0), stop=(jt == TT - 1))
                    at += w
                mm.then_inc(o_sum, 1)
                stat(4 + n)
            pairs("out0", g_hi, g_lo, fresh=(g_ready, 0, IN_ORDER))

            def ffn(layer, groups):
                for g, w in enumerate(groups):
                    up = f"ffn{layer}_up{g}"
                    pairs(up, h_hi, h_lo, fresh=(h_ready, KT * (1 + 2 * layer), IN_ORDER) if g == 0 else None)
                    pairs(f"ffn{layer}_down{g}", g_hi, g_lo, kts=w, fresh=(bank_free[1], PAIR0[up], IN_ORDER))

            norm(1)
            ffn(0, FFN_GROUPS)
            norm(2)

            pairs("nsa_in", h_hi, h_lo, count=4, fresh=(h_ready, 2 * KT, IN_ORDER))
            pairs("nsa_in", h_hi, h_lo, first=4)
            pe.wait_ge(nsa_in, 80)
            for qi in range(TT):
                for k in range(KT):
                    for a, part in enumerate((h_hi, h_lo)):
                        mm = pe.matmul(psum[2][:, 48 * qi:48 * qi + 48], part[:, k, qi * P:(qi + 1) * P].bitcast(F32),
                                       S1["glw"][:, k, :], start=(k == 0 and a == 0), stop=(k == KT - 1 and a == 1))
            mm.then_inc(gl_done, 1)
            p0 = PAIR0["nsa_in"]
            pe.wait_ge(bank_free[1], p0 + 7)
            for b in range(2):
                for t in range(TT):
                    mm = pe.transpose(psum[6 + b][:, t * P:(t + 1) * P], S["raw"][:, 2 + b, t * P:(t + 1) * P], ident)
                mm.then_inc(vt_done, 1)
            for b in range(2):
                pe.wait_ge(flat_done, 2 * b + 2)
                for k in range(CMP_BLOCK):
                    mm = pe.matmul(psum[4 + b][:, 0:NC], S1["w1"][:, b, k, :], S["flat"][:, b, k, :],
                                   start=(k == 0), stop=(k == CMP_BLOCK - 1))
                mm.then_inc(cmp_sum, 1)
            pe.wait_ge(ada_taken, PAIR0["nsa_in"] + 4)
            for b in range(2):
                pe.wait_ge(cmp_act, 2)
                pe.matmul(psum[3 + b][:, 0:NC], S1["w2"][:, b, :], S["hid"][:, b, 0:NC],
                          start=True, stop=True).then_inc(cmp_out, 1)
            pe.wait_ge(cmp_kept, 1)
            pe.transpose(psum[5][:, 0:P], S["vrep"][:].rearrange("p j c -> p (j c)"), ident).then_inc(cmp_out, 1)
            pe.wait_ge(vt_copied, 2)
            pe.wait_ge(cmp_kept, 2)
            pe.wait_ge(gl_ready, 1)
            for qi in range(TT):
                if qi:
                    pe.wait_ge(c_sub, qi)
                for par in range(2):
                    rows = slice(64 * par, 64 * par + 64)
                    for m in range(8):
                        mm = pe.matmul(psum[2 + par][:, NCP * m:NCP * m + NCP], S["q"][rows, m, qi * P:(qi + 1) * P],
                                       S["kc"][rows, m // 4, :], start=True, stop=True)
                mm.then_inc(c_s, 1)
                pe.wait_ge(c_p, qi + 1)
                if qi:
                    pe.wait_ge(c_kept, qi)
                pc = S["pc"][:].rearrange("p r m c -> p (r m c)")
                for g in range(4):
                    mm = pe.transpose(psum[7][:, g * P:(g + 1) * P], pc[:, g * P:(g + 1) * P], ident)
                mm.then_inc(c_turned, 1)
            pe.wait_ge(c_kept, TT)
            for j in range(NSA_JOBS + 3):
                if j < NSA_JOBS:
                    m, qi, half = j // 8, (j // 2) % TT, j % 2
                    rows = slice(64 * half, 64 * half + 64)
                    if j > 1:
                        pe.wait_ge(n_max, j - 1)
                    for b, keys in enumerate((S["ks"], S["kw"])):
                        mm = pe.matmul(banks[:, 2 + 2 * (j % 2) + b, 0:P * (qi + 1)], S["q"][rows, m, qi * P:(qi + 1) * P],
                                       keys[rows, m // 4, 0:P * (qi + 1)], start=True, stop=True)
                    mm.then_inc(n_s, 1)
                if 2 <= j < NSA_JOBS + 2:
                    i = j - 2
                    qi = (i // 2) % TT
                    for b in range(2):
                        pe.wait_ge(n_p, 2 * i + b + 1)
                        if i:
                            pe.wait_ge(n_tk, 2 * (i - 1) + b + 1)
                        for t in range(qi + 1):
                            mm = pe.transpose(psum[6 + b][:, t * P:(t + 1) * P], S2["s"][:, i % 3, b, t * P:(t + 1) * P],
                                              ident)
                        mm.then_inc(n_t, 1)
                if j >= 3:
                    i = j - 3
                    m, qi, half = i // 8, (i // 2) % TT, i % 2
                    g = m // 4
                    if i % 8 == 0 and m >= 2:
                        pe.wait_ge(g_ready, G_BEFORE["nsa_in"] + m - 1)
                    pe.wait_ge(n_tk, 2 * i + 2)
                    o = psum[m % 2][64 * half:64 * half + 64, qi * P:(qi + 1) * P]
                    pe.matmul(o, S["vz"][:, m % 4, 64 * g:64 * g + 64], S2["pct"][:, qi, 2 * half + g, :],
                              start=True, stop=False)
                    for b, values in enumerate((S["vs"], S["vw"])):
                        for t in range(qi + 1):
                            mm = pe.matmul(o, values[:, t, 64 * g:64 * g + 64], S2["pt"][:, i % 2, b, t * P:(t + 1) * P],
                                           start=False, stop=(b == 1 and t == qi))
                    mm.then_inc(n_o, 1)
            pairs("out1", g_hi, g_lo, fresh=(g_ready, G_BEFORE["nsa_in"], IN_ORDER))
            norm(3)
            ffn(1, FFN_GROUPS)

            def mean(r, before):
                pe.wait_ge(x_ready, X_BEFORE[before] if before else X_TOTAL)
                for k in range(KT):
                    mm = pe.matmul(psum[3], ones, x[:, k, :], start=(k == 0), stop=(k == KT - 1))
                mm.then_inc(mean_done, 1)
                norm(r)

            norm(4)
            pe.wait_ge(h_ready, 5 * KT)
            pe.wait_ge(c_ready, KT)
            pe.wait_ge(ada_taken, ADA)
            ctx_hi, ctx_lo = g_hi[:, :, 0:CTX], g_lo[:, :, 0:CTX]

            def attn_unit(i, s, with_ctx):
                moving = [(psum[s], h_hi, h_lo)]
                if with_ctx:
                    moving.append((psum[2 + s][:, 0:CTX], ctx_hi, ctx_lo))
                unit(i, s, moving)

            p0 = PAIR0["attn_in"]
            for first, last, with_ctx in ((0, 2, False), (2, 6, True), (6, 8, False), (8, 9, True)):
                with pe.Fori(p0 + first, p0 + last) as i:
                    for s in range(2):
                        attn_unit(i, s, with_ctx)
            for n in range(5):
                pe.wait_ge(bank_free[1], p0 + 9)
                if n == 0:
                    pe.wait_ge(bank_free[0], p0 + 9)
                if n > 1:
                    pe.wait_ge(vt_copied, 2 + n - 1)
                bank = banks[:, 4 + 2 * (n % 2):6 + 2 * (n % 2), :].rearrange("p b t -> p (b t)")
                src = B3["avt"][:, n, :] if n < 4 else B3["bvt"][:]
                for t in range(KEY_TILES):
                    mm = pe.transpose(bank[:, t * P:(t + 1) * P], src[:, t * P:(t + 1) * P], ident)
                mm.then_inc(vt_done, 1)
            pe.wait_ge(lam_prod, 2)
            pe.matmul(psum[2][:, 0:2], ones, B2["lam"][:, 2:4], start=True, stop=True).then_inc(lam_sum, 1)
            pe.wait_ge(vt_copied, 7)
            pe.wait_ge(lam_exp, 1)
            for n, (kind, m) in enumerate(ROPE_TILES):
                raw = rope_raw(kind, m)
                w = raw.shape[1]
                if kind[0] == "b":
                    u = n - 8
                    pe.wait_ge(rope_sq, u + 1)
                    stat2 = banks[:, 4:6, :].rearrange("p b t -> p (b t)")
                    for c0 in range(0, w, T):
                        mm = pe.matmul(stat2[:, c0:min(c0 + T, w)], half_ones, B3["sq"][:, c0:min(c0 + T, w)],
                                       start=True, stop=True)
                    mm.then_inc(rope_st, 1)
                    pe.wait_ge(rope_n, u + 1)
                if n > 1:
                    pe.wait_ge(rope_done, n - 1)
                pe.matmul(psum[2 + n % 2], rot, raw[:, w - T:w], start=True, stop=True).then_inc(rope_rot, 1)
            pe.wait_ge(rope_done, len(ROPE_TILES))

            def turn_lot(j, t):
                b = 0 if j < 16 else t % 2
                src = B4["comb"][:, j % 2, :] if j < 16 else B4["e"][:, j % 3, b, :]
                pe.wait_ge(a_p, t + 1)
                if t:
                    pe.wait_ge(a_tk, t)
                for k in range(KEY_TILES):
                    mm = pe.transpose(turned[:, k * P:(k + 1) * P], src[:, k * P:(k + 1) * P], ident)
                mm.then_inc(a_t, 1)

            def add_lot(t):
                u = out_tile(t)
                pe.wait_ge(a_tk, t + 1)
                if u >= 2 and t in (8, 12, 16, 24, 32, 40):
                    if u < 6:
                        pe.wait_ge(a_hi, u - 1)
                    else:
                        pe.wait_ge(g_ready, G_BEFORE["attn_in"] + u - 5)
                if t < 16:
                    qi, h = t % 4, t // 4
                    o = psum[u % 2][:, qi * P:(qi + 1) * P]
                    values = B2["av"][:, :, h * P:(h + 1) * P]
                else:
                    m, qi, half = (t - 16) // 8, (t - 16) // 2 % 4, t % 2
                    o = psum[u % 2][64 * half:64 * half + 64, qi * P:(qi + 1) * P]
                    values = B2["bv"][:, :, 64 * (m // 2):64 * (m // 2) + 64]
                for k in range(KEY_TILES):
                    mm = pe.matmul(o, values[:, k, :], B4["pt"][:, t % 2, k * P:(k + 1) * P], start=(k == 0),
                                   stop=(k == KEY_TILES - 1))
                mm.then_inc(a_o, 1)

            for j in range(ATT_JOBS + 2):
                if j < ATT_JOBS:
                    qi = j % 4
                    m = j // 4 if j < 16 else (j - 16) // 4
                    for b in range(2):
                        if j:
                            pe.wait_ge(a_exp, 2 * j + b - 1)
                        rows = slice(64 * b, 64 * b + 64)
                        q = B2["aq" if j < 16 else "bq"][rows, m, qi * P:(qi + 1) * P]
                        keys = B2["ak"][rows, m, :] if j < 16 else B2["bk"][rows, m // 2, :]
                        for a, (c0, c1) in enumerate(((0, T), (T, NK))):
                            mm = pe.matmul(banks[:, 2 + 2 * b + a, 0:c1 - c0], q, keys[:, c0:c1], start=True, stop=True)
                        mm.then_inc(a_s, 1)
                if j > 1:
                    for t in TURNS[j - 2]:
                        turn_lot(j - 2, t)
                        if t:
                            add_lot(t - 1)
            add_lot(N_TURNS - 1)
            for h in range(4):
                pe.wait_ge(f_sq, h + 1)
                pe.matmul(psum[2 + h], ones, B4["osq"][:], start=True, stop=True).then_inc(f_stat, 1)
            pairs("out2", g_hi, g_lo, fresh=(g_ready, G_BEFORE["attn_in"], (4, 5, 6, 7, 0, 1, 2, 3)))

            def mlp(layer):
                for g in range(4):
                    pairs(f"mlp{layer}_up{g}", h_hi, h_lo,
                          fresh=(h_ready, KT * (6 + 2 * layer - 1), IN_ORDER) if g == 0 else None)
                    pairs(f"mlp{layer}_down{g}", g_hi, g_lo, fresh=(hid_lo, 8 * (4 * layer + g), IN_ORDER))

            mean(5, "mlp0_up0")
            mlp(0)
            mean(6, "conv_in")
            pairs("conv_in", h_hi, h_lo, fresh=(h_ready, 6 * KT, IN_ORDER))
            pairs("out3", g_hi, g_lo, fresh=(g_ready, G_BEFORE["conv_in"], IN_ORDER))
            mean(7, "mlp1_up0")
            mlp(1)
            mean(8, None)


def tiles(a, n_in=None):
    k, n = a.shape
    pad = (-k) % D
    if pad:
        a = np.concatenate([a, np.zeros((pad, n), a.dtype)])
    return a.reshape(-1, KT, P, n // P, P).transpose(0, 3, 2, 1, 4).reshape(-1, P, KT * P)


def block_diagonal(ws):
    made = []
    for a in ws:
        a = np.asarray(a)
        n = a.shape[0] // 64
        b = np.zeros((2, 64, n, 2, 64), a.dtype)
        for g in range(2):
            b[g, :, :, g, :] = a.reshape(n, 64, 64).transpose(1, 0, 2)
        made.append(b.reshape(P, n * P))
    return np.concatenate(made, 1)


def lay_out(w):
    w = {k: np.asarray(a) for k, a in w.items()}
    u = {}
    hgrn = tiles(w["even_w_in"][0])
    u["hgrn_in"], u["ret_in"] = hgrn[:16], hgrn[16:]
    u["out0"] = tiles(w["even_w_out"][0])
    for layer in range(2):
        gate_up, down = tiles(w["ffn_w_gate_up"][layer]), w["ffn_w_down"][layer]
        h0, half = 0, gate_up.shape[0] // 2
        for g, n in enumerate(FFN_GROUPS):
            u[f"ffn{layer}_up{g}"] = np.stack([gate_up[h0:h0 + n], gate_up[half + h0:half + h0 + n]], 1)\
                .reshape(2 * n, P, KT * P)
            u[f"ffn{layer}_down{g}"] = tiles(down[h0 * P:(h0 + n) * P])
            h0 += n
    u["nsa_in"] = tiles(w["odd_w_in"][0][:, :14 * P])
    u["out1"] = tiles(w["odd_w_out"][0])
    u["attn_in"], u["out2"] = tiles(w["attn_w_in_2"][0]), tiles(w["attn_w_out_2"][0])
    for layer in range(2):
        w1, w2 = tiles(w["mlp_w1_2"][layer]), tiles(w["mlp_w2_2"][layer])
        for g in range(4):
            u[f"mlp{layer}_up{g}"], u[f"mlp{layer}_down{g}"] = w1[8 * g:8 * g + 8], w2[8 * g:8 * g + 8]
    conv = tiles(w["conv_w_in_2"][0])
    u["conv_in"] = np.concatenate([np.stack([conv[8:16], conv[16:24]], 1).reshape(16, P, KT * P), conv[:8]])
    u["out3"] = tiles(w["conv_w_out_2"][0])

    def feature(a):
        return np.asarray(a).reshape(-1, P).T

    def twice(a):
        return np.concatenate([np.asarray(a).reshape(-1), np.asarray(a).reshape(-1)])[:, None]

    lam = np.asarray(w["diff_lambda_2"][0]).T
    vecs = {
        "mix0": feature(w["mix_norm"][0]), "mix1": feature(w["mix_norm"][1]), "ffn0": feature(w["ffn_norm"][0]),
        "ffn1": feature(w["ffn_norm"][1]), "final": feature(w["final_norm"]), "lb": feature(w["hgrn_lower_bounds"]),
        "hgrn_g": feature(w["hgrn_out_norm"][0]), "ret_g": feature(w["ret_out_norm"][0]), "c": feature(w["c_2"]),
        "cc": feature(w["c_ctx_2"]), "ada_b": feature(w["ada_b_2"]), "subln": feature(w["diff_subln_g_2"][0]),
        "qn": twice(w["q_norm_g_2"][0]), "kn": twice(w["k_norm_g_2"][0]), "conv_w": feature(w["conv_w_2"][0]),
        "conv_b": feature(w["conv_b_2"][0]), "ln_g": feature(w["ln_g_2"]), "ln_b": feature(w["ln_b_2"]),
        "lam": np.concatenate([lam, np.zeros_like(lam)]),
    }
    return {"weights": np.concatenate([u[name] for name, _ in PLAN]),
            "ada": np.concatenate([tiles(w["ada_w_2"][layer]) for layer in range(2)]),
            "vecs": np.concatenate([vecs[name] for name in VEC], 1),
            "cmp_w1": block_diagonal([w["cmp_w1_k"][0], w["cmp_w1_v"][0]]),
            "cmp_w2": block_diagonal([w["cmp_w2_k"][0], w["cmp_w2_v"][0]]),
            "cmp_pos": np.concatenate([np.concatenate([np.asarray(w[k][0]).T] * 2) for k in ("cmp_pos_k", "cmp_pos_v")], 1),
            "gate_w": np.asarray(w["odd_w_in"])[0][:, 14 * P:].reshape(KT, P, 48).transpose(1, 0, 2).reshape(P, -1),
            "ctx": np.asarray(w["ctx_2"])[0].T,
            "x": np.asarray(w["x"])[0].T}


def shape_tables():
    i = np.arange(P)
    eye = np.eye(P)
    half = (i[:, None] // 64 == i[None, :] // 64)
    swap = np.zeros((P, P))
    for m in range(P):
        swap[m + 16 if m % 32 < 16 else m - 16, m] = -1.0 if m % 32 < 16 else 1.0
    t = {"tables": np.concatenate([eye, np.ones((P, P)), half, swap, np.full((P, 1), EPS)], 1)}
    masks = [i[:, None] == i[None, :]]
    for B in LEVELS:
        masks.append((i[:, None] // (2 * B) == i[None, :] // (2 * B)) & (i[:, None] % (2 * B) < B)
                     & (i[None, :] % (2 * B) >= B))
    t["hgrn_tab"] = np.concatenate(masks, 1)
    log_gamma = np.log(1.0 - np.exp2(-5.0 - np.arange(HEADS_L)))
    gap = np.arange(T)[None, :] - i[:, None]
    t["ret_tab"] = np.concatenate([np.where(gap >= 0, np.exp(np.maximum(gap, 0) * g), 0.0) for g in log_gamma], 1)
    far = i[:, None] + (T - P) - np.arange(T)[None, :]
    parts = [np.where(far >= 0, far, BIG)]
    pos = np.arange(T).reshape(TT, P).T
    end = np.arange(NCP) * CMP_STRIDE + CMP_BLOCK - 1
    far_c = (pos[:, :, None] - end[None, None, :]).astype(np.float64)
    ok = (far_c >= 0) & (np.arange(NCP) < NC)
    parts.append(ok.reshape(P, -1))
    slopes = np.array(SLOPES, np.float32).reshape(8, 2).T
    bias = np.where(ok[:, :, None, None, :], -slopes[None, None, :, :, None] * far_c[:, :, None, None, :], -1e30)
    parts.append(bias.reshape(P, -1))
    t["nsa_tab"] = np.concatenate(parts, 1)
    inv = np.float32(10000.0) ** (-np.arange(16, dtype=np.float32) / np.float32(16))
    token = np.arange(T)
    where = np.stack([token // 64, token % 64]).astype(np.float32)
    angle = (where[:, None, :] * inv[None, :, None]).astype(np.float32)
    angle = np.broadcast_to(angle[None, :, None], (2, 2, 2, 16, T)).reshape(P, T)
    t["rope_tab"] = np.concatenate([np.cos(angle), np.sin(angle)], 1)
    return {k: a.astype(np.float32) for k, a in t.items()}


def kernel(**inputs):
    import numpy as _np
    import concourse.bacc as _bacc
    from concourse import mybir as _mybir
    from concourse.bass_utils import run_bass_kernel_spmd as _run

    nc = _bacc.Bacc("TRN2", target_bir_lowering=False, num_devices=1)
    arrays = {k: _np.ascontiguousarray(a) for k, a in {**lay_out(inputs), **shape_tables()}.items()}
    dram = {k: nc.dram_tensor(k, a.shape, _mybir.dt.from_np(a.dtype), kind="ExternalInput").ap()
            for k, a in arrays.items()}
    out = nc.dram_tensor("out", (D, T), _mybir.dt.float32, kind="ExternalOutput").ap()
    program(nc, dram, out)
    r = _run(nc, [arrays], core_ids=[0])
    return _np.ascontiguousarray(r.results[0]["out"].T)[None]
```

```python
from contextlib import ExitStack

import numpy as np

import concourse.bass as bass
from concourse import mybir

F32 = mybir.dt.float32
F32R = mybir.dt.float32r
U32 = mybir.dt.uint32
ACT = mybir.ActivationFunctionType
ALU = mybir.AluOpType
AX = mybir.AxisListType

P = 128
T = 512
TT = T // P
D = 1024
KT = D // P
CTX = 256
NK = CTX + T
KEY_TILES = NK // P
HEADS_L = 4
NSA_HEADS, NSA_GROUPS, NSA_D = 16, 2, 64
CMP_BLOCK, CMP_STRIDE = 32, 16
NC = T // CMP_STRIDE - CMP_BLOCK // CMP_STRIDE + 1
CHUNK = 64
EPS = 1e-6
BIG = 1e33
ALPHA = 4 ** 0.25
LAM_INIT = 0.8 - 0.6
FFN_GROUPS = (8, 8, 6)
MLP_GROUPS = (8, 8, 8, 8)

PLAN = [("hgrn_in", 16), ("ret_in", 16), ("out0", 8)]
PLAN += [(f"ffn0_{d}{g}", n) for g, w in enumerate(FFN_GROUPS) for d, n in (("up", 2 * w), ("down", 8))]
PLAN += [("nsa_in", 14), ("out1", 8)]
PLAN += [(f"ffn1_{d}{g}", n) for g, w in enumerate(FFN_GROUPS) for d, n in (("up", 2 * w), ("down", 8))]
PLAN += [("attn_in", 18), ("out2", 8)]
PLAN += [(f"mlp0_{d}{g}", 8) for g in range(4) for d in ("up", "down")]
PLAN += [("conv_in", 24), ("out3", 8)]
PLAN += [(f"mlp1_{d}{g}", 8) for g in range(4) for d in ("up", "down")]
PAIR0, PAIRS, UNITS = {}, {}, 0
for _name, _n in PLAN:
    PAIR0[_name], PAIRS[_name] = UNITS // 2, _n // 2
    UNITS += _n
LAST_PAIR = UNITS // 2 - 1
ADA = 96
ADA_REST = PAIR0["attn_in"] - ADA
assert PAIR0["out0"] == 2 * KT
ADA_BOTH = PAIR0["out0"]


def with_ada(name, first=0):
    return PAIR0[name] < PAIR0["attn_in"] and not (name == "nsa_in" and first)


def ada_skipped(name):
    return ADA_REST if PAIR0[name] > PAIR0["nsa_in"] else 0

VEC, _c = {}, 0
for _name, _n in [("mix0", 8), ("mix1", 8), ("ffn0", 8), ("ffn1", 8), ("final", 8), ("lb", 8), ("hgrn_g", 1),
                  ("ret_g", 1), ("c", 8), ("cc", 8), ("ada_b", 96), ("subln", 1), ("qn", 1), ("kn", 1),
                  ("conv_w", 24), ("conv_b", 8), ("ln_g", 32), ("ln_b", 32), ("lam", 4)]:
    VEC[_name] = _c
    _c += _n
NVEC = _c

TAB, _c = {}, 0
for _name, _n in [("ident", P), ("ones", P), ("half_ones", P), ("rot", P), ("eps", 1)]:
    TAB[_name] = _c
    _c += _n
NTAB = _c
LEVELS = (1, 2, 4, 8, 16, 32, 64)
HGRN_TAB = P * (1 + len(LEVELS))
RET_TAB = HEADS_L * T
NCP = 32
SLOPES = [2.0 ** (-8.0 * (h + 1) / NSA_HEADS) for h in range(NSA_HEADS)]


def counts_before(step):
    at, before = 0, {}
    for name, _ in PLAN:
        before[name] = at
        at += step(name)
    return before


HIDDEN_BEFORE = counts_before(lambda n: 8 if n[:3] == "mlp" and "up" in n or n == "conv_in"
                              else PAIRS[n] if "up" in n else 0)
G_BEFORE = counts_before(lambda n: 8 if n in ("ret_in", "nsa_in", "attn_in", "conv_in") else 0)


NSA_JOBS = 8 * TT * 2
ATT_JOBS = 32
ROPE_TILES = [("aq", m) for m in range(4)] + [("ak", m) for m in range(4)] + [("bk", 0)] + [("bq", m) for m in range(4)]
TURNS = [[j] if j < 16 else [16 + 2 * (j - 16), 17 + 2 * (j - 16)] for j in range(ATT_JOBS)]
N_TURNS = 48


def out_tile(t):
    return t // 4 if t < 16 else 4 + (t - 16) // 8


O_READY_AT = {(4 * (u + 1) if u < 4 else 16 + 8 * (u - 3)): (u, (4 * (u + 1) if u < 4 else 16 + 8 * (u - 3)) - 1)
              for u in range(7)}


def row(ap):
    return ap.rearrange("p (a n) -> p a n", a=1)


def program(nc, dram, out):
    with ExitStack() as ctx:
        def sem(name):
            return ctx.enter_context(nc.semaphore(name))

        cursor = [nc.sbuf_base]
        cursor[0] = (cursor[0] + 63) // 64 * 64

        def size_of(shape):
            n = 4
            for k in shape[1:]:
                n *= k
            return (n + 63) // 64 * 64

        def sb(name, shape, dt=F32):
            t = nc.alloc_sbuf_tensor_at(name, shape, dt, offset=cursor[0])
            cursor[0] += size_of(shape)
            return t

        def overlay(prefix, items, start=0):
            at, made = ARENA + start, {}
            for name, shape in items:
                made[name] = nc.alloc_sbuf_tensor_at(prefix + name, shape, F32, offset=at)
                at += size_of(shape)
            assert at <= LIMIT, (prefix, at - LIMIT)
            return made

        LIMIT = nc.sbuf_usable_end() if callable(nc.sbuf_usable_end) else nc.sbuf_usable_end
        x = sb("x", [P, KT, T])
        h_hi, h_lo = sb("h_hi", [P, KT, T], F32R), sb("h_lo", [P, KT, T], F32R)
        g_hi, g_lo = sb("g_hi", [P, KT, T], F32R), sb("g_lo", [P, KT, T], F32R)
        w_raw = [sb(f"w_raw{s}", [P, KT, P]) for s in range(2)]
        w_hi = [sb(f"w_hi{s}", [P, KT, P], F32R) for s in range(2)]
        w_lo = [sb(f"w_lo{s}", [P, KT, P], F32R) for s in range(2)]
        ada_raw = sb("ada_raw", [P, KT, P])
        ada_sum = sb("ada_sum", [P, 2, P])
        tab = sb("tab", [P, NTAB])
        vec = sb("vec", [P, NVEC])
        mod = sb("mod", [P, 96, 2])
        c_act = sb("c_act", [P, KT, 2])
        sb_aux = sb("aux", [P, 64])
        ARENA = cursor[0]

        banks = ctx.enter_context(nc.psum_tensor("banks", [P, 8, T], F32))
        psum = [banks[:, b, :] for b in range(8)]

        def table(name, rows=P, cols=P):
            return tab[0:rows, TAB[name]:TAB[name] + cols]

        ident, ones, half_ones, rot = (table(n) for n in ("ident", "ones", "half_ones", "rot"))

        eps = table("eps", cols=1)

        def v(name, k=0, rows=P):
            return vec[0:rows, VEC[name] + k:VEC[name] + k + 1]

        norm_items = [("sq", [P, KT, T]), ("s2", [P, T]), ("diag", [P, TT, P]),
                      ("r", [P, TT]), ("y", [P, KT, T])]
        centred_items = [("xc", [P, KT, T]), ("s1", [P, T]), ("st", [P, 16])]
        N = overlay("norm_", norm_items + centred_items)
        F = overlay("ffn_", [("act", [P, 2, T]), ("hid", [P, 2, T])])
        A = overlay("hgrn_", [("q", [P, 4, T]), ("k", [P, 4, T]), ("cum", [P, 4, T]), ("d", [P, 4, T]),
                              ("v", [P, 4, T]), ("gate", [P, 4, T]), ("x0", [P, 4, T]), ("x1", [P, 4, T]),
                              ("attn", [P, 4, 10, P]), ("mask", [P, 1 + len(LEVELS), P]),
                              ("adj", [P, 4, 4, 8]), ("lb", [P, 4, 4]), ("ex", [P, 4, 2]),
                              ("o", [P, 2, T])])
        A["osq"], A["rstd"] = A["d"][:, 0, :], A["d"][:, 1, :]
        R = overlay("ret_", [("q", [P, 4, T]), ("k", [P, 4, T]), ("vt", [P, 4, T]), ("v", [P, 4, T]),
                             ("gate", [P, 4, T]), ("gamma", [P, 4, T]), ("attn", [P, 2, 1280]),
                             ("o", [P, 2, T]), ("osq", [P, T]), ("rstd", [P, T])])

        low_items = [("q", [P, 8, T]), ("ks", [P, 2, T]), ("kw", [P, 2, T]), ("raw", [P, 4, T]), ("vs", [P, TT, P]),
                     ("vw", [P, TT, P]), ("flat", [P, 2, CMP_BLOCK, NC]), ("pc", [P, 2, 8, NCP]), ("kc", [P, 2, NCP]),
                     ("vz", [P, 4, P]), ("gates", [P, TT, 48]),
                     ("cm", [P, 2, 8]), ("cr", [P, 2, 8]), ("nm", [P, 2, 2]), ("sum", [P, 2, 2]), ("r", [P, 2, 2])]
        S = overlay("nsa_", low_items)
        probs = [S["pc"], S["raw"][:, 0, :].rearrange("p (r m c) -> p r m c", r=2, m=8)]
        early = S["pc"][:].rearrange("p r m c -> p (r m) c")
        S["vrep"], S["hid"] = early[:, 0:4, :], early[:, 4:6, :]
        NSA_HIGH = max(sum(size_of(shape) for _, shape in low_items), sum(size_of(shape) for _, shape in norm_items))
        S1 = overlay("nsa1_", [("w1", [P, 2, CMP_BLOCK, P]), ("w2", [P, 2, P]), ("pos", [P, 2, CMP_BLOCK]),
                               ("glw", [P, KT, 48]), ("tab", [P, T + 4 * NCP + 16 * 4 * NCP])], NSA_HIGH)
        S2 = overlay("nsa2_", [("s", [P, 3, 2, T]), ("pt", [P, 2, 2, T]), ("pct", [P, TT, 4, P])], NSA_HIGH)
        dist = S1["tab"][:, 0:T]
        cvalid = S1["tab"][:, T:T + 4 * NCP].rearrange("p (q c) -> p q c", q=TT)
        cbias = S1["tab"][:, T + 4 * NCP:].rearrange("p (q r m c) -> p q r m c", q=TT, r=2, m=8)
        keep = [("aq", [P, 4, T]), ("bq", [P, 4, T]), ("ak", [P, 4, NK]), ("bk", [P, 2, NK]),
                ("av", [P, KEY_TILES, T]), ("bv", [P, KEY_TILES, P]), ("ao", [P, 4, T]), ("lam", [P, 4]),
                ("nm", [P, 2, 2]), ("sum", [P, 2, 2]), ("r", [P, 2, 2])]
        B2 = overlay("attn_", keep)
        ATT_HIGH = sum(size_of(shape) for _, shape in keep)
        B3 = overlay("attn1_", [("ctx", [P, KT, CTX]), ("avt", [P, 4, NK]), ("bvt", [P, NK]), ("bkt", [P, NK]),
                                ("rope", [P, 2, T]), ("sq", [P, NK]), ("rstd", [P, NK])], ATT_HIGH)
        B4 = overlay("attn2_", [("e", [P, 3, 2, NK]), ("comb", [P, 2, NK]), ("pt", [P, 2, NK])], ATT_HIGH)
        spare = B4["e"][:].rearrange("p n b t -> p (n b t)")[:, 0:8 * T].rearrange("p (n t) -> p n t", t=T)
        B4["osq"], B4["rstd"], B4["o"] = spare[:, 0:4, :], spare[:, 4:8, :], B4["comb"][:, :, 0:T]
        C = overlay("conv_", [("u", [P, T + 2]), ("c", [P, T]), ("y", [P, KT, T]), ("hid", [P, 2, T])])
        cosines, sines = B3["rope"][:, 0, :], B3["rope"][:, 1, :]

        w_loaded = [sem(f"w_loaded{s}") for s in range(2)]
        w_hi_done, w_lo_done = sem("w_hi_done"), sem("w_lo_done")
        unit_done = sem("unit_done")
        bank_free = [sem(f"bank_free{s}") for s in range(2)]
        tab_in, x_in = sem("tab_in"), [sem(f"x_in{q}") for q in range(4)]
        mask_in, gamma_in = sem("mask_in"), sem("gamma_in")
        out_done = sem("out_done")
        dve_step, act_step = sem("dve_step"), sem("act_step")
        c_silu, c_hi, c_ready = sem("c_silu"), sem("c_hi"), sem("c_ready")
        ada_loaded, ada_done, ada_taken = sem("ada_loaded"), sem("ada_done"), sem("ada_taken")
        ada_added, ctx_added, ada_step, ctx_step = (sem(n) for n in ("ada_added", "ctx_added", "ada_step", "ctx_step"))
        acc_done = sem("acc_done")
        s1_done, s2_done = sem("s1_done"), sem("s2_done")
        rope_c, rope_ln, bk_copied = sem("rope_c"), sem("rope_ln"), sem("bk_copied")
        var_done, diag_done, scale_done, pool_step = (sem(n) for n in ("var_done", "diag_done", "scale_done",
                                                                      "pool_step"))
        sq_done, stat_done = sem("sq_done"), sem("stat_done")
        y_done, y_hi, h_ready = sem("y_done"), sem("y_hi"), sem("h_ready")
        hid_done, hid_hi, g_ready = sem("hid_done"), sem("hid_hi"), sem("g_ready")
        hg_v, hg_f, hg_log = sem("hg_v"), sem("hg_f"), sem("hg_log")
        lb_m, lb_e, tr_done, tr_copied = sem("lb_m"), sem("lb_e"), sem("tr_done"), sem("tr_copied")
        lv_d, lv_e, lv_x0, lv_x1, lv_gram, lv_kept = (sem(n) for n in ("lv_d", "lv_e", "lv_x0", "lv_x1", "lv_gram",
                                                                      "lv_kept"))
        o_sum, o_sq, o_stat, o_done, o_hi = (sem(n) for n in ("o_sum", "o_sq", "o_stat", "o_done", "o_hi"))
        root_done, o_root = sem("root_done"), sem("o_root")
        nsa_in, att_in, ctx_in, ctx_h = sem("nsa_in"), sem("att_in"), sem("ctx_in"), sem("ctx_h")
        vt_done, vt_copied, gl_done, gl_ready = sem("vt_done"), sem("vt_copied"), sem("gl_done"), sem("gl_ready")
        flat_done, cmp_sum, cmp_act, cmp_out, cmp_kept = (sem(n) for n in ("flat_done", "cmp_sum", "cmp_act",
                                                                          "cmp_out", "cmp_kept"))
        c_s, c_sub, c_exp, c_p, c_turned, c_kept = (sem(n) for n in ("c_s", "c_sub", "c_exp", "c_p", "c_turned",
                                                                    "c_kept"))
        n_s, n_max, n_exp, n_p, n_t, n_tk, n_o = (sem(n) for n in ("n_s", "n_max", "n_exp", "n_p", "n_t", "n_tk",
                                                                  "n_o"))
        n_hi = sem("n_hi")
        a_s, a_max, a_exp, a_p, a_t, a_tk, a_o, a_hi = (sem(n) for n in ("a_s", "a_max", "a_exp", "a_p", "a_t",
                                                                        "a_tk", "a_o", "a_hi"))
        shift_done, mean_done, xc_done, x_new = sem("shift_done"), sem("mean_done"), sem("xc_done"), sem("x_new")
        rope_rot, rope_sq, rope_st, rope_root, rope_n, rope_done = (sem(n) for n in (
            "rope_rot", "rope_sq", "rope_st", "rope_root", "rope_n", "rope_done"))
        lam_prod, lam_sum, lam_exp, u_done = sem("lam_prod"), sem("lam_sum"), sem("lam_exp"), sem("u_done")
        f_sq, f_stat, f_ln, f_root, f_o, f_hi = (sem(n) for n in ("f_sq", "f_stat", "f_ln", "f_root", "f_o", "f_hi"))
        ret_s, ret_a = sem("ret_s"), sem("ret_a")

        h_mod, hid_lo, aux_done = sem("h_mod"), sem("hid_lo"), sem("aux_done")
        turned = banks[:, 6:8, :].rearrange("p b t -> p (b t)")[:, 0:NK]
        aux = sb_aux

        def halves(t, B):
            s = t[:].rearrange("p h (n s b) -> p (h n) s b", s=2, b=B)
            return s[:, :, 0, :], s[:, :, 1, :]

        def rope_raw(kind, m):
            return {"aq": B2["aq"][:, m, :], "ak": B2["ak"][:, m, :], "bq": B2["bq"][:, m, :],
                    "bk": B3["bkt"][:]}[kind]

        def modcol(part, k, who=0):
            return mod[:, 8 * part + k, who:who + 1]

        def modulation(r, k):
            if r == 4:
                return modcol(1, k), modcol(0, k)
            return modcol(3 * r - 11, k), aux[:, 8 * r - 8 + k:8 * r - 7 + k]

        rope_cos = B3["ctx"][:].rearrange("p k t -> p (k t)").rearrange("p (b t) -> p b t", t=T)
        rope_scales = B3["avt"][:].rearrange("p k t -> p (k t)")

        def rope_scale(u):
            return rope_scales[:, 0:NK] if u == 0 else rope_scales[:, NK + (u - 1) * T:NK + u * T]

        def rope_sums(u):
            return banks[:, 0:2, :].rearrange("p b t -> p (b t)")[:, 0:NK] if u == 0 else psum[3 + u]

        block = ctx.enter_context(nc.Block())

        @block.sync
        def _(sp):
            for s in range(2):
                sp.dma_start(w_raw[s][:], dram["weights"][s]).then_inc(w_loaded[s], 16)
            with sp.Fori(1, LAST_PAIR + 1) as i:
                for s in range(2):
                    sp.wait_ge(w_lo_done, 2 * i + s - 1)
                    sp.dma_start(w_raw[s][:], dram["weights"][bass.ds(2 * i + s, 1)].rearrange(
                        "a p (k n) -> p (a k) n", n=P)).then_inc(w_loaded[s], 16)
            for k in range(KT):
                sp.wait_ge(x_new, 4 * KT + k + 1)
                sp.dma_start(out[k * P:(k + 1) * P, :], x[:, k, :]).then_inc(out_done, 16)
            sp.wait_ge(out_done, 16 * KT)

        @block.gpsimd
        def _(pool):
            steps = [0]

            def landed(ins):
                ins.then_inc(pool_step, 1)
                steps[0] += 1
                pool.wait_ge(pool_step, steps[0])

            def sums(r, centred, tiles=range(KT)):
                for k in tiles:
                    if k in (0, KT - 1):
                        continue
                    for src, acc, done, base in ((N["xc"], N["s1"], xc_done, KT * (r - 5)),
                                                 (N["sq"], N["s2"], sq_done, KT * r)):
                        if src is N["xc"] and not centred:
                            continue
                        pool.wait_ge(done, base + k + 1)
                        ins = pool.tensor_tensor(acc[:], src[:, 0, :] if k == 1 else acc[:], src[:, k, :], ALU.add)
                        if k < KT - 2:
                            landed(ins)
                        else:
                            ins.then_inc(acc_done, 1)

            def low(r, src):
                for k in range(KT):
                    pool.wait_ge(y_hi, KT * r + k + 1)
                    pool.tensor_tensor(h_lo[:, k, :], src[:, k, :], h_hi[:, k, :].bitcast(F32), ALU.subtract)\
                        .then_inc(h_ready, 1)

            def weigh(a, who, src, dst, step, added):
                vector = c_act[:, :, who:who + 1].broadcast_to([P, KT, P])
                pool.tensor_tensor(dst, src, vector, ALU.mult).then_inc(step, 1)
                for n in (4, 2, 1):
                    pool.wait_ge(step, 3 * a + (1 if n == 4 else 2 if n == 2 else 3))
                    if n > 1:
                        pool.tensor_tensor(dst[:, 0:n], dst[:, 0:n], dst[:, n:2 * n], ALU.add).then_inc(step, 1)
                    else:
                        if not isinstance(a, int) or a > 0:
                            pool.wait_ge(ada_done, a)
                        pool.tensor_tensor(row(ada_sum[:, who, :]), dst[:, 0:1], dst[:, 1:2], ALU.add)\
                            .then_inc(added, 1)

            def condition(a, room=None):
                pool.wait_ge(ada_loaded, 16 * a + 16)
                if room is not None:
                    weigh(a, 1, ada_raw[:], room, ctx_step, ctx_added)
                weigh(a, 0, ada_raw[:], ada_raw[:], ada_step, ada_added)

            def condition_pairs(name, first=0):
                a0 = PAIR0[name] - ada_skipped(name)
                with pool.Fori(a0, a0 + PAIRS[name]) as a:
                    condition(a)

            def last_product(name, r):
                a0 = PAIR0[name] - ada_skipped(name)
                for n in range(PAIRS[name]):
                    condition(a0 + n)
                    sums(r, False, (2 * n, 2 * n + 1))

            def stack_layer(layer):
                for g in range(len(FFN_GROUPS)):
                    condition_pairs(f"ffn{layer}_up{g}")
                    if g < len(FFN_GROUPS) - 1:
                        condition_pairs(f"ffn{layer}_down{g}")
                last_product(f"ffn{layer}_down{len(FFN_GROUPS) - 1}", 2 + 2 * layer)

            pool.wait_ge(c_silu, 2)
            low(0, N["y"])
            room = A["attn"][:, 0, 0:KT, :]
            condition(0, room)
            with pool.Fori(1, PAIRS["hgrn_in"]) as a:
                condition(a, room)
            for e in range(1, 10):
                pool.wait_ge(lv_e, e)
                if e > 1:
                    pool.wait_ge(lv_gram, 4 * (e - 1))
                (_, e1), (_, x1) = halves(A["d"], 1 << (e - 1)), halves(A["x0"] if e % 2 else A["x1"], 1 << (e - 1))
                _, q1 = halves(A["q"], 1 << (e - 1))
                pool.tensor_tensor(x1, e1, q1, ALU.mult).then_inc(lv_x1, 1)
            pool.wait_ge(o_done, HEADS_L)
            room = R["attn"][:, 0, 0:D].rearrange("p (k n) -> p k n", n=P)
            with pool.Fori(PAIRS["hgrn_in"], ADA_BOTH) as a:
                condition(a, room)
            last_product("out0", 1)
            low(1, N["y"])
            stack_layer(0)
            low(2, N["y"])
            with pool.Fori(PAIR0["nsa_in"], PAIR0["nsa_in"] + 4) as a:
                condition(a)
            last_product("out1", 3)
            low(3, N["y"])
            stack_layer(1)
            low(4, N["sq"])
            pool.wait_ge(att_in, 16)
            for n, (kind, m) in enumerate(ROPE_TILES):
                raw = rope_raw(kind, m)
                w = raw.shape[1]
                if kind[0] == "b":
                    pool.wait_ge(rope_n, n - 7)
                elif n == 0:
                    pool.wait_ge(vt_copied, 7)
                if n > 1:
                    pool.wait_ge(rope_done, n - 1)
                pool.tensor_tensor(rope_cos[:, n % 2, :], raw[:, w - T:w], cosines, ALU.mult).then_inc(rope_c, 1)
            for r in range(5, 9):
                sums(r, True)
                if r < 8:
                    low(r, N["sq"])

        @block.scalar
        def _(act):
            steps = [0]

            def landed(ins):
                ins.then_inc(act_step, 1)
                steps[0] += 1
                act.wait_ge(act_step, steps[0])

            act.dma_start(vec[:], dram["vecs"]).then_inc(tab_in, 16)
            act.dma_start(tab[:], dram["tables"]).then_inc(tab_in, 16)
            for q in range(4):
                part = slice(2 * q, 2 * q + 2)
                act.dma_start(x[:, part, :], dram["x"].rearrange("(k p) t -> p k t", p=P)[:, part, :])\
                   .then_inc(x_in[q], 16)
            act.dma_start(ada_raw[:], dram["ada"][0].rearrange("p (k n) -> p k n", n=P)).then_inc(ada_loaded, 16)
            act.dma_start(A["mask"][:], dram["hgrn_tab"].rearrange("p (l n) -> p l n", n=P)).then_inc(mask_in, 16)

            def split_hi(i, s):
                act.wait_ge(w_loaded[s], 16 * i + 16)
                if not isinstance(i, int) or i > 0:
                    act.wait_ge(unit_done, 2 * i + s - 1)
                act.activation(w_hi[s][:], w_raw[s][:], ACT.Copy).then_inc(w_hi_done, 1)

            def split_next(i, s):
                if s == 0:
                    split_hi(i, 1)
                elif not isinstance(i, int) or i < LAST_PAIR:
                    split_hi(i + 1, 0)

            def load_ada(name, i, first):
                if with_ada(name, first):
                    a = i - ada_skipped(name)
                    act.wait_ge(ada_added, a + 1)
                    act.dma_start(ada_raw[:], dram["ada"][bass.ds(a + 1, 1)].rearrange("a p (k n) -> p (a k) n", n=P))\
                       .then_inc(ada_loaded, 16)

            def pairs(name, body, first=0, count=None):
                p0 = PAIR0[name] + first
                p1 = PAIR0[name] + PAIRS[name] if count is None else p0 + count
                if p0 == 0:
                    for s in range(2):
                        split_next(0, s)
                        if s:
                            load_ada(name, 0, first)
                        body(0, s, s)
                    p0 = 1
                tail = p1 - 1 in (LAST_PAIR, PAIR0["attn_in"] - 1)
                with act.Fori(p0, p1 - tail) as i:
                    for s in range(2):
                        split_next(i, s)
                        if s:
                            load_ada(name, i, first and name == "nsa_in")
                        body(i, s, 2 * (i - PAIR0[name]) + s)
                if tail:
                    for s in range(2):
                        split_next(p1 - 1, s)
                        body(p1 - 1, s, 2 * (p1 - 1 - PAIR0[name]) + s)

            def nothing(i, s, m):
                pass

            def table_of_sqrt():
                act.activation(aux[:, 63:64], eps, ACT.Sqrt)

            def squares(r):
                def body(i, s, m):
                    if r > 4:
                        act.wait_ge(xc_done, KT * (r - 5) + m + 1)
                    else:
                        act.wait_ge(bank_free[s], i + 1)
                    act.activation(N["sq"][:, bass.ds(m, 1), :], (N["xc"] if r > 4 else x)[:, bass.ds(m, 1), :],
                                   ACT.Square).then_inc(sq_done, 1)
                return body

            def last_product(name, r):
                table_of_sqrt()
                pairs(name, squares(r))

            def root(r):
                if r > 4:
                    act.wait_ge(var_done, r - 4)
                    act.activation(N["r"][:], N["st"][:, 8:12], ACT.Sqrt, bias=eps).then_inc(root_done, 1)
                else:
                    act.wait_ge(stat_done, r + 1)
                    act.activation(N["r"][:], psum[2][:, 0:TT], ACT.Sqrt, bias=eps, scale=1.0 / D)\
                       .then_inc(root_done, 1)

            def norm(r):
                if r == 0:
                    for k in range(KT):
                        act.wait_ge(x_in[k // 2], 16)
                        act.activation(N["sq"][:, k, :], x[:, k, :], ACT.Square).then_inc(sq_done, 1)
                root(r)
                for k in range(KT):
                    act.wait_ge(y_done, KT * r + k + 1)
                    act.activation(h_hi[:, k, :], N["y"][:, k, :], ACT.Copy).then_inc(y_hi, 1)

            def head_norm(n):
                bank = psum[6 + n % 2]
                B = A if n < 4 else R
                act.wait_ge(o_sum, n + 1)
                if n > 0:
                    act.wait_ge(o_stat, n)
                act.activation(B["osq"][:], bank, ACT.Square).then_inc(o_sq, 1)
                act.wait_ge(o_stat, n + 1)
                act.activation(B["rstd"][:], psum[4 + n % 2], ACT.Sqrt, bias=eps, scale=1.0 / P).then_inc(o_root, 1)
                act.wait_ge(o_done, n + 1)
                act.activation(g_hi[:, n, :], B["o"][:, n % 2, :], ACT.Copy).then_inc(o_hi, 1)

            act.wait_ge(tab_in, 32)
            for j, name in enumerate(("c", "cc")):
                src = vec[:, VEC[name]:VEC[name] + KT]
                act.activation(c_act[:, :, j], src, ACT.Silu).then_inc(c_silu, 1)
            split_hi(0, 0)

            norm(0)

            act.wait_ge(lb_m, 2)
            act.activation(A["ex"][:], A["ex"][:], ACT.Exp).then_inc(lb_e, 1)

            def take(dst, func):
                def body(i, s, m):
                    act.wait_ge(unit_done, 2 * i + s + 1)
                    act.activation(dst(m), row(psum[s]), func).then_inc(bank_free[s], 1)
                return body

            def sig(i, s, m):
                act.wait_ge(unit_done, 2 * i + s + 1)
                act.activation(A["k"][:, bass.ds(m - 4, 1), :], row(psum[s]), ACT.Sigmoid).then_inc(bank_free[s], 1)

            pairs("hgrn_in", take(lambda m: A["q"][:, bass.ds(m, 1), :], ACT.Silu), 0, 2)
            pairs("hgrn_in", sig, 2, 2)
            pairs("hgrn_in", nothing, 4, 2)
            pairs("hgrn_in", take(lambda m: A["gate"][:, bass.ds(m - 12, 1), :], ACT.Silu), 6, 2)
            act.wait_ge(hg_f, 4)
            act.activation(A["cum"][:], A["cum"][:], ACT.Ln).then_inc(hg_log, 1)
            for e in range(1, 10):
                act.wait_ge(lv_d, 2 * e)
                act.activation(A["d"][:], A["d"][:], ACT.Exp).then_inc(lv_e, 1)
            for n in range(4):
                head_norm(n)

            act.wait_ge(o_stat, 4)
            act.dma_start(R["gamma"][:], dram["ret_tab"].rearrange("p (h t) -> p h t", t=T)).then_inc(gamma_in, 16)
            pairs("ret_in", nothing, 0, 6)
            pairs("ret_in", take(lambda m: R["gate"][:, bass.ds(m - 12, 1), :], ACT.Silu), 6, 2)
            for n in range(4, 8):
                head_norm(n)
            last_product("out0", 1)

            def ffn(layer, groups):
                for g, w in enumerate(groups):
                    name = f"ffn{layer}_up{g}"

                    def gate(i, s, m, base=HIDDEN_BEFORE[name]):
                        if s == 0:
                            act.wait_ge(unit_done, 2 * i + 1)
                            act.activation(F["act"][:, 0, :], psum[0], ACT.Silu).then_inc(bank_free[0], 1)
                        else:
                            h = i - PAIR0[name]
                            act.wait_ge(hid_done, base + h + 1)
                            act.activation(g_hi[:, bass.ds(h, 1), :], row(F["hid"][:, 0, :]), ACT.Copy)\
                               .then_inc(hid_hi, 1)
                    pairs(name, gate)
                    if g < len(groups) - 1:
                        pairs(f"ffn{layer}_down{g}", nothing)
                    else:
                        last_product(f"ffn{layer}_down{g}", 2 + 2 * layer)

            norm(1)
            act.dma_start(S1["w1"][:], dram["cmp_w1"].rearrange("p (b k n) -> p b k n", b=2, n=P)).then_inc(nsa_in, 16)
            act.dma_start(S1["w2"][:], dram["cmp_w2"].rearrange("p (b n) -> p b n", b=2)).then_inc(nsa_in, 16)
            act.dma_start(S1["pos"][:], dram["cmp_pos"].rearrange("p (b n) -> p b n", b=2)).then_inc(nsa_in, 16)
            act.dma_start(S1["glw"][:], dram["gate_w"].rearrange("p (k n) -> p k n", k=KT)).then_inc(nsa_in, 16)
            act.dma_start(S1["tab"][:], dram["nsa_tab"]).then_inc(nsa_in, 16)
            ffn(0, FFN_GROUPS)
            norm(2)

            pairs("nsa_in", nothing, count=4)
            pairs("nsa_in", nothing, first=4)
            act.wait_ge(gl_done, 1)
            act.activation(S["gates"][:], psum[2][:, 0:TT * 48].rearrange("p (q n) -> p q n", q=TT), ACT.Sigmoid)\
               .then_inc(gl_ready, 1)
            for b in range(2):
                act.wait_ge(cmp_sum, b + 1)
                act.activation(S["hid"][:, b, 0:NC], psum[4 + b][:, 0:NC], ACT.Silu).then_inc(cmp_act, 1)
            for qi in range(TT + 1):
                if qi < TT:
                    act.wait_ge(c_sub, qi + 1)
                    act.activation(probs[qi % 2][:], probs[qi % 2][:], ACT.Exp).then_inc(c_exp, 1)
                if qi:
                    act.wait_ge(c_turned, qi)
                    act.activation(S2["pct"][:, qi - 1], psum[7].rearrange("p (g n) -> p g n", g=4), ACT.Copy)\
                       .then_inc(c_kept, 1)
            for j in range(NSA_JOBS + 2):
                if j > 1:
                    i = j - 2
                    W = P * ((i // 2) % TT + 1)
                    for b in range(2):
                        act.wait_ge(n_t, 2 * i + b + 1)
                        if i > 1:
                            act.wait_ge(n_o, i - 1)
                        act.activation(S2["pt"][:, i % 2, b, 0:W], psum[6 + b][:, 0:W], ACT.Copy).then_inc(n_tk, 1)
                if j < NSA_JOBS:
                    qi, W = (j // 2) % TT, P * ((j // 2) % TT + 1)
                    act.wait_ge(n_max, j + 1)
                    if j > 1:
                        act.wait_ge(n_p, 2 * j - 2)
                    for b in range(2):
                        s2 = S2["s"][:, j % 3, b, 0:W]
                        act.activation(s2, s2, ACT.Exp, bias=S["nm"][:, j % 2, b:b + 1],
                                       accum_out=S["sum"][:, j % 2, b:b + 1]).then_inc(n_exp, 1)
                if j > 1:
                    i = j - 2
                    if i % 8 == 1 and i > 8:
                        m = i // 8 - 1
                        act.wait_ge(n_o, 8 * (m + 1))
                        act.activation(g_hi[:, m, :], psum[m % 2], ACT.Copy).then_inc(n_hi, 1)
            act.wait_ge(n_o, NSA_JOBS)
            act.activation(g_hi[:, 7, :], psum[1], ACT.Copy).then_inc(n_hi, 1)
            last_product("out1", 3)
            norm(3)
            ffn(1, FFN_GROUPS)

            act.dma_start(B3["ctx"][:], dram["ctx"].rearrange("(k p) t -> p k t", p=P)).then_inc(ctx_in, 16)
            act.dma_start(B3["rope"][:], dram["rope_tab"].rearrange("p (c t) -> p c t", c=2)).then_inc(att_in, 16)

            def settle(k, bias, scale):
                act.activation(x[:, k, :], N["y"][:, k, :], ACT.Identity, scale=scale, bias=bias).then_inc(x_new, 1)

            def norm_mod(r, bias):
                root(r)
                if r == 4:
                    act.wait_ge(aux_done, 1)
                if r < 8:
                    for k in range(KT):
                        act.wait_ge(y_done, KT * r + k + 1)
                        scale, shift = modulation(r, k)
                        act.activation(N["sq"][:, k, :], N["y"][:, k, :], ACT.Identity, scale=scale, bias=shift)\
                           .then_inc(h_mod, 1)
                        act.wait_ge(h_mod, KT * (r - 4) + k + 1)
                        act.activation(h_hi[:, k, :], N["sq"][:, k, :], ACT.Copy).then_inc(y_hi, 1)
                for k in range(KT):
                    act.wait_ge(y_done, KT * r + k + 1)
                    settle(k, bias(k), ALPHA if r < 8 else 1.0)

            norm_mod(4, lambda k: 0.0)
            for k in range(KT):
                act.wait_ge(ctx_h, k + 1)
                act.activation(g_hi[:, k, 0:CTX], B3["ctx"][:, k, :], ACT.Copy).then_inc(c_hi, 1)

            def rope_steps():
                act.wait_ge(vt_copied, 7)
                for u in range(5):
                    raw = rope_raw(*ROPE_TILES[8 + u])
                    w = raw.shape[1]
                    if u > 1:
                        act.wait_ge(rope_st, u - 1)
                    act.activation((B3["sq"] if u % 2 == 0 else B3["rstd"])[:, 0:w], raw, ACT.Square)\
                       .then_inc(rope_sq, 1)
                for u in range(5):
                    act.wait_ge(rope_st, u + 1)
                    act.activation(rope_scale(u), rope_sums(u), ACT.Ln, bias=eps, scale=1.0 / 64).then_inc(rope_ln, 1)
                act.wait_ge(rope_ln, 5)
                for u in range(5):
                    act.activation(rope_scale(u), rope_scale(u), ACT.Exp, scale=-0.5).then_inc(rope_root, 1)
                act.wait_ge(rope_done, 9)
                for g in range(2):
                    for half in range(2):
                        act.activation(B2["bk"][64 * half:64 * half + 64, g, :], B3["bkt"][64 * g:64 * g + 64, :],
                                       ACT.Copy).then_inc(bk_copied, 1)

            pairs("attn_in", nothing)
            act.wait_ge(lam_sum, 1)
            act.activation(B2["lam"][:, 0:2], psum[2][:, 0:2], ACT.Exp).then_inc(lam_exp, 1)
            rope_steps()

            def exponentials(j, b):
                act.wait_ge(a_max, 2 * j + b + 1)
                src = banks[:, 2 + 2 * b:4 + 2 * b, :].rearrange("p a t -> p (a t)")[:, 0:NK]
                act.activation(B4["e"][:, j % 3, b, :], src, ACT.Exp, bias=B2["nm"][:, j % 2, b:b + 1],
                               accum_out=B2["sum"][:, j % 2, b:b + 1]).then_inc(a_exp, 1)

            def copy_lot(t):
                act.wait_ge(a_t, t + 1)
                if t > 1:
                    act.wait_ge(a_o, t - 1)
                act.activation(B4["pt"][:, t % 2, :], turned, ACT.Copy).then_inc(a_tk, 1)
                if O_READY_AT.get(t) is not None:
                    u, last = O_READY_AT[t]
                    act.wait_ge(a_o, last + 1)
                    dst = B2["ao"][:, u, :] if u < 4 else g_hi[:, u, :]
                    act.activation(dst, psum[u % 2], ACT.Copy).then_inc(a_hi, 1)

            for j in range(ATT_JOBS + 2):
                lots = TURNS[j - 2] if j > 1 else []
                if j < ATT_JOBS:
                    if j > 1:
                        act.wait_ge(a_p, TURNS[j - 2][-1] + 1)
                    if j > 2:
                        act.wait_ge(a_t, TURNS[j - 3][-1] + 1)
                    exponentials(j, 0)
                    if len(lots) > 1:
                        copy_lot(lots[0])
                        lots = lots[1:]
                    exponentials(j, 1)
                for t in lots:
                    copy_lot(t)
            act.wait_ge(a_o, N_TURNS)
            act.activation(g_hi[:, 7, :], psum[1], ACT.Copy).then_inc(a_hi, 1)
            for h in range(4):
                act.activation(B4["osq"][:, h, :], B2["ao"][:, h, :], ACT.Square).then_inc(f_sq, 1)
            for h in range(4):
                act.wait_ge(f_stat, h + 1)
                act.activation(B4["rstd"][:, h, :], psum[2 + h], ACT.Ln, bias=eps, scale=1.0 / P).then_inc(f_ln, 1)
            act.wait_ge(f_ln, 4)
            for h in range(4):
                act.activation(B4["rstd"][:, h, :], B4["rstd"][:, h, :], ACT.Exp, scale=-0.5).then_inc(f_root, 1)
            for h in range(4):
                act.wait_ge(f_o, h + 1)
                act.activation(g_hi[:, h, :], B4["o"][:, h % 2, :], ACT.Copy).then_inc(f_hi, 1)
            last_product("out2", 5)

            def mlp(layer):
                for g in range(4):
                    name = f"mlp{layer}_up{g}"

                    def hidden(i, s, m, base=HIDDEN_BEFORE[name]):
                        act.wait_ge(unit_done, 2 * i + s + 1)
                        act.activation(F["act"][:, s, :], psum[s], ACT.Relu).then_inc(bank_free[s], 1)
                        act.wait_ge(hid_done, base + m + 1)
                        act.activation(g_hi[:, bass.ds(m, 1), :], row(F["hid"][:, s, :]), ACT.Copy).then_inc(hid_hi, 1)
                    pairs(name, hidden)
                    if g < 3:
                        pairs(f"mlp{layer}_down{g}", nothing)
                    else:
                        last_product(f"mlp{layer}_down{g}", 6 + 2 * layer)

            def ln_bias(j):
                return lambda k: aux[:, 8 * j + k:8 * j + k + 1] if j < 3 else v("ln_b", 24 + k)

            norm_mod(5, ln_bias(0))
            mlp(0)
            norm_mod(6, ln_bias(1))

            def take_c(i, s, m):
                if s == 0:
                    act.wait_ge(unit_done, 2 * i + 1)
                    act.activation(C["c"][:], psum[0], ACT.Copy).then_inc(bank_free[0], 1)
                else:
                    act.wait_ge(bank_free[1], i + 1)

            def gated(i, s, m):
                k = m - 16
                act.wait_ge(hid_done, HIDDEN_BEFORE["conv_in"] + k + 1)
                act.activation(g_hi[:, bass.ds(k, 1), :], row(C["hid"][:, s, :]), ACT.Copy).then_inc(hid_hi, 1)

            pairs("conv_in", take_c, 0, 8)
            pairs("conv_in", gated, 8, 4)
            last_product("out3", 7)
            norm_mod(7, ln_bias(2))
            mlp(1)
            norm_mod(8, ln_bias(3))

        @block.vector
        def _(dve):
            steps = [0]

            def landed(ins):
                ins.then_inc(dve_step, 1)
                steps[0] += 1
                dve.wait_ge(dve_step, steps[0])

            def split_lo(i, s):
                dve.wait_ge(w_hi_done, 2 * i + s + 1)
                dve.tensor_tensor(w_lo[s][:], w_raw[s][:], w_hi[s][:].bitcast(F32), ALU.subtract)\
                   .then_inc(w_lo_done, 1)

            def split_next(i, s):
                if s == 0:
                    split_lo(i, 1)
                elif not isinstance(i, int) or i < LAST_PAIR:
                    split_lo(i + 1, 0)

            def take_ada(name, i, first):
                if with_ada(name, first):
                    a = i - ada_skipped(name)
                    who = 2 if PAIR0[name] < ADA_BOTH else 1
                    dve.wait_ge(ada_done, a + 1)
                    dve.tensor_scalar(mod[:, bass.ds(a, 1), 0:who], row(psum[3][:, 0:who]),
                                      vec[:, bass.ds(VEC["ada_b"] + a, 1)], None, ALU.add).then_inc(ada_taken, 1)

            def pairs(name, body, first=0, count=None):
                p0 = PAIR0[name] + first
                p1 = PAIR0[name] + PAIRS[name] if count is None else p0 + count
                if p0 == 0:
                    for s in range(2):
                        split_next(0, s)
                        body(0, s, s)
                    take_ada(name, 0, first)
                    p0 = 1
                tail = p1 - 1 == LAST_PAIR
                with dve.Fori(p0, p1 - tail) as i:
                    for s in range(2):
                        split_next(i, s)
                        body(i, s, 2 * (i - PAIR0[name]) + s)
                    take_ada(name, i, first and name == "nsa_in")
                if tail:
                    for s in range(2):
                        split_next(LAST_PAIR, s)
                        body(LAST_PAIR, s, 2 * (LAST_PAIR - PAIR0[name]) + s)

            def nothing(i, s, m):
                pass

            def close_sums(r):
                last = KT - 1
                if r == 0:
                    for k in range(1, last):
                        dve.wait_ge(sq_done, k + 1)
                        landed(dve.tensor_tensor(N["s2"][:], N["sq"][:, 0, :] if k == 1 else N["s2"][:],
                                                 N["sq"][:, k, :], ALU.add))
                if r > 4:
                    dve.wait_ge(acc_done, 2 * r - 5)
                    dve.tensor_tensor(N["s1"][:], N["s1"][:], N["xc"][:, last, :], ALU.add).then_inc(s1_done, 1)
                if r:
                    dve.wait_ge(acc_done, r if r < 5 else 2 * r - 4)
                dve.wait_ge(sq_done, KT * r + KT)
                dve.tensor_tensor(N["s2"][:], N["s2"][:], N["sq"][:, last, :], ALU.add).then_inc(s2_done, 1)

            def scales(r):
                dve.wait_ge(root_done, r + 1)
                landed(dve.reciprocal(N["r"][:], N["r"][:]))
                spread = N["r"][:].rearrange("p (t o) -> p t o", o=1).broadcast_to([P, TT, P])
                eye = ident.rearrange("p (o n) -> p o n", o=1).broadcast_to([P, TT, P])
                dve.tensor_tensor(N["diag"][:], eye, spread, ALU.mult).then_inc(diag_done, 1)

            def norm(r, gain):
                close_sums(r)
                scales(r)
                dve.wait_ge(scale_done, r + 1)
                for k in range(KT):
                    dve.scalar_tensor_tensor(N["y"][:, k, :], x[:, k, :], v(gain, k), psum[2],
                                             ALU.mult, ALU.mult).then_inc(y_done, 1)

            def add_residual(i, s, m):
                dve.wait_ge(unit_done, 2 * i + s + 1)
                dve.tensor_tensor(x[:, bass.ds(m, 1), :], x[:, bass.ds(m, 1), :], row(psum[s]), ALU.add)\
                   .then_inc(bank_free[s], 1)

            def residual(name):
                pairs(name, add_residual)
                dve.wait_ge(bank_free[1], PAIR0[name] + PAIRS[name])

            def head_norm(n):
                bank = psum[6 + n % 2]
                B = A if n < 4 else R
                dve.wait_ge(o_root, n + 1)
                landed(dve.reciprocal(B["rstd"][:], B["rstd"][:]))
                o = B["o"][:, n % 2, :]
                landed(dve.scalar_tensor_tensor(o, bank, v("hgrn_g" if n < 4 else "ret_g"), B["rstd"][:],
                                                ALU.mult, ALU.mult))
                dve.tensor_tensor(o, o, B["gate"][:, n % 4, :], ALU.mult).then_inc(o_done, 1)
                dve.wait_ge(o_hi, n + 1)
                dve.tensor_tensor(g_lo[:, n, :], o, g_hi[:, n, :].bitcast(F32), ALU.subtract).then_inc(g_ready, 1)

            split_lo(0, 0)
            norm(0, "mix0")

            lb0 = vec[:, VEC["lb"]:VEC["lb"] + 4]
            lb1 = vec[:, VEC["lb"] + 4:VEC["lb"] + 8]
            mx, den, low, rest = (A["lb"][:, :, j] for j in range(4))
            landed(dve.tensor_tensor(mx, lb0, lb1, ALU.max))
            dve.tensor_tensor(A["ex"][:, :, 0], lb0, mx, ALU.subtract).then_inc(lb_m, 1)
            dve.tensor_tensor(A["ex"][:, :, 1], lb1, mx, ALU.subtract).then_inc(lb_m, 1)
            dve.wait_ge(lb_e, 1)
            landed(dve.tensor_tensor(den, A["ex"][:, :, 0], A["ex"][:, :, 1], ALU.add))
            landed(dve.reciprocal(den, den))
            landed(dve.tensor_tensor(low, A["ex"][:, :, 0], den, ALU.mult))
            landed(dve.tensor_scalar(rest, low, -1.0, 1.0, ALU.mult, ALU.add))

            def forget(i, s, m):
                h = i * 2 + s - 2 * PAIR0["hgrn_in"] - 4
                dve.wait_ge(bank_free[s], i + 1)
                dve.tensor_scalar(A["cum"][:, bass.ds(h, 1), :], A["k"][:, bass.ds(h, 1), :],
                                  A["lb"][:, bass.ds(h, 1), 3], A["lb"][:, bass.ds(h, 1), 2], ALU.mult, ALU.add)\
                   .then_inc(hg_f, 1)
                dve.wait_ge(hg_f, h + 1)
                dve.tensor_scalar(A["k"][:, bass.ds(h, 1), :], A["cum"][:, bass.ds(h, 1), :],
                                  -1.0, 1.0, ALU.mult, ALU.add).then_inc(hg_v, 1)

            def take(dst, scale=None):
                def body(i, s, m):
                    dve.wait_ge(unit_done, 2 * i + s + 1)
                    if scale is None:
                        dve.tensor_copy(dst(m), row(psum[s])).then_inc(bank_free[s], 1)
                    else:
                        dve.tensor_scalar(dst(m), row(psum[s]), scale, None, ALU.mult).then_inc(bank_free[s], 1)
                return body

            pairs("hgrn_in", nothing, 0, 2)
            pairs("hgrn_in", forget, 2, 2)
            pairs("hgrn_in", take(lambda m: A["d"][:, bass.ds(m - 8, 1), :]), 4, 2)
            pairs("hgrn_in", nothing, 6, 2)

            def copy_turned(B, n0):
                for h in range(4):
                    dve.wait_ge(tr_done, n0 + h + 1)
                    dve.tensor_copy(B["v"][:, h, :], psum[2 + h]).then_inc(tr_copied, 1)

            copy_turned(A, 0)
            reset = A["x0"][:].rearrange("p h t -> p (h t)")
            landed(dve.memset(reset, 1.0))
            landed(dve.memset(reset.rearrange("p (c t) -> p c t", t=CHUNK)[:, :, 0:1], 0.0))
            dve.wait_ge(hg_log, 1)
            cum = A["cum"][:].rearrange("p h t -> p (h t)")
            landed(dve.tensor_tensor_scan(cum, reset, cum, 0.0, ALU.mult, ALU.add))
            total = cum.rearrange("p (h c t) -> p h c t", h=4, t=CHUNK)[:, :, :, CHUNK - 1]
            adj = A["adj"]
            fwd128, bwd128, fwd256, bwd256 = (adj[:, :, j, :] for j in range(4))
            landed(dve.memset(adj[:], 0.0))
            for c in (3, 7):
                landed(dve.tensor_copy(fwd128[:, :, c], total[:, :, c - 1]))
            for c in (0, 4):
                landed(dve.tensor_tensor(bwd128[:, :, c], total[:, :, c], total[:, :, c + 1], ALU.add))
            for c in (1, 5):
                landed(dve.tensor_copy(bwd128[:, :, c], total[:, :, c]))
            for c in (5, 6, 7):
                landed(dve.tensor_tensor(fwd256[:, :, c], fwd256[:, :, c - 1], total[:, :, c - 1], ALU.add))
            landed(dve.tensor_copy(bwd256[:, :, 3], total[:, :, 3]))
            for c in (2, 1, 0):
                landed(dve.tensor_tensor(bwd256[:, :, c], bwd256[:, :, c + 1], total[:, :, c], ALU.add))

            def exponents(e):
                B = 1 << (e - 1)
                c0, c1 = halves(A["cum"], B)
                d0, d1 = halves(A["d"], B)

                if e > 1:
                    dve.wait_ge(lv_x1, e - 1)
                if B < 64:
                    ref = c0[:, :, B - 1:B].broadcast_to([P, 4 * T // (2 * B), B])
                    dve.tensor_tensor(d0, ref, c0, ALU.subtract).then_inc(lv_d, 1)
                    dve.tensor_tensor(d1, c1, ref, ALU.subtract).then_inc(lv_d, 1)
                elif B == 64:
                    ref = c0[:, :, B - 1:B].broadcast_to([P, 4 * T // (2 * B), B])
                    dve.tensor_tensor(d0, ref, c0, ALU.subtract).then_inc(lv_d, 1)
                    dve.tensor_copy(d1, c1).then_inc(lv_d, 1)
                else:
                    fwd, bwd = (fwd128, bwd128) if B == 128 else (fwd256, bwd256)
                    n = B // CHUNK
                    def cut(t):
                        return t[:].rearrange("p h (m s c t) -> p h m s c t", s=2, c=n, t=CHUNK)
                    cc, dd = cut(A["cum"]), cut(A["d"])
                    last = None
                    for h in range(4):
                        for m in range(4 // n if n == 2 else 1):
                            c = 2 * n * m
                            b = bwd[:, h, c:c + n].rearrange("p (c o) -> p c o", o=1).broadcast_to([P, n, CHUNK])
                            f = fwd[:, h, c + n:c + 2 * n].rearrange("p (c o) -> p c o", o=1)\
                                .broadcast_to([P, n, CHUNK])
                            dve.tensor_tensor(dd[:, h, m, 0], b, cc[:, h, m, 0], ALU.subtract)
                            last = dve.tensor_tensor(dd[:, h, m, 1], cc[:, h, m, 1], f, ALU.add)
                    last.then_inc(lv_d, 2)

            dve.wait_ge(tr_done, 4)
            dve.wait_ge(mask_in, 16)
            for e in range(0, 11):
                if 1 <= e < 10:
                    exponents(e)
                if e:
                    for h in range(4):
                        j = 4 * (e - 1) + h
                        dve.wait_ge(lv_gram, j + 1)
                        if e > 1:
                            dve.wait_ge(lv_kept, j - 3)
                        grams, kept = psum[2 + h], A["attn"][:, h]
                        blocks = grams.rearrange("p (b n) -> p b n", n=P)
                        if e == 1:
                            mask = A["mask"][:, 0:1, :].broadcast_to([P, 4, P])
                            ins = dve.tensor_tensor(kept[:, 0:4, :], blocks, mask, ALU.mult)
                        elif e < 9:
                            mask = A["mask"][:, e - 1:e, :].bitcast(U32).broadcast_to([P, 4, P])
                            ins = dve.copy_predicated(kept[:, 0:4, :], mask, blocks)
                        elif e == 9:
                            ins = dve.tensor_copy(kept[:, 4:6, :], blocks[:, 0:2, :])
                        else:
                            ins = dve.tensor_copy(kept[:, 6:10, :], blocks)
                        ins.then_inc(lv_kept, 1)
                if 1 <= e < 10:
                    X = A["x0"] if e % 2 else A["x1"]
                    dve.wait_ge(lv_e, e)
                    B = 1 << (e - 1)
                    (e0, e1), (x0, x1) = halves(A["d"], B), halves(X, B)
                    k0, _ = halves(A["k"], B)
                    dve.tensor_tensor(x0, e0, k0, ALU.mult).then_inc(lv_x0, 1)
                    dve.wait_ge(lv_x0, e)
            for n in range(4):
                head_norm(n)

            dve.wait_ge(o_done, 4)
            pairs("ret_in", take(lambda m: R["q"][:, bass.ds(m, 1), :]), 0, 2)
            pairs("ret_in", take(lambda m: R["k"][:, bass.ds(m - 4, 1), :], P ** -0.5), 2, 2)
            pairs("ret_in", take(lambda m: R["vt"][:, bass.ds(m - 8, 1), :]), 4, 2)
            pairs("ret_in", nothing, 6, 2)
            copy_turned(R, 4)
            dve.wait_ge(gamma_in, 16)
            for n in range(4):
                at = 0
                for jt in range(TT):
                    w = T - P * jt
                    dve.wait_ge(ret_s, 4 * n + jt + 1)
                    if n > 1:
                        dve.wait_ge(o_sum, 4 + n - 1)
                    dve.tensor_tensor(R["attn"][:, n % 2, at:at + w], psum[2 + jt % 2][:, 0:w],
                                      R["gamma"][:, n, 0:w], ALU.mult).then_inc(ret_a, 1)
                    at += w
                if n:
                    head_norm(4 + n - 1)
            head_norm(7)
            residual("out0")

            def ffn(layer, groups):
                for g, w in enumerate(groups):
                    name = f"ffn{layer}_up{g}"

                    def hidden(i, s, m, base=HIDDEN_BEFORE[name]):
                        h = i - PAIR0[name]
                        if s == 1:
                            dve.wait_ge(bank_free[0], i + 1)
                            dve.wait_ge(unit_done, 2 * i + 2)
                            dve.tensor_tensor(F["hid"][:, 0, :], F["act"][:, 0, :], psum[1], ALU.mult)\
                               .then_inc(hid_done, 1)
                            dve.wait_ge(hid_hi, base + h + 1)
                            dve.tensor_tensor(g_lo[:, bass.ds(h, 1), :], row(F["hid"][:, 0, :]),
                                              g_hi[:, bass.ds(h, 1), :].bitcast(F32), ALU.subtract)\
                               .then_inc(bank_free[1], 1)
                    pairs(name, hidden)
                    residual(f"ffn{layer}_down{g}")

            norm(1, "ffn0")
            ffn(0, FFN_GROUPS)
            norm(2, "mix1")

            def nsa_keys(dst, bank, inc):
                n = 0
                for g in range(2):
                    for half in range(2):
                        ins = dve.tensor_copy(dst[64 * half:64 * half + 64, g, :], bank[64 * g:64 * g + 64, :])
                        n += 1
                ins.then_inc(*inc)

            pairs("nsa_in", take(lambda m: S["q"][:, bass.ds(m, 1), :], NSA_D ** -0.5), 0, 4)
            p0 = PAIR0["nsa_in"]
            slots = {0: 0, 1: 1, 3: 2, 5: 3}
            for u in range(6):
                i, s = p0 + 4 + u // 2, u % 2
                split_next(i, s)
                dve.wait_ge(unit_done, 2 * i + s + 1)
                if u in slots:
                    dve.tensor_copy(S["raw"][:, slots[u], :], psum[s]).then_inc(bank_free[s], 1)
                else:
                    nsa_keys(S["ks"] if u == 2 else S["kw"], psum[s], (bank_free[s], 1))
            dve.wait_ge(nsa_in, 80)
            dve.wait_ge(bank_free[1], p0 + 7)
            for b in range(2):
                for a in range(2):
                    src = S["raw"][:, b, 16 * a:16 * a + 16 * NC].rearrange("p (i c) -> p c i", c=16)
                    pos = S1["pos"][:, b, 16 * a:16 * a + 16].rearrange("p (c o) -> p c o", o=1)\
                        .broadcast_to([P, 16, NC])
                    dve.tensor_tensor(S["flat"][:, b, 16 * a:16 * a + 16, :], src, pos, ALU.add).then_inc(flat_done, 1)
            landed(dve.memset(S["kc"][:], 0.0))
            landed(dve.memset(S["vrep"][:], 0.0))
            landed(dve.memset(S["vz"][:], 0.0))
            for b in range(2):
                dve.wait_ge(vt_done, b + 1)
                dve.tensor_copy(S["vs" if b == 0 else "vw"][:], psum[6 + b].rearrange("p (q n) -> p q n", q=TT))\
                   .then_inc(vt_copied, 1)
            dve.wait_ge(cmp_out, 1)
            for g in range(2):
                for half in range(2):
                    landed(dve.tensor_copy(S["kc"][64 * half:64 * half + 64, g, 0:NC],
                                           psum[3][64 * g:64 * g + 64, 0:NC]))
            dve.wait_ge(cmp_out, 2)
            out_v = psum[4][:, 0:NC].rearrange("p (o n) -> p o n", o=1).broadcast_to([P, 4, NC])
            dve.tensor_copy(S["vrep"][:, :, 0:NC], out_v).then_inc(cmp_kept, 1)
            dve.wait_ge(cmp_out, 3)
            for j in range(4):
                ins = dve.tensor_copy(S["vz"][32 * j:32 * j + 32, j, :], psum[5][32 * j:32 * j + 32, 0:P])
            ins.then_inc(cmp_kept, 1)
            dve.wait_ge(gl_ready, 1)
            def shifted_scores(qi):
                pc = probs[qi % 2]
                dve.wait_ge(c_s, qi + 1)
                if qi > 1:
                    dve.wait_ge(c_turned, qi - 1)
                for par in range(2):
                    landed(dve.tensor_tensor(pc[:, par], psum[2 + 2 * (qi % 2) + par][:, 0:256].rearrange(
                        "p (m c) -> p m c", m=8), cbias[:, qi, par], ALU.add))
                landed(dve.tensor_reduce(S["cm"][:], pc[:], AX.X, ALU.max))
                cm = S["cm"][:].rearrange("p r (m o) -> p r m o", o=1).broadcast_to([P, 2, 8, NCP])
                dve.tensor_tensor(pc[:], pc[:], cm, ALU.subtract).then_inc(c_sub, 1)

            def gated_probs(qi):
                pc = probs[qi % 2]
                dve.wait_ge(c_exp, qi + 1)
                landed(dve.tensor_reduce(S["cr"][:], pc[:], AX.X, ALU.add))
                landed(dve.reciprocal(S["cr"][:], S["cr"][:]))
                gate = S["gates"][:, qi, :].rearrange("p (m r c) -> p r m c", r=2, c=3)[:, :, :, 0]
                landed(dve.tensor_tensor(S["cr"][:], S["cr"][:], gate, ALU.mult))
                cr = S["cr"][:].rearrange("p r (m o) -> p r m o", o=1).broadcast_to([P, 2, 8, NCP])
                landed(dve.tensor_tensor(pc[:], pc[:], cr, ALU.mult))
                valid = cvalid[:, qi, :].rearrange("p (o c) -> p o c", o=1).broadcast_to([P, 16, NCP])
                flat_pc = pc[:].rearrange("p r m c -> p (r m) c")
                dve.tensor_tensor(flat_pc, flat_pc, valid, ALU.mult).then_inc(c_p, 1)

            for qi in range(TT + 1):
                if qi < TT:
                    shifted_scores(qi)
                if qi:
                    gated_probs(qi - 1)

            def low_out(m, ready, bank):
                dve.wait_ge(ready, m + 1)
                dve.tensor_tensor(g_lo[:, m, :], bank, g_hi[:, m, :].bitcast(F32), ALU.subtract).then_inc(g_ready, 1)

            for j in range(NSA_JOBS + 1):
                if j < NSA_JOBS:
                    m, qi, half = j // 8, (j // 2) % TT, j % 2
                    h, W = 2 * m + half, P * (qi + 1)
                    dve.wait_ge(n_s, j + 1)
                    if j > 2:
                        dve.wait_ge(n_t, 2 * (j - 2))
                    far = dist[:, T - W:T].rearrange("p (o n) -> p o n", o=1).broadcast_to([P, 2, W])
                    s2 = S2["s"][:, j % 3, :, 0:W]
                    sums = banks[:, 2 + 2 * (j % 2):4 + 2 * (j % 2), 0:W]
                    landed(dve.scalar_tensor_tensor(s2, far, -SLOPES[h], sums, ALU.mult, ALU.add))
                    dve.tensor_reduce(S["nm"][:, j % 2, :], s2, AX.X, ALU.max, negate=True).then_inc(n_max, 1)
                if j:
                    i = j - 1
                    m, qi, half = i // 8, (i // 2) % TT, i % 2
                    h, W = 2 * m + half, P * (qi + 1)
                    dve.wait_ge(n_exp, 2 * i + 2)
                    r = S["r"][:, i % 2, :]
                    landed(dve.reciprocal(r, S["sum"][:, i % 2, :]))
                    landed(dve.tensor_tensor(r, r, S["gates"][:, qi, 3 * h + 1:3 * h + 3], ALU.mult))
                    for b in range(2):
                        p = S2["s"][:, i % 3, b, 0:W]
                        dve.tensor_scalar(p, p, S["r"][:, i % 2, b:b + 1], None, ALU.mult).then_inc(n_p, 1)
                    if i % 8 == 3 and i > 8:
                        low_out(i // 8 - 1, n_hi, psum[(i // 8 - 1) % 2])
            low_out(7, n_hi, psum[1])
            residual("out1")
            norm(3, "ffn1")
            ffn(1, FFN_GROUPS)

            dve.wait_ge(ada_taken, ADA)
            for j in (1, 4, 7, 10):
                part = mod[:, 8 * j:8 * j + 8, 0:2 if j == 1 else 1]
                landed(dve.tensor_scalar(part, part, 1.0, None, ALU.add))
            lnb = vec[:, VEC["ln_b"]:VEC["ln_b"] + 32]
            landed(dve.tensor_scalar(aux[:, 0:32], lnb, ALPHA, None, ALU.mult))
            for j, (sc, sh) in enumerate(((4, 3), (7, 6), (10, 9))):
                dst = aux[:, 32 + 8 * j:40 + 8 * j]
                landed(dve.tensor_tensor(dst, lnb[:, 8 * j:8 * j + 8], mod[:, 8 * sc:8 * sc + 8, 0], ALU.mult))
                landed(dve.tensor_tensor(dst, dst, mod[:, 8 * sh:8 * sh + 8, 0], ALU.add))
            dve.sem_inc(aux_done, 1)

            def norm_mod(r, gain):
                src = N["xc"] if r > 4 else x

                def centre(k):
                    landed(dve.scalar_tensor_tensor(N["xc"][:, k, :], psum[4], -1.0 / D, N["xc"][:, k, :],
                                                    ALU.mult, ALU.add))
                close_sums(r)
                if r > 4:
                    dve.wait_ge(stat_done, r + 1)
                    st = N["st"]
                    landed(dve.tensor_scalar(st[:, 0:8], psum[2][:, 0:8], 1.0 / D, None, ALU.mult))
                    landed(dve.tensor_tensor(st[:, 8:12], st[:, 4:8], st[:, 4:8], ALU.mult))
                    landed(dve.tensor_tensor(st[:, 8:12], st[:, 0:4], st[:, 8:12], ALU.subtract))
                    dve.tensor_scalar(st[:, 8:12], st[:, 8:12], 0.0, None, ALU.max).then_inc(var_done, 1)
                    dve.wait_ge(mean_done, r - 4)
                    centre(0)
                scales(r)
                if r > 4:
                    centre(1)
                dve.wait_ge(scale_done, r + 1)
                for k in range(KT):
                    if r > 4 and k > 1:
                        centre(k)
                    dve.scalar_tensor_tensor(N["y"][:, k, :], src[:, k, :], gain(k), psum[2], ALU.mult, ALU.mult)\
                       .then_inc(y_done, 1)

            norm_mod(4, lambda k: v("final", k))
            dve.wait_ge(ctx_in, 16)
            for k in range(KT):
                dve.tensor_scalar(B3["ctx"][:, k, :], B3["ctx"][:, k, :], modcol(1, k, 1), modcol(0, k, 1),
                                  ALU.mult, ALU.add).then_inc(ctx_h, 1)
            for k in range(KT):
                dve.wait_ge(c_hi, k + 1)
                dve.tensor_tensor(g_lo[:, k, 0:CTX], B3["ctx"][:, k, :], g_hi[:, k, 0:CTX].bitcast(F32), ALU.subtract)\
                   .then_inc(c_ready, 1)
            lam = vec[0:64, VEC["lam"]:VEC["lam"] + 4].rearrange("p (a b) -> p a b", b=2)
            dve.memset(B2["lam"][:, 2:4], 0.0).then_inc(lam_prod, 1)
            dve.wait_ge(lam_prod, 1)
            dve.tensor_tensor(B2["lam"][0:64, 2:4], lam[:, :, 0], lam[:, :, 1], ALU.mult).then_inc(lam_prod, 1)

            def take2(dst, scale=None):
                def body(i, s, m):
                    dve.wait_ge(unit_done, 2 * i + s + 1)
                    d = dst(m)
                    dve.tensor_copy(d[:, :, 0:CTX], row(psum[2 + s][:, 0:CTX]))
                    dve.tensor_copy(d[:, :, CTX:NK], row(psum[s])).then_inc(bank_free[s], 1)
                return body

            pairs("attn_in", take(lambda m: B2["aq"][:, bass.ds(m, 1), :], 0.125), 0, 2)
            pairs("attn_in", take2(lambda m: B2["ak"][:, bass.ds(m - 4, 1), :]), 2, 2)
            pairs("attn_in", take2(lambda m: B3["avt"][:, bass.ds(m - 8, 1), :]), 4, 2)
            pairs("attn_in", take(lambda m: B2["bq"][:, bass.ds(m - 12, 1), :]), 6, 2)
            i = PAIR0["attn_in"] + 8
            split_next(i, 0)
            take2(lambda m: row(B3["bkt"][:]))(i, 0, 16)
            split_next(i, 1)
            take2(lambda m: row(B3["bvt"][:]))(i, 1, 17)
            for n in range(5):
                dve.wait_ge(vt_done, 2 + n + 1)
                bank = banks[:, 4 + 2 * (n % 2):6 + 2 * (n % 2), :].rearrange("p b t -> p (b t)")[:, 0:NK]
                bank = bank.rearrange("p (k n) -> p k n", n=P)
                dst = B2["av"][:, :, n * P:(n + 1) * P] if n < 4 else B2["bv"][:]
                dve.tensor_copy(dst, bank).then_inc(vt_copied, 1)
            dve.wait_ge(lam_exp, 1)
            lc = B2["lam"]
            landed(dve.tensor_tensor(lc[:, 2:3], lc[:, 1:2], lc[:, 0:1], ALU.subtract))
            landed(dve.tensor_scalar(lc[:, 3:4], lc[:, 2:3], -LAM_INIT, None, ALU.add))
            landed(dve.tensor_scalar(lc[:, 2:3], v("subln"), 1.0 - LAM_INIT, None, ALU.mult))
            landed(dve.tensor_scalar(aux[:, 62:63], v("qn"), 0.125, None, ALU.mult))
            dve.wait_ge(att_in, 16)

            def norm_rows(u):
                raw = rope_raw(*ROPE_TILES[8 + u])
                dve.wait_ge(rope_root, u + 1)
                dve.scalar_tensor_tensor(raw, raw, v("kn") if u == 0 else aux[:, 62:63], rope_scale(u),
                                         ALU.mult, ALU.mult).then_inc(rope_n, 1)

            for n, (kind, m) in enumerate(ROPE_TILES):
                if n >= 7 and n < 12:
                    norm_rows(n - 7)
                raw = rope_raw(kind, m)
                w = raw.shape[1]
                dve.wait_ge(rope_rot, n + 1)
                sine = rope_cos[:, 2 + n % 2, :]
                landed(dve.tensor_tensor(sine, psum[2 + n % 2], sines, ALU.mult))
                dve.wait_ge(rope_c, n + 1)
                dve.tensor_tensor(raw[:, w - T:w], sine, rope_cos[:, n % 2, :], ALU.add).then_inc(rope_done, 1)

            def low_out2(u):
                dve.wait_ge(a_hi, u + 1)
                dve.tensor_tensor(g_lo[:, u, :], psum[u % 2], g_hi[:, u, :].bitcast(F32), ALU.subtract)\
                   .then_inc(g_ready, 1)

            for j in range(ATT_JOBS + 1):
                if j < ATT_JOBS:
                    if j > 1:
                        dve.wait_ge(a_exp, 2 * j - 2)
                    for b in range(2):
                        dve.wait_ge(a_s, 2 * j + b + 1)
                        sums = banks[:, 2 + 2 * b:4 + 2 * b, :].rearrange("p a t -> p (a t)")[:, 0:NK]
                        dve.tensor_reduce(B2["nm"][:, j % 2, b:b + 1], sums, AX.X, ALU.max, negate=True)\
                           .then_inc(a_max, 1)
                if j:
                    i = j - 1
                    dve.wait_ge(a_exp, 2 * i + 2)
                    e, r = B4["e"][:, i % 3], B2["r"][:, i % 2, :]
                    landed(dve.reciprocal(r, B2["sum"][:, i % 2, :]))
                    if i < 16:
                        landed(dve.tensor_scalar(r[:, 1:2], r[:, 1:2], lc[:, 3:4], None, ALU.mult))
                        landed(dve.tensor_scalar(e[:, 1, :], e[:, 1, :], r[:, 1:2], None, ALU.mult))
                        if i > 1:
                            dve.wait_ge(a_t, i - 1)
                        dve.scalar_tensor_tensor(B4["comb"][:, i % 2, :], e[:, 0, :], r[:, 0:1], e[:, 1, :],
                                                 ALU.mult, ALU.add).then_inc(a_p, 1)
                    else:
                        for b in range(2):
                            dve.tensor_scalar(e[:, b, :], e[:, b, :], r[:, b:b + 1], None, ALU.mult).then_inc(a_p, 1)
                        if i in (22, 26, 30):
                            low_out2(4 + (i - 22) // 4)
            low_out2(7)
            for h in range(5):
                if h < 4:
                    if h > 1:
                        dve.wait_ge(g_ready, G_BEFORE["attn_in"] + 4 + h - 1)
                    dve.wait_ge(f_root, h + 1)
                    dve.scalar_tensor_tensor(B4["o"][:, h % 2, :], B2["ao"][:, h, :], lc[:, 2:3], B4["rstd"][:, h, :],
                                             ALU.mult, ALU.mult).then_inc(f_o, 1)
                if h:
                    dve.wait_ge(f_hi, h)
                    dve.tensor_tensor(g_lo[:, h - 1, :], B4["o"][:, (h - 1) % 2, :], g_hi[:, h - 1, :].bitcast(F32),
                                      ALU.subtract).then_inc(g_ready, 1)

            def gated_residual(name, part, r=None):
                def body(i, s, m):
                    dve.wait_ge(unit_done, 2 * i + s + 1)
                    xm = x[:, bass.ds(m, 1), :]
                    dve.scalar_tensor_tensor(xm, row(psum[s]), mod[:, bass.ds(8 * part + m, 1), 0], xm,
                                             ALU.mult, ALU.add).then_inc(bank_free[s], 1)
                    if r:
                        dve.wait_ge(bank_free[s], i + 1)
                        dve.wait_ge(shift_done, r - 4)
                        dve.scalar_tensor_tensor(N["xc"][:, bass.ds(m, 1), :], row(psum[3]), -1.0 / P, xm,
                                                 ALU.mult, ALU.add).then_inc(xc_done, 1)
                pairs(name, body)
                dve.wait_ge(bank_free[1], PAIR0[name] + PAIRS[name])
                if r:
                    dve.wait_ge(xc_done, KT * (r - 4))

            def mlp(layer):
                for g in range(4):
                    name = f"mlp{layer}_up{g}"

                    def hidden(i, s, m, base=HIDDEN_BEFORE[name]):
                        dve.wait_ge(bank_free[s], i + 1)
                        dve.tensor_tensor(F["hid"][:, s, :], F["act"][:, s, :], F["act"][:, s, :], ALU.mult)\
                           .then_inc(hid_done, 1)
                        dve.wait_ge(hid_hi, base + m + 1)
                        dve.tensor_tensor(g_lo[:, bass.ds(m, 1), :], row(F["hid"][:, s, :]),
                                          g_hi[:, bass.ds(m, 1), :].bitcast(F32), ALU.subtract).then_inc(hid_lo, 1)
                    pairs(name, hidden)
                    gated_residual(f"mlp{layer}_down{g}", 6 * layer + 5, 6 + 2 * layer if g == 3 else None)

            def ln_gain(j):
                return lambda k: v("ln_g", 8 * j + k)

            gated_residual("out2", 2, 5)
            norm_mod(5, ln_gain(0))
            mlp(0)
            norm_mod(6, ln_gain(1))

            dve.wait_ge(h_ready, 7 * KT)
            landed(dve.memset(C["u"][:, 0:1], 0.0))
            landed(dve.memset(C["u"][:, T + 1:T + 2], 0.0))

            def convolve(i, s, m):
                if s == 1:
                    k = i - PAIR0["conv_in"]
                    dve.wait_ge(bank_free[0], i + 1)
                    dve.wait_ge(unit_done, 2 * i + 2)
                    dve.tensor_tensor(C["u"][:, 1:T + 1], C["c"][:], psum[1], ALU.mult).then_inc(bank_free[1], 1)
                    dve.wait_ge(bank_free[1], i + 1)
                    y = C["y"][:, bass.ds(k, 1), :]
                    for n in range(3):
                        u = row(C["u"][:, n:n + T])
                        gain = vec[:, bass.ds(VEC["conv_w"] + 8 * n + k, 1)]
                        if n == 0:
                            ins = dve.tensor_scalar(y, u, gain, vec[:, bass.ds(VEC["conv_b"] + k, 1)], ALU.mult, ALU.add)
                        else:
                            ins = dve.scalar_tensor_tensor(y, u, gain, y, ALU.mult, ALU.add)
                        ins.then_inc(u_done, 1)
                        dve.wait_ge(u_done, 3 * k + n + 1)

            def gated(i, s, m):
                k = m - 16
                dve.wait_ge(unit_done, 2 * i + s + 1)
                dve.tensor_tensor(row(C["hid"][:, s, :]), C["y"][:, bass.ds(k, 1), :], row(psum[s]), ALU.mult)\
                   .then_inc(hid_done, 1)
                dve.wait_ge(hid_hi, HIDDEN_BEFORE["conv_in"] + k + 1)
                dve.tensor_tensor(g_lo[:, bass.ds(k, 1), :], row(C["hid"][:, s, :]),
                                  g_hi[:, bass.ds(k, 1), :].bitcast(F32), ALU.subtract).then_inc(g_ready, 1)
                dve.wait_ge(g_ready, G_BEFORE["conv_in"] + k + 1)
                dve.sem_inc(bank_free[s], 1)

            pairs("conv_in", convolve, 0, 8)
            pairs("conv_in", gated, 8, 4)
            gated_residual("out3", 8, 7)
            norm_mod(7, ln_gain(2))
            mlp(1)
            norm_mod(8, ln_gain(3))

        @block.tensor
        def _(pe):
            def unit(i, s, moving, kts=KT, fresh=None):
                pe.wait_ge(w_lo_done, 2 * i + s + 1)
                if not isinstance(i, int) or i > 0:
                    pe.wait_ge(bank_free[s], i)
                for bank, hi, lo in moving:
                    for n, k in enumerate(fresh[2][:kts] if fresh else range(kts)):
                        if fresh:
                            pe.wait_ge(fresh[0], fresh[1] + n + 1)
                        for a, (w, m) in enumerate(((w_hi, hi), (w_hi, lo), (w_lo, hi))):
                            mm = pe.matmul(bank, w[s][:, k, :], m[:, k, :], start=(n == 0 and a == 0),
                                           stop=(n == kts - 1 and a == 2))
                mm.then_inc(unit_done, 1)

            def ada_unit(name, i, first):
                if with_ada(name, first):
                    a = i - ada_skipped(name)
                    pe.wait_ge(ada_added, a + 1)
                    if not isinstance(a, int) or a > 0:
                        pe.wait_ge(ada_taken, a)
                    if PAIR0[name] < ADA_BOTH:
                        pe.matmul(psum[3][:, 1:2], ada_sum[:, 1, :], ones[:, 0:1], start=True, stop=True)
                    pe.matmul(psum[3][:, 0:1], ada_sum[:, 0, :], ones[:, 0:1], start=True, stop=True)\
                        .then_inc(ada_done, 1)

            IN_ORDER = tuple(range(KT))

            def pairs(name, hi, lo, kts=KT, first=0, count=None, fresh=None, r=None):
                p0 = PAIR0[name] + first
                p1 = PAIR0[name] + PAIRS[name] if count is None else p0 + count
                if fresh:
                    unit(p0, 0, [(psum[0], hi, lo)], kts, fresh)
                    if r:
                        pe.wait_ge(bank_free[0], p0 + 1)
                        pe.matmul(psum[3], ones, x[:, 0, :], start=True, stop=True).then_inc(shift_done, 1)
                    unit(p0, 1, [(psum[1], hi, lo)], kts)
                    ada_unit(name, p0, first)
                    p0 += 1
                with pe.Fori(p0, p1) as i:
                    unit(i, 0, [(psum[0], hi, lo)], kts)
                    unit(i, 1, [(psum[1], hi, lo)], kts)
                    ada_unit(name, i, first)

            def norm(r):
                def token_sums(acc, first):
                    for t in range(TT):
                        mm = pe.matmul(psum[2][:, first + t:first + t + 1], acc[:, t * P:(t + 1) * P], ones[:, 0:1],
                                       start=True, stop=True)
                    return mm
                if r > 4:
                    pe.wait_ge(s1_done, r - 4)
                    token_sums(N["s1"], TT)
                    pe.matmul(psum[4], ones, N["s1"][:], start=True, stop=True).then_inc(mean_done, 1)
                pe.wait_ge(s2_done, r + 1)
                token_sums(N["s2"], 0).then_inc(stat_done, 1)
                pe.wait_ge(diag_done, r + 1)
                pe.matmul(psum[2], ones, N["diag"][:].rearrange("p t n -> p (t n)"), start=True, stop=True)\
                    .then_inc(scale_done, 1)

            def turn(B, name, n0, ready):
                pe.wait_ge(ada_taken, ready + 4)
                for h in range(4):
                    pe.wait_ge(bank_free[h % 2], ready + h // 2 + 1)
                    for t in range(TT):
                        mm = pe.transpose(psum[2 + h][:, t * P:(t + 1) * P], B[name][:, h, t * P:(t + 1) * P], ident)
                    mm.then_inc(tr_done, 1)

            def stat(n):
                B = A if n < 4 else R
                pe.wait_ge(o_sq, n + 1)
                if n > 1:
                    pe.wait_ge(o_done, n - 1)
                pe.matmul(psum[4 + n % 2], ones, B["osq"][:], start=True, stop=True).then_inc(o_stat, 1)

            pe.wait_ge(c_silu, 2)
            norm(0)
            pairs("hgrn_in", h_hi, h_lo, fresh=(h_ready, 0, IN_ORDER))
            turn(A, "d", 0, PAIR0["hgrn_in"] + 4)
            for e in range(10):
                if e:
                    pe.wait_ge(lv_x0, e)
                    pe.wait_ge(lv_x1, e)
                else:
                    pe.wait_ge(hg_v, 4)
                    pe.wait_ge(tr_copied, 4)
                for h in range(4):
                    grams = psum[2 + h]
                    if e:
                        pe.wait_ge(lv_kept, 4 * (e - 1) + h + 1)
                    X = A["x0"] if e % 2 else A["x1"]
                    left, right = (A["k"], A["q"]) if e == 0 else (X, X)

                    def cols(t, n=1):
                        return slice(t * P, (t + n) * P)
                    if e < 8:
                        for t in range(TT):
                            mm = pe.matmul(grams[:, cols(t)], left[:, h, cols(t)], right[:, h, cols(t)],
                                           start=True, stop=True)
                    elif e == 8:
                        for t in (0, 2):
                            mm = pe.matmul(grams[:, cols(t // 2)], X[:, h, cols(t)], X[:, h, cols(t + 1)],
                                           start=True, stop=True)
                    else:
                        for t in (0, 1):
                            mm = pe.matmul(grams[:, cols(2 * t, 2)], X[:, h, cols(t)], X[:, h, cols(2, 2)],
                                           start=True, stop=True)
                    mm.then_inc(lv_gram, 1)
            where = {(t, t): t for t in range(4)} | {(0, 1): 4, (2, 3): 5, (0, 2): 6, (0, 3): 7, (1, 2): 8, (1, 3): 9}
            for n in range(4):
                pe.wait_ge(lv_kept, 40)
                if n > 1:
                    pe.wait_ge(o_done, n - 1)
                for it in range(TT):
                    for jt in range(it + 1):
                        mm = pe.matmul(psum[6 + n % 2][:, it * P:(it + 1) * P], A["v"][:, n, jt * P:(jt + 1) * P],
                                       A["attn"][:, n, where[jt, it], :], start=(jt == 0), stop=(jt == it))
                mm.then_inc(o_sum, 1)
                stat(n)

            pairs("ret_in", h_hi, h_lo)
            turn(R, "vt", 4, PAIR0["ret_in"] + 4)
            pe.wait_ge(tr_copied, 8)
            for n in range(4):
                for jt in range(TT):
                    w = T - P * jt
                    if 4 * n + jt >= 2:
                        pe.wait_ge(ret_a, 4 * n + jt - 1)
                    pe.matmul(psum[2 + jt % 2][:, 0:w], R["k"][:, n, jt * P:(jt + 1) * P], R["q"][:, n, jt * P:T],
                              start=True, stop=True).then_inc(ret_s, 1)
                if n > 1:
                    pe.wait_ge(o_done, 4 + n - 1)
                at = 0
                for jt in range(TT):
                    pe.wait_ge(ret_a, 4 * n + jt + 1)
                    w = T - P * jt
                    mm = pe.matmul(psum[6 + n % 2][:, jt * P:T], R["v"][:, n, jt * P:(jt + 1) * P],
                                   R["attn"][:, n % 2, at:at + w], start=(jt == 0), stop=(jt == TT - 1))
                    at += w
                mm.then_inc(o_sum, 1)
                stat(4 + n)
            pairs("out0", g_hi, g_lo, fresh=(g_ready, 0, IN_ORDER))

            def ffn(layer, groups):
                for g, w in enumerate(groups):
                    up = f"ffn{layer}_up{g}"
                    pairs(up, h_hi, h_lo, fresh=(h_ready, KT * (1 + 2 * layer), IN_ORDER) if g == 0 else None)
                    pairs(f"ffn{layer}_down{g}", g_hi, g_lo, kts=w, fresh=(bank_free[1], PAIR0[up], IN_ORDER))

            norm(1)
            ffn(0, FFN_GROUPS)
            norm(2)

            pairs("nsa_in", h_hi, h_lo, count=4, fresh=(h_ready, 2 * KT, IN_ORDER))
            pairs("nsa_in", h_hi, h_lo, first=4)
            pe.wait_ge(nsa_in, 80)
            for qi in range(TT):
                for k in range(KT):
                    for a, part in enumerate((h_hi, h_lo)):
                        mm = pe.matmul(psum[2][:, 48 * qi:48 * qi + 48], part[:, k, qi * P:(qi + 1) * P].bitcast(F32),
                                       S1["glw"][:, k, :], start=(k == 0 and a == 0), stop=(k == KT - 1 and a == 1))
            mm.then_inc(gl_done, 1)
            p0 = PAIR0["nsa_in"]
            pe.wait_ge(bank_free[1], p0 + 7)
            for b in range(2):
                for t in range(TT):
                    mm = pe.transpose(psum[6 + b][:, t * P:(t + 1) * P], S["raw"][:, 2 + b, t * P:(t + 1) * P], ident)
                mm.then_inc(vt_done, 1)
            for b in range(2):
                pe.wait_ge(flat_done, 2 * b + 2)
                for k in range(CMP_BLOCK):
                    mm = pe.matmul(psum[4 + b][:, 0:NC], S1["w1"][:, b, k, :], S["flat"][:, b, k, :],
                                   start=(k == 0), stop=(k == CMP_BLOCK - 1))
                mm.then_inc(cmp_sum, 1)
            pe.wait_ge(ada_taken, PAIR0["nsa_in"] + 4)
            for b in range(2):
                pe.wait_ge(cmp_act, 2)
                pe.matmul(psum[3 + b][:, 0:NC], S1["w2"][:, b, :], S["hid"][:, b, 0:NC],
                          start=True, stop=True).then_inc(cmp_out, 1)
            pe.wait_ge(cmp_kept, 1)
            pe.transpose(psum[5][:, 0:P], S["vrep"][:].rearrange("p j c -> p (j c)"), ident).then_inc(cmp_out, 1)
            pe.wait_ge(vt_copied, 2)
            pe.wait_ge(cmp_kept, 2)
            pe.wait_ge(gl_ready, 1)
            def compressed_scores(qi):
                if qi > 1:
                    pe.wait_ge(c_sub, qi - 1)
                for par in range(2):
                    rows = slice(64 * par, 64 * par + 64)
                    for m in range(8):
                        bank = psum[2 + 2 * (qi % 2) + par]
                        mm = pe.matmul(bank[:, NCP * m:NCP * m + NCP], S["q"][rows, m, qi * P:(qi + 1) * P],
                                       S["kc"][rows, m // 4, :], start=True, stop=True)
                mm.then_inc(c_s, 1)

            compressed_scores(0)
            for qi in range(TT):
                if qi + 1 < TT:
                    compressed_scores(qi + 1)
                pe.wait_ge(c_p, qi + 1)
                if qi:
                    pe.wait_ge(c_kept, qi)
                pc = probs[qi % 2][:].rearrange("p r m c -> p (r m c)")
                for g in range(4):
                    mm = pe.transpose(psum[7][:, g * P:(g + 1) * P], pc[:, g * P:(g + 1) * P], ident)
                mm.then_inc(c_turned, 1)
            pe.wait_ge(c_kept, TT)
            for j in range(NSA_JOBS + 3):
                if j < NSA_JOBS:
                    m, qi, half = j // 8, (j // 2) % TT, j % 2
                    rows = slice(64 * half, 64 * half + 64)
                    if j > 1:
                        pe.wait_ge(n_max, j - 1)
                    for b, keys in enumerate((S["ks"], S["kw"])):
                        mm = pe.matmul(banks[:, 2 + 2 * (j % 2) + b, 0:P * (qi + 1)], S["q"][rows, m, qi * P:(qi + 1) * P],
                                       keys[rows, m // 4, 0:P * (qi + 1)], start=True, stop=True)
                    mm.then_inc(n_s, 1)
                if 2 <= j < NSA_JOBS + 2:
                    i = j - 2
                    qi = (i // 2) % TT
                    for b in range(2):
                        pe.wait_ge(n_p, 2 * i + b + 1)
                        if i:
                            pe.wait_ge(n_tk, 2 * (i - 1) + b + 1)
                        for t in range(qi + 1):
                            mm = pe.transpose(psum[6 + b][:, t * P:(t + 1) * P], S2["s"][:, i % 3, b, t * P:(t + 1) * P],
                                              ident)
                        mm.then_inc(n_t, 1)
                if j >= 3:
                    i = j - 3
                    m, qi, half = i // 8, (i // 2) % TT, i % 2
                    g = m // 4
                    if i % 8 == 0 and m >= 2:
                        pe.wait_ge(g_ready, G_BEFORE["nsa_in"] + m - 1)
                    pe.wait_ge(n_tk, 2 * i + 2)
                    o = psum[m % 2][64 * half:64 * half + 64, qi * P:(qi + 1) * P]
                    pe.matmul(o, S["vz"][:, m % 4, 64 * g:64 * g + 64], S2["pct"][:, qi, 2 * half + g, :],
                              start=True, stop=False)
                    for b, values in enumerate((S["vs"], S["vw"])):
                        for t in range(qi + 1):
                            mm = pe.matmul(o, values[:, t, 64 * g:64 * g + 64], S2["pt"][:, i % 2, b, t * P:(t + 1) * P],
                                           start=False, stop=(b == 1 and t == qi))
                    mm.then_inc(n_o, 1)
            pairs("out1", g_hi, g_lo, fresh=(g_ready, G_BEFORE["nsa_in"], IN_ORDER))
            norm(3)
            ffn(1, FFN_GROUPS)

            norm(4)
            pe.wait_ge(ada_taken, ADA)
            ctx_hi, ctx_lo = g_hi[:, :, 0:CTX], g_lo[:, :, 0:CTX]

            def attn_unit(i, s, with_ctx, fresh=None):
                moving = [(psum[s], h_hi, h_lo)]
                if with_ctx:
                    moving.append((psum[2 + s][:, 0:CTX], ctx_hi, ctx_lo))
                unit(i, s, moving, fresh=fresh)

            p0 = PAIR0["attn_in"]
            for s in range(2):
                attn_unit(p0, s, False, (h_ready, 4 * KT, IN_ORDER) if s == 0 else None)
            for first, last, with_ctx in ((1, 2, False), (2, 6, True), (6, 8, False), (8, 9, True)):
                if first == 2:
                    pe.wait_ge(c_ready, KT)
                with pe.Fori(p0 + first, p0 + last) as i:
                    for s in range(2):
                        attn_unit(i, s, with_ctx)
            for n in range(5):
                pe.wait_ge(bank_free[1], p0 + 9)
                if n == 0:
                    pe.wait_ge(bank_free[0], p0 + 9)
                if n > 1:
                    pe.wait_ge(vt_copied, 2 + n - 1)
                bank = banks[:, 4 + 2 * (n % 2):6 + 2 * (n % 2), :].rearrange("p b t -> p (b t)")
                src = B3["avt"][:, n, :] if n < 4 else B3["bvt"][:]
                for t in range(KEY_TILES):
                    mm = pe.transpose(bank[:, t * P:(t + 1) * P], src[:, t * P:(t + 1) * P], ident)
                mm.then_inc(vt_done, 1)
            pe.wait_ge(lam_prod, 2)
            pe.matmul(psum[2][:, 0:2], ones, B2["lam"][:, 2:4], start=True, stop=True).then_inc(lam_sum, 1)
            pe.wait_ge(vt_copied, 7)
            pe.wait_ge(lam_exp, 1)

            def square_sums(u):
                w = NK if u == 0 else T
                squares = B3["sq"] if u % 2 == 0 else B3["rstd"]
                pe.wait_ge(rope_sq, u + 1)
                for c0 in range(0, w, T):
                    mm = pe.matmul(rope_sums(u)[:, c0:min(c0 + T, w)], half_ones, squares[:, c0:min(c0 + T, w)],
                                   start=True, stop=True)
                mm.then_inc(rope_st, 1)

            for n, (kind, m) in enumerate(ROPE_TILES):
                raw = rope_raw(kind, m)
                w = raw.shape[1]
                if n < 5:
                    square_sums(n)
                if kind[0] == "b":
                    pe.wait_ge(rope_n, n - 7)
                if n > 1:
                    pe.wait_ge(rope_done, n - 1)
                pe.matmul(psum[2 + n % 2], rot, raw[:, w - T:w], start=True, stop=True).then_inc(rope_rot, 1)
            pe.wait_ge(rope_done, len(ROPE_TILES))
            pe.wait_ge(bk_copied, 4)

            def turn_lot(j, t):
                b = 0 if j < 16 else t % 2
                src = B4["comb"][:, j % 2, :] if j < 16 else B4["e"][:, j % 3, b, :]
                pe.wait_ge(a_p, t + 1)
                if t:
                    pe.wait_ge(a_tk, t)
                for k in range(KEY_TILES):
                    mm = pe.transpose(turned[:, k * P:(k + 1) * P], src[:, k * P:(k + 1) * P], ident)
                mm.then_inc(a_t, 1)

            def add_lot(t):
                u = out_tile(t)
                pe.wait_ge(a_tk, t + 1)
                if u >= 2 and t in (8, 12, 16, 24, 32, 40):
                    if u < 6:
                        pe.wait_ge(a_hi, u - 1)
                    else:
                        pe.wait_ge(g_ready, G_BEFORE["attn_in"] + u - 5)
                if t < 16:
                    qi, h = t % 4, t // 4
                    o = psum[u % 2][:, qi * P:(qi + 1) * P]
                    values = B2["av"][:, :, h * P:(h + 1) * P]
                else:
                    m, qi, half = (t - 16) // 8, (t - 16) // 2 % 4, t % 2
                    o = psum[u % 2][64 * half:64 * half + 64, qi * P:(qi + 1) * P]
                    values = B2["bv"][:, :, 64 * (m // 2):64 * (m // 2) + 64]
                for k in range(KEY_TILES):
                    mm = pe.matmul(o, values[:, k, :], B4["pt"][:, t % 2, k * P:(k + 1) * P], start=(k == 0),
                                   stop=(k == KEY_TILES - 1))
                mm.then_inc(a_o, 1)

            for j in range(ATT_JOBS + 2):
                if j < ATT_JOBS:
                    qi = j % 4
                    m = j // 4 if j < 16 else (j - 16) // 4
                    for b in range(2):
                        if j:
                            pe.wait_ge(a_exp, 2 * j + b - 1)
                        rows = slice(64 * b, 64 * b + 64)
                        q = B2["aq" if j < 16 else "bq"][rows, m, qi * P:(qi + 1) * P]
                        keys = B2["ak"][rows, m, :] if j < 16 else B2["bk"][rows, m // 2, :]
                        for a, (c0, c1) in enumerate(((0, T), (T, NK))):
                            mm = pe.matmul(banks[:, 2 + 2 * b + a, 0:c1 - c0], q, keys[:, c0:c1], start=True, stop=True)
                        mm.then_inc(a_s, 1)
                if j > 1:
                    for t in TURNS[j - 2]:
                        turn_lot(j - 2, t)
                        if t:
                            add_lot(t - 1)
            add_lot(N_TURNS - 1)
            for h in range(4):
                pe.wait_ge(f_sq, h + 1)
                pe.matmul(psum[2 + h], ones, B4["osq"][:, h, :], start=True, stop=True).then_inc(f_stat, 1)
            pairs("out2", g_hi, g_lo, fresh=(g_ready, G_BEFORE["attn_in"], (4, 5, 6, 7, 0, 1, 2, 3)), r=5)

            def mlp(layer):
                for g in range(4):
                    pairs(f"mlp{layer}_up{g}", h_hi, h_lo,
                          fresh=(h_ready, KT * (6 + 2 * layer - 1), IN_ORDER) if g == 0 else None)
                    pairs(f"mlp{layer}_down{g}", g_hi, g_lo, fresh=(hid_lo, 8 * (4 * layer + g), IN_ORDER),
                          r=6 + 2 * layer if g == 3 else None)

            norm(5)
            mlp(0)
            norm(6)
            pairs("conv_in", h_hi, h_lo, fresh=(h_ready, 6 * KT, IN_ORDER))
            pairs("out3", g_hi, g_lo, fresh=(g_ready, G_BEFORE["conv_in"], IN_ORDER), r=7)
            norm(7)
            mlp(1)
            norm(8)


def tiles(a, n_in=None):
    k, n = a.shape
    pad = (-k) % D
    if pad:
        a = np.concatenate([a, np.zeros((pad, n), a.dtype)])
    return a.reshape(-1, KT, P, n // P, P).transpose(0, 3, 2, 1, 4).reshape(-1, P, KT * P)


def block_diagonal(ws):
    made = []
    for a in ws:
        a = np.asarray(a)
        n = a.shape[0] // 64
        b = np.zeros((2, 64, n, 2, 64), a.dtype)
        for g in range(2):
            b[g, :, :, g, :] = a.reshape(n, 64, 64).transpose(1, 0, 2)
        made.append(b.reshape(P, n * P))
    return np.concatenate(made, 1)


def lay_out(w):
    w = {k: np.asarray(a) for k, a in w.items()}
    u = {}
    hgrn = tiles(w["even_w_in"][0])
    u["hgrn_in"], u["ret_in"] = hgrn[:16], hgrn[16:]
    u["out0"] = tiles(w["even_w_out"][0])
    for layer in range(2):
        gate_up, down = tiles(w["ffn_w_gate_up"][layer]), w["ffn_w_down"][layer]
        h0, half = 0, gate_up.shape[0] // 2
        for g, n in enumerate(FFN_GROUPS):
            u[f"ffn{layer}_up{g}"] = np.stack([gate_up[h0:h0 + n], gate_up[half + h0:half + h0 + n]], 1)\
                .reshape(2 * n, P, KT * P)
            u[f"ffn{layer}_down{g}"] = tiles(down[h0 * P:(h0 + n) * P])
            h0 += n
    u["nsa_in"] = tiles(w["odd_w_in"][0][:, :14 * P])
    u["out1"] = tiles(w["odd_w_out"][0])
    u["attn_in"], u["out2"] = tiles(w["attn_w_in_2"][0]), tiles(w["attn_w_out_2"][0])
    for layer in range(2):
        w1, w2 = tiles(w["mlp_w1_2"][layer]), tiles(w["mlp_w2_2"][layer])
        for g in range(4):
            u[f"mlp{layer}_up{g}"], u[f"mlp{layer}_down{g}"] = w1[8 * g:8 * g + 8], w2[8 * g:8 * g + 8]
    conv = tiles(w["conv_w_in_2"][0])
    u["conv_in"] = np.concatenate([np.stack([conv[8:16], conv[16:24]], 1).reshape(16, P, KT * P), conv[:8]])
    u["out3"] = tiles(w["conv_w_out_2"][0])

    def feature(a):
        return np.asarray(a).reshape(-1, P).T

    def twice(a):
        return np.concatenate([np.asarray(a).reshape(-1), np.asarray(a).reshape(-1)])[:, None]

    lam = np.asarray(w["diff_lambda_2"][0]).T
    vecs = {
        "mix0": feature(w["mix_norm"][0]), "mix1": feature(w["mix_norm"][1]), "ffn0": feature(w["ffn_norm"][0]),
        "ffn1": feature(w["ffn_norm"][1]), "final": feature(w["final_norm"]), "lb": feature(w["hgrn_lower_bounds"]),
        "hgrn_g": feature(w["hgrn_out_norm"][0]), "ret_g": feature(w["ret_out_norm"][0]), "c": feature(w["c_2"]),
        "cc": feature(w["c_ctx_2"]), "ada_b": feature(w["ada_b_2"]), "subln": feature(w["diff_subln_g_2"][0]),
        "qn": twice(w["q_norm_g_2"][0]), "kn": twice(w["k_norm_g_2"][0]), "conv_w": feature(w["conv_w_2"][0]),
        "conv_b": feature(w["conv_b_2"][0]), "ln_g": feature(w["ln_g_2"]), "ln_b": feature(w["ln_b_2"]),
        "lam": np.concatenate([lam, np.zeros_like(lam)]),
    }
    return {"weights": np.concatenate([u[name] for name, _ in PLAN]),
            "ada": np.concatenate([tiles(w["ada_w_2"][layer]) for layer in range(2)]),
            "vecs": np.concatenate([vecs[name] for name in VEC], 1),
            "cmp_w1": block_diagonal([w["cmp_w1_k"][0], w["cmp_w1_v"][0]]),
            "cmp_w2": block_diagonal([w["cmp_w2_k"][0], w["cmp_w2_v"][0]]),
            "cmp_pos": np.concatenate([np.concatenate([np.asarray(w[k][0]).T] * 2) for k in ("cmp_pos_k", "cmp_pos_v")], 1),
            "gate_w": np.asarray(w["odd_w_in"])[0][:, 14 * P:].reshape(KT, P, 48).transpose(1, 0, 2).reshape(P, -1),
            "ctx": np.asarray(w["ctx_2"])[0].T,
            "x": np.asarray(w["x"])[0].T}


def shape_tables():
    i = np.arange(P)
    eye = np.eye(P)
    half = (i[:, None] // 64 == i[None, :] // 64)
    swap = np.zeros((P, P))
    for m in range(P):
        swap[m + 16 if m % 32 < 16 else m - 16, m] = -1.0 if m % 32 < 16 else 1.0
    t = {"tables": np.concatenate([eye, np.ones((P, P)), half, swap, np.full((P, 1), EPS)], 1)}
    masks = [i[:, None] == i[None, :]]
    for B in LEVELS:
        masks.append((i[:, None] // (2 * B) == i[None, :] // (2 * B)) & (i[:, None] % (2 * B) < B)
                     & (i[None, :] % (2 * B) >= B))
    t["hgrn_tab"] = np.concatenate(masks, 1)
    log_gamma = np.log(1.0 - np.exp2(-5.0 - np.arange(HEADS_L)))
    gap = np.arange(T)[None, :] - i[:, None]
    t["ret_tab"] = np.concatenate([np.where(gap >= 0, np.exp(np.maximum(gap, 0) * g), 0.0) for g in log_gamma], 1)
    far = i[:, None] + (T - P) - np.arange(T)[None, :]
    parts = [np.where(far >= 0, far, BIG)]
    pos = np.arange(T).reshape(TT, P).T
    end = np.arange(NCP) * CMP_STRIDE + CMP_BLOCK - 1
    far_c = (pos[:, :, None] - end[None, None, :]).astype(np.float64)
    ok = (far_c >= 0) & (np.arange(NCP) < NC)
    parts.append(ok.reshape(P, -1))
    slopes = np.array(SLOPES, np.float32).reshape(8, 2).T
    bias = np.where(ok[:, :, None, None, :], -slopes[None, None, :, :, None] * far_c[:, :, None, None, :], -1e30)
    parts.append(bias.reshape(P, -1))
    t["nsa_tab"] = np.concatenate(parts, 1)
    inv = np.float32(10000.0) ** (-np.arange(16, dtype=np.float32) / np.float32(16))
    token = np.arange(T)
    where = np.stack([token // 64, token % 64]).astype(np.float32)
    angle = (where[:, None, :] * inv[None, :, None]).astype(np.float32)
    angle = np.broadcast_to(angle[None, :, None], (2, 2, 2, 16, T)).reshape(P, T)
    t["rope_tab"] = np.concatenate([np.cos(angle), np.sin(angle)], 1)
    return {k: a.astype(np.float32) for k, a in t.items()}


def kernel(**inputs):
    import numpy as _np
    import concourse.bacc as _bacc
    from concourse import mybir as _mybir
    from concourse.bass_utils import run_bass_kernel_spmd as _run

    nc = _bacc.Bacc("TRN2", target_bir_lowering=False, num_devices=1)
    arrays = {k: _np.ascontiguousarray(a) for k, a in {**lay_out(inputs), **shape_tables()}.items()}
    dram = {k: nc.dram_tensor(k, a.shape, _mybir.dt.from_np(a.dtype), kind="ExternalInput").ap()
            for k, a in arrays.items()}
    out = nc.dram_tensor("out", (D, T), _mybir.dt.float32, kind="ExternalOutput").ap()
    program(nc, dram, out)
    r = _run(nc, [arrays], core_ids=[0])
    return _np.ascontiguousarray(r.results[0]["out"].T)[None]
```
